# Optimizing a Trainium2 kernel written in Bass

```python
import jax, jax.numpy as jnp
from jax import lax
import numpy as np

D_MODEL = 1024
BATCH = 1
SEQ = 1024
DEPTH = 2

N_MIXERS = 2
N_RG = (DEPTH + 1) // 2
N_HG = DEPTH // 2
LRU_WIDTH = D_MODEL
RG_HEADS = 8
RG_BLOCK = LRU_WIDTH // RG_HEADS
CONV_WIDTH = 4
LRU_C = 8.0
HG_HEADS = 8
HG_DK = D_MODEL // HG_HEADS
HG_DV = D_MODEL // HG_HEADS
HG_CHUNK = 64
D_FF = 4 * D_MODEL
NORM_EPS = 1e-6
GNORM_EPS = 1e-5

kernel_name = "hybrid_rglru_hgrn2_adaln_trunk"

def rms_norm(x, gain, eps=NORM_EPS):
    xf = x.astype(jnp.float32)
    y = xf * lax.rsqrt(jnp.mean(xf * xf, axis=-1, keepdims=True) + eps)
    return (y * gain.astype(jnp.float32)).astype(x.dtype)

def causal_depthwise_conv(x, w, b):
    T = x.shape[1]
    xp = jnp.pad(x, ((0, 0), (CONV_WIDTH - 1, 0), (0, 0)))
    y = b
    for tap in range(CONV_WIDTH):
        y = y + xp[:, tap:tap + T, :] * w[tap]
    return y

def rg_lru(x, w_a, b_a, w_x, b_x, lam):
    B, T, _ = x.shape
    xh = x.reshape(B, T, RG_HEADS, RG_BLOCK)
    r = jax.nn.sigmoid(jnp.einsum('bthi,hij->bthj', xh, w_a).reshape(B, T, LRU_WIDTH) + b_a)
    i = jax.nn.sigmoid(jnp.einsum('bthi,hij->bthj', xh, w_x).reshape(B, T, LRU_WIDTH) + b_x)
    log_a = -LRU_C * r.astype(jnp.float32) * jax.nn.softplus(-lam.astype(jnp.float32))
    a = jnp.exp(log_a)
    mult = jnp.sqrt(-jnp.expm1(2.0 * log_a))
    mult = jnp.where(jnp.arange(T)[None, :, None] == 0, 1.0, mult)
    u = mult * (i * x).astype(jnp.float32)

    def combine(left, right):
        a1, b1 = left
        a2, b2 = right
        return a1 * a2, a2 * b1 + b2

    _, h = lax.associative_scan(combine, (a, u), axis=1)
    return h.astype(x.dtype)

def rglru_block(h, w_in, conv_w, conv_b, w_a, b_a, w_x, b_x, lam, w_out):
    xb, yb = jnp.split(h @ w_in, 2, axis=-1)
    gate = jax.nn.gelu(yb, approximate=True)
    xb = causal_depthwise_conv(xb, conv_w, conv_b)
    hr = rg_lru(xb, w_a, b_a, w_x, b_x, lam)
    return (hr * gate) @ w_out

def hgrn2_chunk_scan(q, k, v, log_f):
    B, T, H, _ = q.shape
    N = T // HG_CHUNK

    def to_chunks(t):
        return t.astype(jnp.float32).reshape(B, N, HG_CHUNK, H, -1).transpose(1, 0, 3, 2, 4)

    qc, kc, vc, lc = to_chunks(q), to_chunks(k), to_chunks(v), to_chunks(log_f)
    bc = jnp.cumsum(lc, axis=3)
    causal = jnp.tril(jnp.ones((HG_CHUNK, HG_CHUNK), dtype=bool))

    def step(S, inp):
        q_, k_, v_, b_ = inp
        diff = b_[:, :, :, None, :] - b_[:, :, None, :, :]
        decay = jnp.exp(jnp.where(causal[:, :, None], diff, -jnp.inf))
        A = jnp.einsum('bhtsk,bhsk->bhts', q_[:, :, :, None, :] * decay, k_)
        o = A @ v_ + jnp.einsum('bhtk,bhkv->bhtv', q_ * jnp.exp(b_), S)
        b_last = b_[:, :, -1:, :]
        S = jnp.exp(b_last)[:, :, 0, :, None] * S + jnp.einsum(
            'bhsk,bhsv->bhkv', k_ * jnp.exp(b_last - b_), v_)
        return S, o

    S0 = jnp.zeros((B, H, HG_DK, HG_DV), jnp.float32)
    _, o = lax.scan(step, S0, (qc, kc, vc, bc))
    return o.transpose(1, 0, 3, 2, 4).reshape(B, T, H, HG_DV)

def hgrn2_block(h, w_in, lb, gnorm_w, w_out):
    B, T, _ = h.shape
    q, f, i, g = jnp.split(h @ w_in, 4, axis=-1)
    q = jax.nn.silu(q)
    fg = lb + (1.0 - lb) * jax.nn.sigmoid(f.astype(jnp.float32))
    log_f = jnp.log(fg)
    k = 1.0 - fg

    def heads(t):
        return t.reshape(B, T, HG_HEADS, -1)

    o = hgrn2_chunk_scan(heads(q), heads(k), heads(i), heads(log_f))
    o = rms_norm(o, gnorm_w, GNORM_EPS) * jax.nn.silu(heads(g).astype(jnp.float32))
    return (o.reshape(B, T, D_MODEL) @ w_out).astype(h.dtype)

def setup_inputs(seed: int = 0) -> dict:
    key = jax.random.key(seed)
    ks = jax.random.split(key, 24)
    f32 = jnp.float32
    nrm = lambda k, shape, s: jax.random.normal(k, shape, f32) * s
    u = jax.random.uniform(ks[11], (N_RG, LRU_WIDTH), f32, 0.9, 0.999)
    s = u ** (1.0 / LRU_C)
    lam = jnp.log(s) - jnp.log1p(-s)
    return {
        "x": nrm(ks[0], (BATCH, SEQ, D_MODEL), 1.0),
        "c": nrm(ks[1], (BATCH, D_MODEL), 1.0),
        "mod_w": nrm(ks[2], (DEPTH, D_MODEL, 6 * D_MODEL), D_MODEL ** -0.5),
        "mod_b": nrm(ks[3], (DEPTH, 6 * D_MODEL), 0.02),
        "norm_mix": 1.0 + nrm(ks[4], (DEPTH, D_MODEL), 0.02),
        "norm_mlp": 1.0 + nrm(ks[5], (DEPTH, D_MODEL), 0.02),
        "norm_final": 1.0 + nrm(ks[6], (D_MODEL,), 0.02),
        "rg_w_in": nrm(ks[7], (N_RG, D_MODEL, 2 * LRU_WIDTH), D_MODEL ** -0.5),
        "rg_conv_w": nrm(ks[8], (N_RG, CONV_WIDTH, LRU_WIDTH), CONV_WIDTH ** -0.5),
        "rg_conv_b": nrm(ks[9], (N_RG, LRU_WIDTH), 0.02),
        "rg_w_a": nrm(ks[10], (N_RG, RG_HEADS, RG_BLOCK, RG_BLOCK), RG_BLOCK ** -0.5),
        "rg_b_a": nrm(ks[12], (N_RG, LRU_WIDTH), 0.1),
        "rg_w_x": nrm(ks[13], (N_RG, RG_HEADS, RG_BLOCK, RG_BLOCK), RG_BLOCK ** -0.5),
        "rg_b_x": nrm(ks[14], (N_RG, LRU_WIDTH), 0.1),
        "rg_lambda": lam,
        "rg_w_out": nrm(ks[15], (N_RG, LRU_WIDTH, D_MODEL), LRU_WIDTH ** -0.5),
        "hg_w_in": nrm(ks[16], (N_HG, D_MODEL, 4 * D_MODEL), D_MODEL ** -0.5),
        "hg_lower_bounds": nrm(ks[17], (DEPTH, D_MODEL), 0.1),
        "hg_gnorm": 1.0 + nrm(ks[18], (N_HG, HG_DV), 0.02),
        "hg_w_out": nrm(ks[19], (N_HG, D_MODEL, D_MODEL), D_MODEL ** -0.5),
        "mlp_w1": nrm(ks[20], (DEPTH, D_MODEL, D_FF), D_MODEL ** -0.5),
        "mlp_w2": nrm(ks[21], (DEPTH, D_FF, D_MODEL), D_FF ** -0.5),
    }

def reference(x, c, mod_w, mod_b, norm_mix, norm_mlp, norm_final,
              rg_w_in, rg_conv_w, rg_conv_b, rg_w_a, rg_b_a, rg_w_x, rg_b_x, rg_lambda, rg_w_out,
              hg_w_in, hg_lower_bounds, hg_gnorm, hg_w_out, mlp_w1, mlp_w2):
    cs = jax.nn.silu(c)
    lb_all = jnp.cumsum(jax.nn.softmax(hg_lower_bounds.astype(jnp.float32), axis=0), axis=0)
    lb_all = lb_all - lb_all[0]
    for layer in range(DEPTH):
        mod = cs @ mod_w[layer] + mod_b[layer]
        sh_t, sc_t, g_t, sh_c, sc_c, g_c = [m[:, None, :] for m in jnp.split(mod, 6, axis=-1)]
        h = rms_norm(x, norm_mix[layer]) * (1.0 + sc_t) + sh_t
        j = layer // N_MIXERS
        if layer % N_MIXERS == 0:
            y = rglru_block(h, rg_w_in[j], rg_conv_w[j], rg_conv_b[j], rg_w_a[j], rg_b_a[j],
                            rg_w_x[j], rg_b_x[j], rg_lambda[j], rg_w_out[j])
        else:
            y = hgrn2_block(h, hg_w_in[j], lb_all[layer], hg_gnorm[j], hg_w_out[j])
        x = (x + g_t * y).astype(x.dtype)
        h = rms_norm(x, norm_mlp[layer]) * (1.0 + sc_c) + sh_c
        ff = jnp.square(jax.nn.relu(h @ mlp_w1[layer])) @ mlp_w2[layer]
        x = (x + g_c * ff).astype(x.dtype)
    return rms_norm(x, norm_final)


_drawn_inputs = setup_inputs


def setup_inputs(seed=0):
    import zlib

    import numpy as np

    out = dict(_drawn_inputs(seed))
    spreads = {}
    factors = {'norm_mix': 3.201,
     'norm_mlp': 3.745,
     'norm_final': 2.812,
     'rg_b_a': 5.069,
     'hg_lower_bounds': 8.0,
     'hg_gnorm': 8.0}
    for name, (base, spread) in spreads.items():
        noise = np.random.default_rng([zlib.crc32(name.encode()), seed]).standard_normal(out[name].shape)
        drawn = base * np.exp(spread * noise) if base else spread * noise
        out[name] = __import__('jax').numpy.asarray(drawn.astype(out[name].dtype))
    for name, factor in factors.items():
        out[name] = (out[name] * factor).astype(out[name].dtype)
    return out
```

```python
from collections import namedtuple
from contextlib import ExitStack

import concourse.bass as bass
from concourse import mybir

P = 128
D = 1024
T = 1024
NT = D // P
NC = T // P
HALF = T // 2
DFF = 4 * D
BLOCKS = DFF // D
TAPS = 4
LEVELS = 7
EPS, GEPS = 1e-6, 1e-5

RG_IN, RG_OUT = 0, 2 * NT
MLP0 = RG_OUT + NT
HG_IN = MLP0 + 2 * NT * BLOCKS
HG_OUT = HG_IN + 4 * NT
MLP1 = HG_OUT + NT
END = MLP1 + 2 * NT * BLOCKS

MOD0 = {"sh_t": 0, "sc_t": 8, "g_t": 16, "sc_c": 24, "sh_c": 32, "g_c": 40}
MOD1 = {"sh_t": 48, "sc_t": 56, "g_t": 64, "sh_c": 72, "sc_c": 80, "g_c": 88}
PART = {"sh_t": 0, "sc_t": 1, "g_t": 2, "sh_c": 3, "sc_c": 4, "g_c": 5}
C_C, C_NF, C_CW, C_CB, C_BA, C_BX, C_LAM, C_LB, C_GN = 0, 8, 16, 48, 56, 64, 72, 80, 96
V2 = 97

Step = namedtuple("Step", "t half odd")


def step_of(base, mult, r, c):
    return Step(base + mult * r + c, base // 2 + (mult // 2) * r + c // 2, c % 2)


def trunk(nc, x, c, mod_w, mod_b, norm_mix, norm_mlp, norm_final, rg_w_in, rg_conv_w, rg_conv_b,
          rg_w_a, rg_b_a, rg_w_x, rg_b_x, rg_lambda, rg_w_out, hg_w_in, hg_lower_bounds, hg_gnorm,
          hg_w_out, mlp_w1, mlp_w2, out):
    f32, f32r, u32 = mybir.dt.float32, mybir.dt.float32r, mybir.dt.uint32
    ALU = mybir.AluOpType
    ACT = mybir.ActivationFunctionType
    x_spill = nc.dram_tensor("x_spill", (2, NT, P, T), f32, kind="Internal").ap()

    ctx = ExitStack()
    with ctx:
        def sb(name, shape, dt=f32):
            at = nc.sbuf_base
            h = ctx.enter_context(nc.sbuf_tensor(name, shape, dt))
            return h, at

        def over(name, shape, at, dt=f32):
            return nc.alloc_sbuf_tensor_at(name, shape, dt, offset=at)

        def sem(name):
            return ctx.enter_context(nc.semaphore(name))

        res, _ = sb("res", [P, NT, T])
        a_hi, at_ahi = sb("a_hi", [P, NT, T], f32r)
        a_lo, at_alo = sb("a_lo", [P, NT, T], f32r)
        b_hi, at_bhi = sb("b_hi", [P, NT, T], f32r)
        b_lo, at_blo = sb("b_lo", [P, NT, T], f32r)
        w_hi, _ = sb("w_hi", [P, 2, NT, P], f32r)
        w_lo, _ = sb("w_lo", [P, 2, NT, P], f32r)
        stage, _ = sb("stage", [P, 2, NT, P])
        mstage, _ = sb("mstage", [P, 2, NT, P])
        rstd, _ = sb("rstd", [P, T])
        tmp, _ = sb("tmp", [P, T])
        pv, _ = sb("pv", [P, 2, 2, P])
        ident, _ = sb("ident", [P, P])
        mask, _ = sb("mask", [P, LEVELS, P // 2])
        vec1, _ = sb("vec1", [P, P])
        vec2, _ = sb("vec2", [P, V2])
        mod, _ = sb("mod", [P, 96])
        amp, _ = sb("amp", [P, 4, NT])
        cs, _ = sb("cs", [P, NT])
        decay, _ = sb("decay", [P, 2, NT])
        lbs, _ = sb("lbs", [P, 3, NT])
        sm, _ = sb("sm", [P, 6, NT])
        bcol, _ = sb("bcol", [P, 2])
        gbias, _ = sb("gbias", [P, 2])
        nst, _ = sb("nst", [P, 4, NT])
        ones = over("ones", [P, P], nc.sbuf_base)
        _, _ = sb("ones_slab", [P, P])

        xin = over("xin", [P, NT, D], at_blo)
        w_scale = over("w_scale", [P, NT, D], at_bhi)
        w_shift = over("w_shift", [P, NT, D], at_blo)
        o_rg = over("o_rg", [P, NT, T], at_blo)
        o_hg = over("o_hg", [P, NT, T], at_alo)
        K4 = 4
        xbp = over("xbp", [P, T + TAPS - 1], at_bhi)
        gst = over("gst", [P, 2, P], at_bhi + 1032 * K4)
        gw_hi = over("gw_hi", [P, 2, P], at_bhi + 1288 * K4, f32r)
        gw_lo = over("gw_lo", [P, 2, P], at_bhi + 1544 * K4, f32r)
        xc_hi = over("xc_hi", [P, T], at_bhi + 1800 * K4, f32r)
        xc_lo = over("xc_lo", [P, T], at_bhi + 2824 * K4, f32r)
        yb = over("yb", [P, T], at_bhi + 3848 * K4)
        ysig = over("ysig", [P, T], at_bhi + 4872 * K4)
        ytmp = over("ytmp", [P, T], at_bhi + 5896 * K4)
        xc, r_g, i_g, th, a_g, m_g, ix_g, h_g = (res[:, n, :] for n in range(8))
        at2 = over("at2", [P, NT, T], at_ahi)
        L_q, L_s, L_v, L_g, q_w, k_w, f_w, tot = (res[:, n, :] for n in range(8))
        v_t, k_t, att, s_st, o_sb, o_sq, t_s = (at2[:, n, :] for n in range(7))

        acc = [ctx.enter_context(nc.psum_tensor(f"acc{n}", [P, T], f32)) for n in range(2)]
        bank = [ctx.enter_context(nc.psum_tensor(f"bank{n}", [P, HALF], f32)) for n in range(3)]
        cols = ctx.enter_context(nc.psum_tensor("cols", [P, HALF], f32))

        vec_loaded = sem("vec_loaded")
        x_loaded = [sem(f"x_loaded{r}") for r in range(NC)]
        scale_loaded, shift_loaded = sem("scale_loaded"), sem("shift_loaded")
        w_loaded = [sem(f"w_loaded{n}") for n in range(2)]
        m_loaded = [sem(f"m_loaded{n}") for n in range(2)]
        g_loaded = sem("g_loaded")
        spilled, reloaded = sem("spilled"), [sem("reloaded0"), sem("reloaded1")]
        stored = sem("stored")
        consts = sem("consts")
        vec_t, vec_c, small_a, small_d = sem("vec_t"), sem("vec_c"), sem("small_a"), sem("small_d")
        xt_mm, xt_cp = sem("xt_mm"), sem("xt_cp")
        hi_ready, lo_ready = sem("hi_ready"), sem("lo_ready")
        in_hi, in_lo = sem("in_hi"), sem("in_lo")
        mm_done, ps_free = sem("mm_done"), sem("ps_free")
        scaled = sem("scaled")
        sums_ready = sem("sums_ready")
        mod_used = sem("mod_used")
        cols_read = sem("cols_read")
        stat_mm, ms_ready, root_ready, diag_ready, bc_mm, rstd_ready = (
            sem(n) for n in ("stat_mm", "ms_ready", "root_ready", "diag_ready", "bc_mm", "rstd_ready"))
        x_new = sem("x_new")
        sq_done = sem("sq_done")
        relu_done = sem("relu_done")
        xb_out, xc0, xc_done, gw_hi_r, gw_lo_r = (
            sem(n) for n in ("xb_out", "xc0", "xc_done", "gw_hi_r", "gw_lo_r"))
        xc_hi_r, xc_lo_r = sem("xc_hi_r"), sem("xc_lo_r")
        gate_mm, gate_rd = sem("gate_mm"), sem("gate_rd")
        y_poly, y_arg, y_sig, gy_done = (sem(n) for n in ("y_poly", "y_arg", "y_sig", "gy_done"))
        ga_done, gp_done, gm_done, ix_done, og_done = (
            sem(n) for n in ("ga_done", "gp_done", "gm_done", "ix_done", "og_done"))
        sg_done = sem("sg_done")
        vt_mm, vt_cp = sem("vt_mm"), sem("vt_cp")
        prep = sem("prep")
        dg_mm, dg_rd = sem("dg_mm"), sem("dg_rd")
        lv_mm, lv_rd, lv_up = sem("lv_mm"), sem("lv_rd"), sem("lv_up")
        kt_mm, kt_cp, kv_mm, st_done = sem("kt_mm"), sem("kt_cp"), sem("kv_mm"), sem("st_done")
        o_mm, o_cp = sem("o_mm"), sem("o_cp")
        hst_mm, hms, hroot, hdiag, hbc_mm, on_done = (
            sem(n) for n in ("hst_mm", "hms", "hroot", "hdiag", "hbc_mm", "on_done"))

        def events(t):
            return t

        def ev_mlp1(b, n):
            return HG_OUT + NT * b + n

        def seen(t, norms):
            return t + 2 + norms

        def tiled(w):
            return w.rearrange("(k p) n -> p k n", p=P)

        block = ctx.enter_context(nc.Block())

        @block.sync
        def _(sp):
            vr1, vr2 = rstd[:, 0:P], rstd[0:V2, P:2 * P]

            def rows(dst, src):
                sp.dma_start(dst, src).then_inc(vec_loaded, 16)

            mb = mod_b.rearrange("l (n p) -> l n p", p=P)
            for name, at in MOD0.items():
                rows(vr1[at:at + 8, :], mb[0, 8 * PART[name]:8 * PART[name] + 8, :])
            rows(vr1[48:96, :], mb[1])
            rows(vr1[96:112, :], norm_mix.rearrange("l (n p) -> (l n) p", p=P))
            rows(vr1[112:128, :], norm_mlp.rearrange("l (n p) -> (l n) p", p=P))
            for at, n, src in ((C_C, 8, c.rearrange("a (n p) -> (a n) p", p=P)),
                               (C_NF, 8, norm_final.rearrange("(n p) -> n p", p=P)),
                               (C_CW, 32, rg_conv_w.rearrange("a w (n p) -> (a w n) p", p=P)),
                               (C_CB, 8, rg_conv_b.rearrange("a (n p) -> (a n) p", p=P)),
                               (C_BA, 8, rg_b_a.rearrange("a (n p) -> (a n) p", p=P)),
                               (C_BX, 8, rg_b_x.rearrange("a (n p) -> (a n) p", p=P)),
                               (C_LAM, 8, rg_lambda.rearrange("a (n p) -> (a n) p", p=P)),
                               (C_LB, 16, hg_lower_bounds.rearrange("l (n p) -> (l n) p", p=P)),
                               (C_GN, 1, hg_gnorm)):
                rows(vr2[at:at + n, :], src)
            for r in range(NC):
                sp.dma_start(xin[:, r, :], x[0, r * P:(r + 1) * P, :]).then_inc(x_loaded[r], 16)

            def mod_part(layer, name):
                return tiled(mod_w[layer])[:, :, D * PART[name]:D * PART[name] + D]

            sp.dma_start(w_scale[:, :, :], mod_part(0, "sc_t")).then_inc(scale_loaded, 16)

            def load_w(s, src, summed=None, split=None):
                if summed is not None:
                    sp.wait_ge(sums_ready, summed)
                if split is not None:
                    sp.wait_ge(lo_ready, split)
                sp.dma_start(stage[:, s.odd, :, :], src).then_inc(w_loaded[s.odd], 16)

            def load_mod(n, odd, src):
                sp.dma_start(mstage[:, odd, :, :], src).then_inc(m_loaded[odd], 16)

            rg_in = tiled(rg_w_in[0]).rearrange("p k (s n c) -> p k s n c", s=2, c=P)
            rg_out = tiled(rg_w_out[0])
            hg_in = tiled(hg_w_in[0]).rearrange("p k (s n c) -> p k s n c", s=4, c=P)
            hg_out = tiled(hg_w_out[0])

            load_w(step_of(0, 2, 0, 0), rg_in[:, :, 0, 0, :])
            load_w(step_of(0, 2, 0, 1), rg_in[:, :, 1, 0, :])
            sp.wait_ge(xt_mm, NT)
            sp.dma_start(w_shift[:, :, :], mod_part(0, "sh_t")).then_inc(shift_loaded, 16)
            g_t, sc_c = mod_part(0, "g_t"), mod_part(0, "sc_c")
            load_mod(0, 0, g_t[:, :, 0:P])
            load_mod(1, 1, g_t[:, :, P:2 * P])
            for n in range(NT):
                sp.wait_ge(xt_cp, n + 1)
                sp.dma_start(x_spill[0, n], res[:, n, :]).then_inc(spilled, 16)

            def load_gate(h):
                sp.dma_start(gst[:, 0, :], rg_w_a[0, bass.ds(h, 1)].rearrange("a p n -> p (a n)")
                             ).then_inc(g_loaded, 16)
                sp.dma_start(gst[:, 1, :], rg_w_x[0, bass.ds(h, 1)].rearrange("a p n -> p (a n)")
                             ).then_inc(g_loaded, 16)

            sp.wait_ge(small_d, 2)
            load_gate(0)

            def rg_loads(j, part, at):
                for k in range(2):
                    s = step_of(RG_IN, 2, j, k)
                    load_w(s, rg_in[:, :, k, bass.ds(j, 1), :].rearrange("p k a c -> p k (a c)"), s.t - 1)
                    sp.wait_ge(mod_used, s.t - 1)
                    load_mod(s.t, k, part[:, :, bass.ds(at + k * P, P)])
                sp.wait_ge(gw_lo_r, j)
                load_gate(j)

            with sp.Fori(1, 4) as j:
                rg_loads(j, g_t, j * (2 * P))
            with sp.Fori(4, 8) as j:
                rg_loads(j, sc_c, j * (2 * P) - D)

            def rg_out_loads(m, part, at):
                for k in range(2):
                    s = step_of(RG_OUT, 2, m, k)
                    load_w(s, rg_out[:, :, bass.ds(m * (2 * P) + k * P, P)], s.t - 1)
                    for q in range(2):
                        n = 2 * NT + m * 4 + 2 * k + q
                        sp.wait_ge(mod_used, n - 1)
                        load_mod(n, q, part[:, :, bass.ds(at + (2 * k + q) * P, P)])

            def reload(which):
                for n in range(NT):
                    sp.dma_start(res[:, n, :], x_spill[which, n]).then_inc(reloaded[which], 16)

            rg_out_loads(0, mod_part(0, "sh_c"), 0)
            sp.wait_ge(og_done, NT)
            reload(0)
            rg_out_loads(1, mod_part(0, "sh_c"), 4 * P)
            with sp.Fori(2, 4) as m:
                rg_out_loads(m, mod_part(0, "g_c"), m * (4 * P) - D)

            mod1 = tiled(mod_w[1])

            def mlp_loads(layer, base, b):
                w1 = tiled(mlp_w1[layer])
                w2 = mlp_w2[layer].rearrange("(b k p) n -> p b k n", p=P, k=NT)
                for n in range(NT):
                    s = step_of(base, 2 * NT, b, n)
                    src = w1[:, :, bass.ds(b * D + n * P, P)]
                    if layer == 0:
                        load_w(s, src, summed=s.t - 1)
                    elif n < 2:
                        load_w(s, src, split=s.t - 1)
                    else:
                        load_w(s, src, summed=ev_mlp1(b, n - 1))
                m = 0
                for n in range(NT):
                    s = step_of(base + NT, 2 * NT, b, n)
                    src = w2[:, bass.ds(b, 1), :, n * P:(n + 1) * P].rearrange("p a k n -> p (a k) n")
                    if layer == 0:
                        load_w(s, src, summed=s.t - 1)
                    elif n < 2:
                        load_w(s, src, summed=ev_mlp1(b, NT - 1 + n))
                    else:
                        load_w(s, src, split=s.t - 1)
                    for _ in range(2 - n % 2 if layer == 0 else 0):
                        sp.wait_ge(mod_used, b * 12 + (m + 31))
                        load_mod(None, m % 2, mod1[:, :, bass.ds(b * (12 * P) + m * P, P)])
                        m += 1

            with sp.Fori(0, BLOCKS) as b:
                mlp_loads(0, MLP0, b)

            def hg_loads(h, ks=range(4)):
                for k in ks:
                    s = step_of(HG_IN, 4, h, k)
                    load_w(s, hg_in[:, :, k, bass.ds(h, 1), :].rearrange("p k a c -> p k (a c)"), s.t - 1)

            hg_loads(0, (0, 1))
            for n in range(NT):
                sp.wait_ge(x_new, NT + NT * (BLOCKS - 1) + n + 1)
                sp.dma_start(x_spill[1, n], res[:, n, :]).then_inc(spilled, 16)
            hg_loads(0, (2, 3))
            with sp.Fori(1, NT) as h:
                hg_loads(h)
            sp.wait_ge(sums_ready, HG_OUT)
            for n in range(NT):
                s = step_of(HG_OUT, 2 * NT, 0, n)
                load_w(s, hg_out[:, :, n * P:(n + 1) * P], split=s.t - 1)
                if n == 2:
                    sp.wait_ge(on_done, NT)
                    reload(1)
            with sp.Fori(0, BLOCKS) as b:
                mlp_loads(1, MLP1, b)
            for r in range(NC):
                sp.wait_ge(xt_cp, NT + r + 1)
                sp.dma_start(out[0, r * P:(r + 1) * P, :], o_hg[:, r, :]).then_inc(stored, 16)
            sp.wait_ge(stored, 16 * NC)
            sp.wait_ge(spilled, 2 * 16 * NT)

        @block.gpsimd
        def _(pool):
            pool.memset(ident[:, :], 0.0)
            pool.memset(ones[:, :], 1.0)
            pool.memset(mask[:, :, :], 1.0)
            pool.drain()
            pool.affine_select(out=ident[:, :], in_=ident[:, :], compare_op=ALU.not_equal, fill=1.0,
                               base=0, pattern=[[-1, P]], channel_multiplier=1)
            for lv in range(LEVELS):
                h = 1 << lv
                m = mask[:, lv, :].rearrange("p (n j) -> p n j", j=h)
                pool.affine_select(out=m, in_=m, compare_op=ALU.is_ge, fill=0.0, base=0,
                                   pattern=[[-2 * h, P // 2 // h], [0, h]], channel_multiplier=1)
                pool.drain()
                pool.affine_select(out=m, in_=m, compare_op=ALU.is_ge, fill=0.0, base=h - 1,
                                   pattern=[[2 * h, P // 2 // h], [0, h]], channel_multiplier=-1)
            pool.drain().then_inc(consts, 1)

            def sums(buf, vector, slot):
                pool.tensor_tensor(buf, buf, vector.unsqueeze(2).broadcast_to([P, NT, P]), ALU.mult)
                pool.drain()
                pool.tensor_tensor(buf[:, 0:4, :], buf[:, 0:4, :], buf[:, 4:8, :], ALU.add)
                pool.drain()
                pool.tensor_tensor(buf[:, 0:2, :], buf[:, 0:2, :], buf[:, 2:4, :], ALU.add)
                pool.drain()
                return pool.tensor_tensor(slot, buf[:, 0, :], buf[:, 1, :], ALU.add)

            def w_sums(s, shift):
                pool.wait_ge(lo_ready, s.t + 1)
                return sums(stage[:, s.odd, :, :], shift, pv[:, s.odd, 0, :])

            def m_sums(odd, loads, s, slot):
                pool.wait_ge(m_loaded[odd], loads * 16)
                last = sums(mstage[:, odd, :, :], cs[:, :], pv[:, s.odd, slot, :])
                last.then_inc(mod_used, 1)
                pool.drain()

            def pv_free(s):
                pool.wait_ge(mm_done, s.t - 1)

            def mark():
                pool.drain().then_inc(sums_ready, 1)

            def square(n, first=False):
                src = res[:, bass.ds(n, 1), :].rearrange("p a t -> p (a t)")
                pool.tensor_tensor(rstd[:, :] if first else tmp[:, :], src, src, ALU.mult)
                pool.drain()
                if not first:
                    pool.tensor_tensor(rstd[:, :], rstd[:, :], tmp[:, :], ALU.add)
                    pool.drain()

            def squared():
                pool.drain().then_inc(sq_done, 1)

            pool.wait_ge(vec_c, 2)
            for n in range(NT):
                pool.wait_ge(xt_cp, n + 1)
                square(n, first=n == 0)
            squared()

            def shift_of(table, name):
                return mod[:, table[name]:table[name] + NT]

            pool.wait_ge(small_d, 3)
            for_head = shift_of(MOD0, "sh_t")

            def rg_sums(j, first=False):
                for k in range(2):
                    s = step_of(RG_IN, 2, j, k)
                    if not first:
                        pv_free(s)
                    w_sums(s, for_head)
                    m_sums(k, j + 1, s, 1)
                    mark()

            def rg_ix(h):
                pool.wait_ge(gate_rd, h * 4 + 4)
                pool.tensor_tensor(ix_g, i_g, xc, ALU.mult).then_inc(ix_done, 1)

            def rg_gy(h):
                pool.wait_ge(y_sig, h + 1)
                pool.tensor_tensor(yb[:, :], yb[:, :], ysig[:, :], ALU.mult).then_inc(gy_done, 1)

            rg_sums(0, first=True)
            rg_gy(0)
            with pool.Fori(1, NT) as j:
                rg_ix(j - 1)
                rg_sums(j)
                rg_gy(j)
            rg_ix(NT - 1)

            def rg_out_sums(m):
                for k in range(2):
                    s = step_of(RG_OUT, 2, m, k)
                    pv_free(s)
                    pool.wait_ge(lo_ready, s.t + 1)
                    for q in range(2):
                        m_sums(q, NT + m * 2 + k + 1, s, q)
                    mark()

            with pool.Fori(0, 4) as m:
                rg_out_sums(m)
                for k in range(2):
                    pool.wait_ge(x_new, m * 2 + k + 1)
                    square(m * 2 + k)
            squared()

            def mlp_sums(layer, base, b, last):
                table = MOD0 if layer == 0 else MOD1
                with pool.Fori(0, 2) as q:
                    for k in range(4):
                        s = Step(base + b * (2 * NT) + q * 4 + k, None, k % 2)
                        pv_free(s)
                        w_sums(s, shift_of(table, "sh_c"))
                        mark()
                if last:
                    pool.wait_ge(scaled, (2 * NT + NT * BLOCKS) if layer == 0
                                 else 2 * NT + 2 * NT * BLOCKS + 4 * NT)
                    pool.memset(rstd[:, :], 0.0)
                    pool.drain()
                with pool.Fori(0, 2) as q:
                    n = 0
                    for k in range(4):
                        s = Step(base + NT + b * (2 * NT) + q * 4 + k, None, k % 2)
                        if layer == 0:
                            pv_free(s)
                            pool.wait_ge(lo_ready, s.t + 1)
                            for slot in range(2 - k % 2):
                                m_sums(n % 2, b * 6 + q * 3 + (n // 2 + 1) + 2 * NT, s, slot)
                                n += 1
                            mark()
                        if last:
                            pool.wait_ge(x_new, (NT + NT * BLOCKS) * (1 + layer) - NT + q * 4 + k + 1)
                            square(q * 4 + k)
                if last:
                    squared()

            with pool.Fori(0, BLOCKS - 1) as b:
                mlp_sums(0, MLP0, b, False)
            mlp_sums(0, MLP0, BLOCKS - 1, True)

            with pool.Fori(0, NT) as h:
                for k in range(4):
                    s = step_of(HG_IN, 4, h, k)
                    pv_free(s)
                    w_sums(s, shift_of(MOD1, "sh_t"))
                    mark()
            pool.wait_ge(scaled, 2 * NT + NT * BLOCKS + 4 * NT)
            pool.memset(rstd[:, :], 0.0)
            pool.drain()
            with pool.Fori(0, NT) as m:
                pool.wait_ge(x_new, m + (NT + NT * BLOCKS + 1))
                square(m)
            squared()
            with pool.Fori(0, BLOCKS - 1) as b:
                mlp_sums(1, MLP1, b, False)
            mlp_sums(1, MLP1, BLOCKS - 1, True)

        @block.tensor
        def _(pe):
            def mm(dst, lhs, rhs, start=True, stop=True):
                return pe.matmul(dst, lhs, rhs, start=start, stop=stop)

            pe.wait_ge(consts, 1)
            pe.wait_ge(vec_loaded, 16 * 18)
            pe.transpose(bank[0][:, 0:P], rstd[:, 0:P], ident[:, :]).then_inc(vec_t, 1)
            pe.transpose(bank[1][:, 0:V2], rstd[0:V2, P:2 * P], ident[0:V2, 0:V2]).then_inc(vec_t, 1)
            for n in range(NT):
                if n >= 2:
                    pe.wait_ge(xt_cp, n - 1)
                for r in range(NC):
                    if n == 0:
                        pe.wait_ge(x_loaded[r], 16)
                    last = pe.transpose(acc[n % 2][:, r * P:(r + 1) * P], xin[:, r, n * P:(n + 1) * P],
                                        ident[:, :])
                last.then_inc(xt_mm, 1)

            pe.wait_ge(small_a, 1)
            for k0, (weights, loaded) in enumerate(((w_scale, scale_loaded), (w_shift, shift_loaded))):
                pe.wait_ge(loaded, 16)
                if k0:
                    pe.wait_ge(cols_read, 1)
                for n in range(NT):
                    for k in range(NT):
                        last = mm(cols[:, n:n + 1], weights[:, k, n * P:(n + 1) * P], cs[:, k:k + 1],
                                  k == 0, k == NT - 1)
                last.then_inc(vec_t, 1)

            def step(s, src, ready=None, gaps=None, fresh=False, tiles=range(NT)):
                hi, lo = src
                if tiles[0] == 0:
                    pe.wait_ge(lo_ready, s.t + 1)
                    if not fresh:
                        pe.wait_ge(ps_free, s.t - 1)
                for k in tiles:
                    if ready is not None:
                        pe.wait_ge(in_lo, ready + k + 1)
                    for w, parts in ((w_hi, (hi, lo)), (w_lo, (hi,))):
                        for v in parts:
                            for n in range(2):
                                last = mm(acc[s.odd][:, n * HALF:(n + 1) * HALF], w[:, s.odd, k, :],
                                          v[:, k, n * HALF:(n + 1) * HALF],
                                          k == 0 and w is w_hi and v is hi,
                                          k == NT - 1 and w is w_lo)
                    if gaps and k in gaps:
                        gaps[k]()
                return last

            def sums(s, n, events_before, cols_before):
                pe.wait_ge(sums_ready, events_before + 1)
                pe.wait_ge(cols_read, cols_before)
                for i in range(n):
                    last = mm(cols[:, i:i + 1], pv[:, s.odd, i, :], ones[:, 0:1])
                return last

            def stats(norm, cols_before):
                pe.wait_ge(sq_done, norm)
                pe.wait_ge(cols_read, cols_before)
                for g in range(NC):
                    last = mm(cols[:, g:g + 1], rstd[:, g * P:(g + 1) * P], ones[:, 0:1])
                last.then_inc(stat_mm, 1)

            def spread(norm):
                pe.wait_ge(diag_ready, norm)
                for n in range(2):
                    last = mm(bank[n][:, :], ones[:, :], tmp[:, n * HALF:(n + 1) * HALF])
                last.then_inc(bc_mm, 1)

            def norm_gaps(norm, cols_before):
                return {5: lambda: stats(norm, cols_before), 7: lambda: spread(norm)}

            A, B = (a_hi, a_lo), (b_hi, b_lo)

            def gates(j, first=False):
                pe.wait_ge(gw_lo_r, j + 1)
                pe.wait_ge(xc_lo_r, j + 1)
                if first:
                    pe.wait_ge(rstd_ready, 1)
                else:
                    pe.wait_ge(gate_rd, j * 4)
                for q in range(4):
                    g, n = q % 2, q // 2
                    if q == 3:
                        pe.wait_ge(gate_rd, j * 4 + 1)
                    cut = slice(n * HALF, (n + 1) * HALF)
                    mm(bank[q % 3][:, :], gw_hi[:, g, :], xc_hi[:, cut], True, False)
                    mm(bank[q % 3][:, :], gw_hi[:, g, :], xc_lo[:, cut], False, False)
                    mm(bank[q % 3][:, :], gw_lo[:, g, :], xc_hi[:, cut], False, True).then_inc(gate_mm, 1)

            def rg_head(j, first=False):
                for k in range(2):
                    s = step_of(RG_IN, 2, j, k)
                    step(s, A, ready=0 if first and k == 0 else None, fresh=first,
                         gaps=norm_gaps(1, 2) if first and k == 0 else None)
                    sums(s, 2, events(s.t), seen(s.t, 1)).then_inc(mm_done, 1)
                gates(j, first)

            rg_head(0, first=True)
            with pe.Fori(1, NT) as j:
                rg_head(j)
            s = step_of(RG_OUT, 2, 0, 0)
            step(s, A, ready=NT)
            sums(s, 2, events(s.t), seen(s.t, 1)).then_inc(mm_done, 1)
            s = step_of(RG_OUT, 2, 0, 1)
            step(s, A)
            sums(s, 2, events(s.t), seen(s.t, 1)).then_inc(mm_done, 1)
            with pe.Fori(1, 4) as m:
                for k in range(2):
                    s = step_of(RG_OUT, 2, m, k)
                    step(s, A)
                    sums(s, 2, events(s.t), seen(s.t, 1)).then_inc(mm_done, 1)

            def mlp(layer, base, b, src, hid, tiles, first=False):
                norms = 2 if layer == 0 else None
                for q in range(2):
                    for k in range(4):
                        n = q * 4 + k
                        s = step_of(base, 2 * NT, b, n)
                        head = first and n == 0
                        step(s, src, ready=tiles - NT if head else None,
                             gaps=norm_gaps(2 + 2 * layer, seen(MLP0, 1) if layer == 0 else
                                            seen(HG_OUT, 3)) if head else None)
                        if layer == 0:
                            sums(s, 1, events(s.t), seen(s.t, norms)).then_inc(mm_done, 1)
                        else:
                            sums(s, 1, ev_mlp1(b, n), ev_mlp1(b, n) + 2 + 4).then_inc(mm_done, 1)
                for n in range(NT):
                    s = step_of(base + NT, 2 * NT, b, n)
                    last = step(s, hid, ready=tiles + b * NT if n == 0 else None)
                    if layer == 0:
                        last = sums(s, 2 - n % 2, events(s.t), seen(s.t, norms))
                    last.then_inc(mm_done, 1)

            mlp(0, MLP0, 0, B, A, 3 * NT, first=True)
            with pe.Fori(1, BLOCKS) as b:
                mlp(0, MLP0, b, B, A, 3 * NT)

            def att_diag(h, first=False):
                pe.wait_ge(prep, h + 1)
                if first:
                    pe.wait_ge(rstd_ready, 3)
                else:
                    pe.wait_ge(on_done, h)
                for n in range(2):
                    for g in range(4):
                        cut = slice((4 * n + g) * P, (4 * n + g + 1) * P)
                        last = mm(bank[2 if n == 0 else 0][:, g * P:(g + 1) * P], k_w[:, cut], L_q[:, cut])
                    last.then_inc(dg_mm, 1)

            def att_vt(h, n):
                if n == 0:
                    pe.wait_ge(ps_free, h * 4 + (HG_IN + 3))
                    pe.wait_ge(dg_rd, h * 2 + 2)
                else:
                    pe.wait_ge(vt_cp, h * 2 + 1)
                for g in range(4):
                    last = pe.transpose(bank[0][:, g * P:(g + 1) * P],
                                        L_v[:, (4 * n + g) * P:(4 * n + g + 1) * P], ident[:, :])
                last.then_inc(vt_mm, 1)

            def att_level(h, lv):
                size = 1 << lv
                if lv == 1:
                    pe.wait_ge(dg_rd, h * 2 + 1)
                if lv:
                    pe.wait_ge(lv_up, h * LEVELS + lv)
                if lv >= 2:
                    pe.wait_ge(lv_rd, h * LEVELS + lv - 1)
                q4 = q_w.rearrange("p (g n two j) -> p g n two j", g=NC, two=2, j=size)
                for g in range(NC):
                    last = mm(bank[1 + lv % 2][:, g * 64:(g + 1) * 64].rearrange("p (n j) -> p n j", j=size),
                              k_w[:, g * P:(g + 1) * P], q4[:, g, :, 1, :])
                last.then_inc(lv_mm, 1)

            def att_kt(h):
                pe.wait_ge(lv_up, h * LEVELS + LEVELS)
                pe.wait_ge(vt_cp, h * 2 + 2)
                pe.wait_ge(lv_rd, h * LEVELS + LEVELS - 1)
                for n in range(2):
                    for g in range(4):
                        last = pe.transpose(bank[2 if n == 0 else 0][:, g * P:(g + 1) * P],
                                            k_w[:, (4 * n + g) * P:(4 * n + g + 1) * P], ident[:, :])
                    last.then_inc(kt_mm, 1)

            def att_kv(h):
                pe.wait_ge(lv_rd, h * LEVELS + LEVELS)
                for n in range(2):
                    pe.wait_ge(kt_cp, h * 2 + 1 + n)
                    for g in range(4 - n):
                        cut = slice((4 * n + g) * P, (4 * n + g + 1) * P)
                        last = mm(bank[1 + n][:, g * P:(g + 1) * P], k_t[:, cut], v_t[:, cut])
                    last.then_inc(kv_mm, 1)

            def att_out(h, n):
                pe.wait_ge(st_done, h * 2 + 1 + n)
                for g in range(4):
                    cut = slice((4 * n + g) * P, (4 * n + g + 1) * P)
                    alone = 4 * n + g == 0
                    last = mm(bank[n][:, g * P:(g + 1) * P], v_t[:, cut], att[:, cut], True, alone)
                    if not alone:
                        last = mm(bank[n][:, g * P:(g + 1) * P], s_st[:, cut], q_w[:, cut], False, True)
                last.then_inc(o_mm, 1)

            def att_stats(h):
                pe.wait_ge(o_cp, h * 2 + 2)
                for g in range(NC):
                    last = mm(bank[2][:, g:g + 1], o_sq[:, g * P:(g + 1) * P], ones[:, 0:1])
                last.then_inc(hst_mm, 1)

            def att_spread(h):
                pe.wait_ge(hdiag, h + 1)
                for n in range(2):
                    last = mm(bank[n][:, :], ones[:, :], att[:, n * HALF:(n + 1) * HALF])
                last.then_inc(hbc_mm, 1)

            def attention(h, first=False):
                def level(lv):
                    return lambda: att_level(h, lv)

                def start():
                    att_diag(h, first)
                    att_level(h, 0)

                return {(0, 1): start, (0, 3): level(1), (0, 5): level(2), (0, 7): lambda: att_vt(h, 0),
                        (1, 1): level(3), (1, 3): level(4), (1, 5): level(5), (1, 7): lambda: att_vt(h, 1),
                        (2, 1): level(6), (2, 3): lambda: att_kt(h), (2, 5): lambda: att_kv(h),
                        (2, 7): lambda: att_out(h, 0), (3, 1): lambda: att_out(h, 1),
                        (3, 3): lambda: att_stats(h), (3, 6): lambda: att_spread(h)}

            def hg_head(h, pieces, first=False):
                for k in range(4):
                    s = step_of(HG_IN, 4, h, k)
                    gaps = {at: piece for (step_at, at), piece in pieces.items() if step_at == k}
                    if first and k == 0:
                        gaps = norm_gaps(3, seen(HG_IN, 2))
                    step(s, B, ready=3 * NT + NT * BLOCKS if first and k == 0 else None, gaps=gaps)
                    sums(s, 1, events(s.t), seen(s.t, 3)).then_inc(mm_done, 1)

            hg_head(0, {}, first=True)
            hg_head(1, attention(0, first=True))
            with pe.Fori(2, NT) as i:
                hg_head(i, attention(i - 1))

            after_hg = 4 * NT + NT * BLOCKS
            pieces = list(attention(NT - 1).values())
            out_steps = [step_of(HG_OUT, 4, 0, n) for n in range(2)]
            for n, s in enumerate(out_steps):
                step(s, B, ready=after_hg if n == 0 else None, tiles=range(NT - 1),
                     gaps={k: pieces.pop(0) for k in range(NT - 1)})
            while pieces:
                pieces.pop(0)()
            for s in out_steps:
                step(s, B, ready=after_hg, tiles=range(NT - 1, NT)).then_inc(mm_done, 1)
            for n in range(2, NT):
                step(step_of(HG_OUT, 4, 0, n), B).then_inc(mm_done, 1)

            mlp(1, MLP1, 0, A, B, after_hg + 2 * NT, first=True)
            with pe.Fori(1, BLOCKS) as b:
                mlp(1, MLP1, b, A, B, after_hg + 2 * NT)

            stats(5, ev_mlp1(BLOCKS, 0) + 2 + 4)
            spread(5)
            for r in range(NC):
                if r >= 2:
                    pe.wait_ge(xt_cp, NT + r - 1)
                else:
                    pe.wait_ge(ps_free, END - 1 + r)
                for n in range(NT):
                    if r == 0:
                        pe.wait_ge(in_lo, after_hg + 2 * NT + NT * BLOCKS + n + 1)
                    last = pe.transpose(acc[r % 2][:, n * P:(n + 1) * P],
                                        at2[:, n, r * P:(r + 1) * P], ident[:, :])
                last.then_inc(xt_mm, 1)

        @block.scalar
        def _(act):
            def split_hi(s, fresh=False):
                act.wait_ge(w_loaded[s.odd], s.half * 16 + 16)
                if not fresh:
                    act.wait_ge(mm_done, s.t - 1)
                act.activation(w_hi[:, s.odd, :, :], stage[:, s.odd, :, :], ACT.Copy).then_inc(hi_ready, 1)

            def tile(buf, n):
                return buf[:, bass.ds(n, 1), :].rearrange("p a t -> p (a t)")

            def root(norm):
                act.wait_ge(ms_ready, norm)
                act.activation(nst[:, 1, :], nst[:, 0, :], ACT.Sqrt).then_inc(root_ready, 1)

            split_hi(step_of(0, 2, 0, 0), fresh=True)
            act.wait_ge(vec_c, 2)
            act.activation(cs[:, :], vec2[:, C_C:C_C + 8], ACT.Silu).then_inc(small_a, 1)
            act.wait_ge(small_d, 1)
            act.activation(sm[:, 1, :], sm[:, 0, :], ACT.Exp, scale=-1.0)
            act.activation(sm[:, 3:5, :], sm[:, 3:5, :], ACT.Exp).then_inc(small_a, 1)
            for n in range(NT):
                act.wait_ge(xt_mm, n + 1)
                act.activation(res[:, n, :], acc[n % 2][:, :], ACT.Copy).then_inc(xt_cp, 1)
            act.drain()
            act.wait_ge(small_d, 2)
            for n in range(NT):
                act.activation(a_hi[:, n, :], res[:, n, :], ACT.Identity, scale=amp[:, 0, n:n + 1]
                               ).then_inc(in_hi, 1)
            split_hi(step_of(0, 2, 0, 1), fresh=True)
            root(1)

            def vcol(at, h):
                return vec2[:, bass.ds(at + h, 1)]

            def gate_split(h, first=False):
                act.wait_ge(g_loaded, h * 32 + 32)
                if not first:
                    act.wait_ge(gate_mm, h * 4)
                act.activation(gw_hi[:, :, :], gst[:, :, :], ACT.Copy).then_inc(gw_hi_r, 1)

            def rg_even(h, first=False):
                act.wait_ge(scaled, h * 2 + 1)
                if first:
                    act.wait_ge(spilled, 16 * NT)
                    act.wait_ge(sq_done, 1)
                    act.wait_ge(in_lo, NT)
                    act.wait_ge(small_d, 4)
                else:
                    act.wait_ge(xc_done, h)
                act.activation(xbp[:, TAPS - 1:], acc[0][:, :], ACT.Identity, bias=bcol[:, 0:1]
                               ).then_inc(ps_free, 1)
                act.drain()
                if not first:
                    act.wait_ge(og_done, h)
                act.activation(xc, xbp[:, 0:T], ACT.Identity, scale=vcol(C_CW, h), bias=vcol(C_CB, h)
                               ).then_inc(xc0, 1)

            def rg_even_split(h, first=False):
                act.wait_ge(xc_done, h + 1)
                if not first:
                    act.wait_ge(gate_mm, h * 4)
                act.activation(xc_hi[:, :], xc, ACT.Copy).then_inc(xc_hi_r, 1)

            def rg_odd(h, first=False):
                act.wait_ge(scaled, h * 2 + 2)
                if not first:
                    act.wait_ge(og_done, h)
                act.activation(yb[:, :], acc[1][:, :], ACT.Identity, bias=bcol[:, 1:2]).then_inc(ps_free, 1)
                act.drain()
                act.activation(ytmp[:, :], yb[:, :], ACT.Square)
                act.drain()
                act.activation(ytmp[:, :], ytmp[:, :], ACT.Identity, scale=0.044715, bias=1.0
                               ).then_inc(y_poly, 1)

            def rg_gates(h):
                act.wait_ge(y_arg, h + 1)
                act.activation(ysig[:, :], ytmp[:, :], ACT.Sigmoid, scale=2 * 0.7978845608028654
                               ).then_inc(y_sig, 1)
                for g in range(2):
                    act.activation(gbias[:, g:g + 1], vcol((C_BA, C_BX)[g], h), ACT.Copy)
                act.drain()
                for q in range(4):
                    g, n = q % 2, q // 2
                    act.wait_ge(gate_mm, h * 4 + q + 1)
                    act.activation((r_g, i_g)[g][:, n * HALF:(n + 1) * HALF], bank[q % 3][:, :], ACT.Sigmoid,
                                   bias=gbias[:, g:g + 1]).then_inc(gate_rd, 1)
                act.drain()
                act.activation(th, r_g, ACT.Tanh, scale=decay[:, 0, bass.ds(h, 1)])
                act.activation(a_g, r_g, ACT.Exp, scale=decay[:, 1, bass.ds(h, 1)])
                act.drain()
                act.activation(m_g, a_g, ACT.Square).then_inc(ga_done, 1)
                act.wait_ge(gp_done, h + 1)
                act.activation(m_g, m_g, ACT.Sqrt).then_inc(gm_done, 1)

            gate_split(0, first=True)
            rg_even(0, first=True)
            split_hi(step_of(RG_IN, 2, 1, 0))
            rg_even_split(0, first=True)
            rg_odd(0, first=True)
            with act.Fori(1, NT) as j:
                split_hi(step_of(RG_IN, 2, j, 1))
                rg_gates(j - 1)
                gate_split(j)
                rg_even(j)
                split_hi(step_of(RG_IN, 2, j, 2))
                rg_even_split(j)
                rg_odd(j)
            split_hi(step_of(RG_OUT, 2, 0, 1))
            rg_gates(NT - 1)

            A, B = (a_hi, a_lo), (b_hi, b_lo)
            for n in range(NT):
                act.wait_ge(og_done, n + 1)
                act.activation(a_hi[:, n, :], o_rg[:, n, :], ACT.Copy).then_inc(in_hi, 1)

            def new_input(dst, k, n, x_before):
                act.wait_ge(x_new, x_before + n + 1)
                act.wait_ge(small_d, 4 + k)
                act.activation(tile(dst, n), tile(res, n), ACT.Identity, scale=amp[:, k, bass.ds(n, 1)]
                               ).then_inc(in_hi, 1)

            with act.Fori(0, 4) as m:
                for k in range(2):
                    split_hi(step_of(RG_OUT, 2, m, k + 2))
                    new_input(b_hi, 1, m * 2 + k, 0)

            def mlp(layer, base, b, hid, scaled_before, last=False, first=False):
                def one(q, k):
                    n = q * 4 + k
                    s = Step(base + b * (2 * NT) + n, None, k % 2)
                    act.wait_ge(scaled, scaled_before + b * NT + n + 1)
                    act.activation(acc[k % 2][:, :], acc[k % 2][:, :], ACT.Relu, bias=bcol[:, k % 2:k % 2 + 1])
                    act.drain()
                    act.activation(acc[k % 2][:, :], acc[k % 2][:, :], ACT.Square)
                    act.drain()
                    act.activation(tile(hid[0], n), acc[k % 2][:, :], ACT.Copy).then_inc(in_hi, 1)

                def ahead(q, k, off):
                    st = step_of(base + off, 2 * NT, b, k + 2)
                    split_hi(Step(st.t + q * 4, st.half + q * 2, st.odd))

                if first:
                    root(2 + 2 * layer)
                with act.Fori(0, 2) as q:
                    for k in range(4):
                        one(q, k)
                        ahead(q, k, 0)
                for q in range(2) if last and layer == 1 else [None]:
                    if q is None:
                        with act.Fori(0, 2) as q:
                            for k in range(4):
                                ahead(q, k, NT)
                                if last:
                                    new_input(last[0], last[1], q * 4 + k, last[2])
                    else:
                        for k in range(4):
                            if q * 4 + k < NT - 2:
                                ahead(q, k, NT)

            mlp(0, MLP0, 0, A, 2 * NT, first=True)
            with act.Fori(1, BLOCKS - 1) as b:
                mlp(0, MLP0, b, A, 2 * NT)
            mlp(0, MLP0, BLOCKS - 1, A, 2 * NT, last=(b_hi, 2, NT * BLOCKS))
            root(3)

            def hg_evict(h, k):
                act.wait_ge(scaled, h * 4 + (2 * NT + NT * BLOCKS) + k + 1)
                b = bcol[:, k % 2:k % 2 + 1]
                if k == 1:
                    act.activation(L_s, acc[1][:, :], ACT.Sigmoid, bias=b).then_inc(ps_free, 1)
                elif k == 2:
                    act.activation(L_v, acc[0][:, :], ACT.Identity, bias=b).then_inc(ps_free, 1)
                else:
                    act.activation(t_s, acc[k % 2][:, :], ACT.Sigmoid, bias=b).then_inc(sg_done, 1)

            def hg_vt(h, n):
                act.wait_ge(vt_mm, h * 2 + n + 1)
                act.activation(v_t[:, n * HALF:(n + 1) * HALF], bank[0][:, :], ACT.Copy).then_inc(vt_cp, 1)

            def hg_kt(h):
                for n in range(2):
                    act.wait_ge(kt_mm, h * 2 + n + 1)
                    act.activation(k_t[:, n * HALF:(n + 1) * HALF], bank[2 if n == 0 else 0][:, :], ACT.Copy
                                   ).then_inc(kt_cp, 1)

            def hg_o(h, n):
                cut = slice(n * HALF, (n + 1) * HALF)
                act.wait_ge(o_mm, h * 2 + n + 1)
                act.activation(o_sb[:, cut], bank[n][:, :], ACT.Copy)
                act.activation(o_sq[:, cut], bank[n][:, :], ACT.Square).then_inc(o_cp, 1)

            def hg_root(h):
                act.wait_ge(hms, h + 1)
                act.activation(nst[:, 1, :], nst[:, 0, :], ACT.Sqrt).then_inc(hroot, 1)

            def hg_step(i, k):
                split_hi(step_of(HG_IN, 4, i, k + 2))
                hg_evict(i, k)

            act.wait_ge(spilled, 2 * 16 * NT)
            act.wait_ge(sq_done, 3)
            act.wait_ge(in_lo, 3 * NT + NT * BLOCKS + NT)
            for k in range(4):
                hg_step(0, k)
            with act.Fori(1, NT) as i:
                hg_vt(i - 1, 0)
                hg_step(i, 0)
                hg_vt(i - 1, 1)
                hg_step(i, 1)
                hg_kt(i - 1)
                hg_o(i - 1, 0)
                hg_step(i, 2)
                hg_o(i - 1, 1)
                hg_root(i - 1)
                hg_step(i, 3)

            def head_split(n):
                act.activation(b_hi[:, n, :], o_hg[:, n, :], ACT.Copy).then_inc(in_hi, 1)

            act.wait_ge(on_done, NT - 1)
            act.wait_ge(mm_done, HG_OUT)
            for n in range(NT - 1):
                head_split(n)
            for n in range(2):
                hg_vt(NT - 1, n)
            hg_kt(NT - 1)
            for n in range(2):
                hg_o(NT - 1, n)
            hg_root(NT - 1)
            act.wait_ge(on_done, NT)
            head_split(NT - 1)
            with act.Fori(0, 2) as m:
                for k in range(4):
                    split_hi(step_of(HG_OUT, 4, m, k + 2))
                    new_input(a_hi, 3, m * 4 + k, NT + NT * BLOCKS)

            before = 2 * NT + NT * BLOCKS + 4 * NT
            mlp(1, MLP1, 0, B, before, first=True)
            with act.Fori(1, BLOCKS - 1) as b:
                mlp(1, MLP1, b, B, before)
            mlp(1, MLP1, BLOCKS - 1, B, before, last=True)
            root(5)
            for r in range(NC):
                act.wait_ge(xt_mm, NT + r + 1)
                act.activation(o_hg[:, r, :], acc[r % 2][:, :], ACT.Copy).then_inc(xt_cp, 1)

        @block.vector
        def _(dve):
            tt, ts, stt = dve.tensor_tensor, dve.tensor_scalar, dve.scalar_tensor_tensor

            def tile(buf, n):
                return buf[:, bass.ds(n, 1), :].rearrange("p a t -> p (a t)")

            def split_lo(s):
                dve.wait_ge(hi_ready, s.t + 1)
                tt(w_lo[:, s.odd, :, :], stage[:, s.odd, :, :], w_hi[:, s.odd, :, :].bitcast(f32),
                   ALU.subtract).then_inc(lo_ready, 1)

            def ops(*todo):
                for op in todo:
                    op()
                    dve.drain()

            dve.memset(nst[:, 3, :], 0.0)
            split_lo(step_of(0, 2, 0, 0))
            dve.wait_ge(vec_t, 2)
            dve.tensor_copy(vec1[:, :], bank[0][:, 0:P]).then_inc(vec_c, 1)
            dve.tensor_copy(vec2[:, :], bank[1][:, 0:V2]).then_inc(vec_c, 1)
            dve.drain()
            lam = vec2[:, C_LAM:C_LAM + 8]
            lb0, lb1 = vec2[:, C_LB:C_LB + 8], vec2[:, C_LB + 8:C_LB + 16]
            ops(lambda: ts(sm[:, 0, :], lam, -1.0, None, ALU.mult),
                lambda: ts(sm[:, 2, :], sm[:, 0, :], 0.0, None, ALU.max),
                lambda: tt(sm[:, 0, :], sm[:, 0, :], lam, ALU.max),
                lambda: tt(sm[:, 5, :], lb0, lb1, ALU.max),
                lambda: tt(sm[:, 3, :], lb0, sm[:, 5, :], ALU.subtract))
            tt(sm[:, 4, :], lb1, sm[:, 5, :], ALU.subtract).then_inc(small_d, 1)
            dve.wait_ge(small_a, 2)
            ops(lambda: tt(sm[:, 5, :], sm[:, 3, :], sm[:, 4, :], ALU.add),
                lambda: dve.reciprocal(sm[:, 5, :], sm[:, 5, :]),
                lambda: tt(sm[:, 3, :], sm[:, 3, :], sm[:, 5, :], ALU.mult),
                lambda: tt(sm[:, 4, :], sm[:, 4, :], sm[:, 5, :], ALU.mult),
                lambda: tt(sm[:, 4, :], sm[:, 3, :], sm[:, 4, :], ALU.add),
                lambda: tt(lbs[:, 0, :], sm[:, 4, :], sm[:, 3, :], ALU.subtract),
                lambda: ts(lbs[:, 1, :], lbs[:, 0, :], -1.0, 1.0, ALU.mult, ALU.add),
                lambda: ts(lbs[:, 2, :], lbs[:, 1, :], -1.0, None, ALU.mult))
            w, z, z2, p = sm[:, 1, :], sm[:, 3, :], sm[:, 4, :], sm[:, 5, :]
            ops(lambda: ts(z, w, 2.0, None, ALU.add),
                lambda: dve.reciprocal(z, z),
                lambda: tt(z, z, w, ALU.mult),
                lambda: tt(z2, z, z, ALU.mult),
                lambda: ts(p, z2, 2.0 / 17, 2.0 / 15, ALU.mult, ALU.add),
                *(lambda n=n, m=m: (tt(p, p, z2, ALU.mult) if m else ts(p, p, 2.0 / n, None, ALU.add))
                  for n in range(13, 0, -2) for m in (1, 0)),
                lambda: tt(p, p, z, ALU.mult),
                lambda: tt(p, p, sm[:, 2, :], ALU.add),
                lambda: ts(decay[:, 0, :], p, 8.0, None, ALU.mult),
                lambda: ts(decay[:, 1, :], p, -8.0, None, ALU.mult))

            def make_amp(k, table, name, gain):
                dve.drain()
                last = stt(amp[:, k, :], mod[:, table[name]:table[name] + NT], 1.0,
                           vec1[:, gain:gain + NT], ALU.add, ALU.mult)
                return last

            dve.wait_ge(vec_t, 3)
            at = MOD0["sc_t"]
            tt(mod[:, at:at + NT], cols[:, 0:NT], vec1[:, at:at + NT], ALU.add).then_inc(cols_read, 1)
            make_amp(0, MOD0, "sc_t", 96).then_inc(small_d, 1)

            def in_lo_res(dst, k, n, hi_before):
                dve.wait_ge(in_hi, hi_before + n + 1)
                stt(tile(dst[1], n), tile(res, n), amp[:, k, bass.ds(n, 1)],
                    tile(dst[0], n).bitcast(f32), ALU.mult, ALU.subtract).then_inc(in_lo, 1)

            A, B = (a_hi, a_lo), (b_hi, b_lo)
            dve.drain()
            for n in range(NT):
                in_lo_res(A, 0, n, 0)
            dve.wait_ge(vec_t, 4)
            tt(mod[:, 0:NT], cols[:, 0:NT], vec1[:, 0:NT], ALU.add).then_inc(cols_read, 1)
            dve.drain().then_inc(small_d, 1)
            split_lo(step_of(0, 2, 0, 1))
            dve.memset(xbp[:, 0:TAPS - 1], 0.0).then_inc(small_d, 1)

            def rms(src, n_mean, eps, after, ready, before, buf):
                ts(nst[:, 0, :], src, 1.0 / n_mean, eps, ALU.mult, ALU.add).then_inc(ready, 1)
                dve.wait_ge(after, before)
                ops(lambda: dve.reciprocal(nst[:, 2, :], nst[:, 1, :]),
                    lambda: tt(nst[:, 3, :], nst[:, 2, :], nst[:, 2, :], ALU.mult),
                    lambda: tt(nst[:, 3, :], nst[:, 3, :], nst[:, 0, :], ALU.mult),
                    lambda: ts(nst[:, 3, :], nst[:, 3, :], -0.5, 1.5, ALU.mult, ALU.add),
                    lambda: tt(nst[:, 2, :], nst[:, 2, :], nst[:, 3, :], ALU.mult))
                return tt(buf.rearrange("p (g t) -> p g t", t=P),
                          ident[:, :].unsqueeze(1).broadcast_to([P, NC, P]),
                          nst[:, 2, :].unsqueeze(2).broadcast_to([P, NC, P]), ALU.mult)

            def norm(n):
                dve.wait_ge(stat_mm, n)
                rms(cols[:, 0:NC], D, EPS, root_ready, ms_ready, n, tmp[:, :]).then_inc(diag_ready, 1)
                dve.drain().then_inc(cols_read, 1)
                dve.wait_ge(bc_mm, n)
                for q in range(2):
                    last = dve.tensor_copy(rstd[:, q * HALF:(q + 1) * HALF], bank[q][:, :])
                last.then_inc(rstd_ready, 1)
                dve.drain()

            def scale_sums(s, mods=0, at=None):
                dve.wait_ge(mm_done, s.t + 1)
                last = dve.tensor_copy(bcol[:, s.odd:s.odd + 1], cols[:, 0:1])
                if mods:
                    last = tt(mod[:, bass.ds(at, mods)], cols[:, 1:1 + mods], vec1[:, bass.ds(at, mods)], ALU.add)
                last.then_inc(cols_read, 1)
                return tt(acc[s.odd][:, :], acc[s.odd][:, :], rstd[:, :], ALU.mult).then_inc(scaled, 1)

            norm(1)

            def gate_split(h):
                dve.wait_ge(gw_hi_r, h + 1)
                tt(gw_lo[:, :, :], gst[:, :, :], gw_hi[:, :, :].bitcast(f32), ALU.subtract
                   ).then_inc(gw_lo_r, 1)

            def rg_conv(h):
                dve.wait_ge(xc0, h + 1)
                for k in range(1, TAPS):
                    stt(xc, xbp[:, k:k + T], vec2[:, bass.ds(C_CW + NT * k + h, 1)], xc,
                               ALU.mult, ALU.add)
                    last = dve.drain()
                last.then_inc(xc_done, 1)
                dve.wait_ge(xc_hi_r, h + 1)
                tt(xc_lo[:, :], xc, xc_hi[:, :].bitcast(f32), ALU.subtract).then_inc(xc_lo_r, 1)

            def rg_y(h):
                dve.wait_ge(y_poly, h + 1)
                tt(ytmp[:, :], ytmp[:, :], yb[:, :], ALU.mult).then_inc(y_arg, 1)

            def rg_scan(h):
                dve.wait_ge(ga_done, h + 1)
                stt(m_g, m_g, 1.0, th, ALU.add, ALU.mult).then_inc(gp_done, 1)
                dve.wait_ge(gm_done, h + 1)
                dve.memset(m_g[:, 0:1], 1.0)
                dve.drain()
                dve.wait_ge(ix_done, h + 1)
                tt(m_g, m_g, ix_g, ALU.mult)
                dve.drain()
                dve.tensor_tensor_scan(h_g, a_g, m_g, 0.0, ALU.mult, ALU.add)
                dve.drain()
                dve.wait_ge(gy_done, h + 1)
                tt(tile(o_rg, h), h_g, yb[:, :], ALU.mult).then_inc(og_done, 1)

            def rg_head(j):
                s = step_of(RG_IN, 2, j, 0)
                scale_sums(s, 1, j * 2 + 16)
                split_lo(step_of(RG_IN, 2, j, 2))
                rg_conv(j)
                s = step_of(RG_IN, 2, j, 1)
                scale_sums(s, 1, j * 2 + 17)
                rg_y(j)

            gate_split(0)
            rg_head(0)
            with dve.Fori(1, NT) as j:
                split_lo(step_of(RG_IN, 2, j, 1))
                rg_scan(j - 1)
                gate_split(j)
                rg_head(j)
            split_lo(step_of(RG_OUT, 2, 0, 1))
            rg_scan(NT - 1)
            for n in range(NT):
                dve.wait_ge(in_hi, NT + n + 1)
                tt(a_lo[:, n, :], o_rg[:, n, :], a_hi[:, n, :].bitcast(f32), ALU.subtract).then_inc(in_lo, 1)
            make_amp(1, MOD0, "sc_c", 112).then_inc(small_d, 1)
            dve.memset(rstd[:, :], 0.0)
            dve.drain()

            def renew(s, n, table, name):
                dve.wait_ge(mm_done, s.t + 1)
                return stt(tile(res, n), acc[s.odd][:, :], mod[:, bass.ds(table[name] + n, 1)], tile(res, n),
                           ALU.mult, ALU.add).then_inc(x_new, 1)

            def freed():
                dve.drain().then_inc(ps_free, 1)

            with dve.Fori(0, 4) as m:
                for k in range(2):
                    s, n = step_of(RG_OUT, 2, m, k), m * 2 + k
                    dve.wait_ge(reloaded[0], 16 * NT)
                    dve.wait_ge(mm_done, s.t + 1)
                    tt(mod[:, bass.ds(n * 2 + 32, 2)], cols[:, 0:2], vec1[:, bass.ds(n * 2 + 32, 2)], ALU.add
                       ).then_inc(cols_read, 1)
                    renew(s, n, MOD0, "g_t")
                    freed()
                    in_lo_res(B, 1, n, 2 * NT)
                    split_lo(step_of(RG_OUT, 2, m, k + 2))

            def mlp(layer, base, b, hid, tiles, last=False, first=False):
                table = MOD0 if layer == 0 else MOD1

                def ahead(q, k, off):
                    split_lo(Step(base + off + b * (2 * NT) + q * 4 + k + 2, None, k % 2))

                if first:
                    norm(2 + 2 * layer)
                with dve.Fori(0, 2) as q:
                    for k in range(4):
                        s = Step(base + b * (2 * NT) + q * 4 + k, None, k % 2)
                        scale_sums(s)
                        dve.wait_ge(in_hi, tiles + b * NT + q * 4 + k + 1)
                        tt(tile(hid[1], q * 4 + k), acc[s.odd][:, :], tile(hid[0], q * 4 + k).bitcast(f32),
                           ALU.subtract).then_inc(in_lo, 1)
                        freed()
                        ahead(q, k, 0)

                def out_step(q, k):
                    s = Step(base + NT + b * (2 * NT) + q * 4 + k, None, k % 2)
                    if layer == 0:
                        mods, at = 2 - k % 2, b * 12 + q * 6 + (0, 2, 3, 5)[k] + 48
                        dve.wait_ge(mm_done, s.t + 1)
                        tt(mod[:, bass.ds(at, mods)], cols[:, 0:mods], vec1[:, bass.ds(at, mods)], ALU.add
                           ).then_inc(cols_read, 1)
                    renew(s, q * 4 + k, table, "g_c")
                    freed()
                    if last and layer == 0:
                        in_lo_res(B, 2, q * 4 + k, 3 * NT + NT * BLOCKS)
                    if not (last and layer == 1 and q * 4 + k >= NT - 2):
                        ahead(q, k, NT)

                if last and layer == 0:
                    make_amp(2, MOD1, "sc_t", 104).then_inc(small_d, 1)
                    dve.drain()
                if last and layer == 1:
                    for q in range(2):
                        for k in range(4):
                            out_step(q, k)
                else:
                    with dve.Fori(0, 2) as q:
                        for k in range(4):
                            out_step(q, k)

            mlp(0, MLP0, 0, A, 3 * NT, first=True)
            with dve.Fori(1, BLOCKS - 1) as b:
                mlp(0, MLP0, b, A, 3 * NT)
            mlp(0, MLP0, BLOCKS - 1, A, 3 * NT, last=True)
            norm(3)

            def hg_evict(h, k):
                s = step_of(HG_IN, 4, h, k)
                scale_sums(s)
                split_lo(step_of(HG_IN, 4, h, k + 2))
                if k in (0, 3):
                    dve.wait_ge(sg_done, h * 2 + (1 if k == 0 else 2))
                    stt(L_q if k == 0 else L_g, acc[s.odd][:, :], bcol[:, s.odd:s.odd + 1], t_s,
                        ALU.add, ALU.mult).then_inc(ps_free, 1)

            def blocks(buf, size):
                return buf.rearrange("p (n two j) -> p n two j", two=2, j=size)

            tot_at = [0]
            for lv in range(LEVELS):
                tot_at.append(tot_at[-1] + (T >> (lv + 1)))

            def totals(lv):
                return f_w if lv == 0 else tot[:, tot_at[lv - 1]:tot_at[lv]]

            def hg_prep(h, first=False):
                if not first:
                    dve.wait_ge(o_mm, h * 2)
                dve.wait_ge(ps_free, h * 4 + (HG_IN + 2))
                lb = lambda n: lbs[:, n, bass.ds(h, 1)]
                ts(f_w, L_s, lb(1), lb(0), ALU.mult, ALU.add)
                ts(k_w, L_s, lb(2), lb(1), ALU.mult, ALU.add)
                dve.drain()
                tt(q_w, L_q, f_w, ALU.mult).then_inc(prep, 1)

            def hg_diag(h):
                for n in range(2):
                    dve.wait_ge(dg_mm, h * 2 + n + 1)
                    tt(att[:, n * HALF:(n + 1) * HALF].rearrange("p (g t) -> p g t", t=P),
                       bank[2 if n == 0 else 0][:, :].rearrange("p (g t) -> p g t", t=P),
                       ident[:, :].unsqueeze(1).broadcast_to([P, 4, P]), ALU.mult).then_inc(dg_rd, 1)

            def hg_reach(h, lv):
                size = 1 << lv
                dve.wait_ge(lv_mm, h * LEVELS + lv + 1)
                q4, k4 = blocks(q_w, size), blocks(k_w, size)
                t2 = totals(lv).rearrange("p (n two) -> p n two", two=2)
                shape = [P, T // 2 // size, size]
                tt(q4[:, :, 1, :], q4[:, :, 1, :], t2[:, :, 0:1].broadcast_to(shape), ALU.mult)
                tt(totals(lv + 1), t2[:, :, 0], t2[:, :, 1], ALU.mult)
                tt(k4[:, :, 0, :], k4[:, :, 0, :], t2[:, :, 1:2].broadcast_to(shape), ALU.mult
                   ).then_inc(lv_up, 1)
                dve.drain()

            def hg_take(h, lv):
                size = 1 << lv
                a5 = att.rearrange("p (g n two j) -> p g n two j", g=NC, two=2, j=size)[:, :, :, 1, :]
                m5 = mask[:, lv, :].rearrange("p (n j) -> p n j", j=size).bitcast(u32)
                dve.copy_predicated(
                    a5, m5.unsqueeze(1).broadcast_to([P, NC, P // 2 // size, size]),
                    bank[1 + lv % 2][:, :].rearrange("p (g n j) -> p g n j", g=NC, j=size)).then_inc(lv_rd, 1)

            def hg_levels(h, levels):
                for lv in levels:
                    hg_reach(h, lv)
                    if lv == 0:
                        hg_diag(h)
                        dve.drain()
                    hg_take(h, lv)

            def hg_states(h):
                for g in range(NC - 1):
                    if g % 4 == 0:
                        dve.wait_ge(kv_mm, h * 2 + g // 4 + 1)
                    src = bank[1 + g // 4][:, (g % 4) * P:(g % 4 + 1) * P]
                    dst = s_st[:, (g + 1) * P:(g + 2) * P]
                    if g == 0:
                        last = dve.tensor_copy(dst, src)
                    else:
                        last = stt(dst, s_st[:, g * P:(g + 1) * P], totals(LEVELS)[:, g:g + 1], src,
                                   ALU.mult, ALU.add)
                    if g == 2 or g == NC - 2:
                        last.then_inc(st_done, 1)
                    dve.drain()

            def hg_norm(h):
                dve.wait_ge(hst_mm, h + 1)
                rms(bank[2][:, 0:NC], P, GEPS, hroot, hms, h + 1, att).then_inc(hdiag, 1)

            def hg_o(h):
                dve.wait_ge(hbc_mm, h + 1)
                for n in range(2):
                    cut = slice(n * HALF, (n + 1) * HALF)
                    tt(o_sb[:, cut], o_sb[:, cut], bank[n][:, :], ALU.mult)
                dve.drain()
                stt(tile(o_hg, h), o_sb, vec2[:, C_GN:C_GN + 1], L_g, ALU.mult, ALU.mult).then_inc(on_done, 1)

            for k in range(4):
                hg_evict(0, k)
            hg_prep(0, first=True)
            with dve.Fori(1, NT) as i:
                hg_levels(i - 1, range(0, 3))
                hg_evict(i, 0)
                hg_levels(i - 1, range(3, 6))
                hg_evict(i, 1)
                hg_levels(i - 1, range(6, LEVELS))
                hg_states(i - 1)
                hg_evict(i, 2)
                hg_prep(i)
                hg_norm(i - 1)
                hg_o(i - 1)
                hg_evict(i, 3)
            after = 4 * NT + NT * BLOCKS

            def head_split(n):
                dve.wait_ge(in_hi, after + n + 1)
                tt(b_lo[:, n, :], o_hg[:, n, :], b_hi[:, n, :].bitcast(f32), ALU.subtract).then_inc(in_lo, 1)

            h = NT - 1
            head_split(0)
            for lv in range(LEVELS):
                for n in {2: (3, 4), 5: ()}.get(lv, (lv + 1 if lv < 2 else lv + 2,)):
                    if n < NT - 1:
                        head_split(n)
                hg_levels(h, [lv])
            hg_states(h)
            hg_norm(h)
            hg_o(h)
            head_split(h)
            make_amp(3, MOD1, "sc_c", 120).then_inc(small_d, 1)
            dve.drain()
            with dve.Fori(0, 2) as m:
                for k in range(4):
                    s, n = step_of(HG_OUT, 4, m, k), m * 4 + k
                    dve.wait_ge(reloaded[1], 16 * NT)
                    renew(s, n, MOD1, "g_t")
                    freed()
                    in_lo_res(A, 3, n, after + NT)
                    split_lo(step_of(HG_OUT, 4, m, k + 2))
            mlp(1, MLP1, 0, B, after + 2 * NT, first=True)
            with dve.Fori(1, BLOCKS - 1) as b:
                mlp(1, MLP1, b, B, after + 2 * NT)
            mlp(1, MLP1, BLOCKS - 1, B, after + 2 * NT, last=True)
            norm(5)
            for n in range(NT):
                stt(at2[:, n, :], res[:, n, :], vec2[:, C_NF + n:C_NF + n + 1], rstd[:, :],
                    ALU.mult, ALU.mult).then_inc(in_lo, 1)


_INS = ['x', 'c', 'mod_w', 'mod_b', 'norm_mix', 'norm_mlp', 'norm_final', 'rg_w_in', 'rg_conv_w',
        'rg_conv_b', 'rg_w_a', 'rg_b_a', 'rg_w_x', 'rg_b_x', 'rg_lambda', 'rg_w_out', 'hg_w_in',
        'hg_lower_bounds', 'hg_gnorm', 'hg_w_out', 'mlp_w1', 'mlp_w2']


def kernel(**inputs):
    import numpy as _np
    import concourse.bacc as _bacc
    from concourse import mybir as _mybir
    from concourse.bass_utils import run_bass_kernel_spmd as _run

    nc = _bacc.Bacc("TRN2", target_bir_lowering=False, num_devices=1)
    arrays, args = {}, []
    for name in _INS:
        a = _np.ascontiguousarray(inputs[name])
        arrays[f"in_{name}"] = a
        args.append(nc.dram_tensor(f"in_{name}", a.shape, _mybir.dt.from_np(a.dtype),
                                   kind="ExternalInput").ap())
    args.append(nc.dram_tensor("out_0", (1, T, D), _mybir.dt.float32, kind="ExternalOutput").ap())
    trunk(nc, *args)
    return _run(nc, [arrays], core_ids=[0]).results[0]["out_0"]
```

```python
from collections import namedtuple
from contextlib import ExitStack

import concourse.bass as bass
from concourse import mybir

P = 128
D = 1024
T = 1024
NT = D // P
NC = T // P
HALF = T // 2
DFF = 4 * D
BLOCKS = DFF // D
TAPS = 4
LEVELS = 7
EPS, GEPS = 1e-6, 1e-5

RG_IN, RG_OUT = 0, 2 * NT
MLP0 = RG_OUT + NT
HG_IN = MLP0 + 2 * NT * BLOCKS
HG_OUT = HG_IN + 4 * NT
MLP1 = HG_OUT + NT
END = MLP1 + 2 * NT * BLOCKS

MOD0 = {"sh_t": 0, "sc_t": 8, "g_t": 16, "sc_c": 24, "sh_c": 32, "g_c": 40}
MOD1 = {"sh_t": 48, "sc_t": 56, "g_t": 64, "sh_c": 72, "sc_c": 80, "g_c": 88}
PART = {"sh_t": 0, "sc_t": 1, "g_t": 2, "sh_c": 3, "sc_c": 4, "g_c": 5}
C_C, C_NF, C_CW, C_CB, C_BA, C_BX, C_LAM, C_LB, C_GN = 0, 8, 16, 48, 56, 64, 72, 80, 96
V2 = 97

Step = namedtuple("Step", "t half odd")


def step_of(base, mult, r, c):
    return Step(base + mult * r + c, base // 2 + (mult // 2) * r + c // 2, c % 2)


def trunk(nc, x, c, mod_w, mod_b, norm_mix, norm_mlp, norm_final, rg_w_in, rg_conv_w, rg_conv_b,
          rg_w_a, rg_b_a, rg_w_x, rg_b_x, rg_lambda, rg_w_out, hg_w_in, hg_lower_bounds, hg_gnorm,
          hg_w_out, mlp_w1, mlp_w2, out):
    f32, f32r, u32 = mybir.dt.float32, mybir.dt.float32r, mybir.dt.uint32
    ALU = mybir.AluOpType
    ACT = mybir.ActivationFunctionType
    x_spill = nc.dram_tensor("x_spill", (2, NT, P, T), f32, kind="Internal").ap()

    ctx = ExitStack()
    with ctx:
        def sb(name, shape, dt=f32):
            at = nc.sbuf_base
            h = ctx.enter_context(nc.sbuf_tensor(name, shape, dt))
            return h, at

        def over(name, shape, at, dt=f32):
            return nc.alloc_sbuf_tensor_at(name, shape, dt, offset=at)

        def sem(name):
            return ctx.enter_context(nc.semaphore(name))

        res, _ = sb("res", [P, NT, T])
        a_hi, at_ahi = sb("a_hi", [P, NT, T], f32r)
        a_lo, at_alo = sb("a_lo", [P, NT, T], f32r)
        b_hi, at_bhi = sb("b_hi", [P, NT, T], f32r)
        b_lo, at_blo = sb("b_lo", [P, NT, T], f32r)
        w_hi, _ = sb("w_hi", [P, 2, NT, P], f32r)
        w_lo, _ = sb("w_lo", [P, 2, NT, P], f32r)
        stage, _ = sb("stage", [P, 2, NT, P])
        mstage, _ = sb("mstage", [P, 2, NT, P])
        rstd, _ = sb("rstd", [P, T])
        tmp, _ = sb("tmp", [P, T])
        pv, _ = sb("pv", [P, 2, 2, P])
        ident, _ = sb("ident", [P, P])
        mask, _ = sb("mask", [P, LEVELS, P // 2])
        vec1, _ = sb("vec1", [P, P])
        vec2, _ = sb("vec2", [P, V2])
        mod, _ = sb("mod", [P, 96])
        amp, _ = sb("amp", [P, 4, NT])
        cs, _ = sb("cs", [P, NT])
        decay, _ = sb("decay", [P, 2, NT])
        lbs, _ = sb("lbs", [P, 3, NT])
        sm, _ = sb("sm", [P, 6, NT])
        bcol, _ = sb("bcol", [P, 2])
        gbias, _ = sb("gbias", [P, 2])
        nst, _ = sb("nst", [P, 4, NT])
        ones = over("ones", [P, P], nc.sbuf_base)
        _, _ = sb("ones_slab", [P, P])

        xin = over("xin", [P, NT, D], at_blo)
        w_scale = over("w_scale", [P, NT, D], at_bhi)
        w_shift = over("w_shift", [P, NT, D], at_blo)
        scale_sum = over("scale_sum", [P, D], at_alo)
        o_rg = over("o_rg", [P, NT, T], at_blo)
        o_hg = over("o_hg", [P, NT, T], at_alo)
        K4 = 4
        xbp = over("xbp", [P, T + TAPS - 1], at_bhi)
        gst = over("gst", [P, 2, P], at_bhi + 1032 * K4)
        gw_hi = over("gw_hi", [P, 2, P], at_bhi + 1288 * K4, f32r)
        gw_lo = over("gw_lo", [P, 2, P], at_bhi + 1544 * K4, f32r)
        xc_hi = over("xc_hi", [P, T], at_bhi + 1800 * K4, f32r)
        xc_lo = over("xc_lo", [P, T], at_bhi + 2824 * K4, f32r)
        yb = over("yb", [P, T], at_bhi + 3848 * K4)
        ysig = over("ysig", [P, T], at_bhi + 4872 * K4)
        ytmp = over("ytmp", [P, T], at_bhi + 5896 * K4)
        shift_sum = over("shift_sum", [P, D], at_bhi + 4872 * K4)
        xc, r_g, i_g, th, a_g, m_g, ix_g, h_g = (res[:, n, :] for n in range(8))
        at2 = over("at2", [P, NT, T], at_ahi)
        L_q, L_s, L_v, L_g, q_w, k_w, f_w, tot = (res[:, n, :] for n in range(8))
        v_t, k_t, att, s_st, o_sb, o_sq, t_s = (at2[:, n, :] for n in range(7))

        acc = [ctx.enter_context(nc.psum_tensor(f"acc{n}", [P, T], f32)) for n in range(2)]
        bank = [ctx.enter_context(nc.psum_tensor(f"bank{n}", [P, HALF], f32)) for n in range(3)]
        cols = ctx.enter_context(nc.psum_tensor("cols", [P, HALF], f32))

        vec_loaded = sem("vec_loaded")
        x_loaded = [sem(f"x_loaded{r}") for r in range(NC)]
        scale_loaded = [sem(f"scale_loaded{k}") for k in range(NT)]
        shift_loaded = [sem(f"shift_loaded{k}") for k in range(NT)]
        x_squared, wsum_done = sem("x_squared"), sem("wsum_done")
        w_loaded = [sem(f"w_loaded{n}") for n in range(2)]
        m_loaded = [sem(f"m_loaded{n}") for n in range(2)]
        g_loaded = sem("g_loaded")
        spilled, spilled0 = sem("spilled"), sem("spilled0")
        reloaded = [sem("reloaded0"), sem("reloaded1")]
        stored = sem("stored")
        consts = sem("consts")
        vec_t, vec_c, small_a, small_d = sem("vec_t"), sem("vec_c"), sem("small_a"), sem("small_d")
        xt_mm, xt_cp = sem("xt_mm"), sem("xt_cp")
        gained, out_mm = sem("gained"), sem("out_mm")
        row_out = [sem("row_out0"), sem("row_out1")]
        last_rms = sem("last_rms")
        hi_ready, lo_ready = sem("hi_ready"), sem("lo_ready")
        in_hi, in_lo = sem("in_hi"), sem("in_lo")
        mm_done, ps_free = sem("mm_done"), sem("ps_free")
        scaled = sem("scaled")
        sums_ready = sem("sums_ready")
        mod_used = sem("mod_used")
        cols_read = sem("cols_read")
        stat_mm, ms_ready, root_ready, diag_ready, bc_mm, rstd_ready = (
            sem(n) for n in ("stat_mm", "ms_ready", "root_ready", "diag_ready", "bc_mm", "rstd_ready"))
        x_new = sem("x_new")
        sq_part = sem("sq_part")
        sq_added = sem("sq_added")
        relu_done = sem("relu_done")
        xb_out, xc0, xc_done, gw_hi_r, gw_lo_r = (
            sem(n) for n in ("xb_out", "xc0", "xc_done", "gw_hi_r", "gw_lo_r"))
        xc_hi_r, xc_lo_r = sem("xc_hi_r"), sem("xc_lo_r")
        gate_mm, gate_rd = sem("gate_mm"), sem("gate_rd")
        y_poly, y_arg, y_sig, gy_done = (sem(n) for n in ("y_poly", "y_arg", "y_sig", "gy_done"))
        ga_done, gp_done, gm_done, ix_done, og_done = (
            sem(n) for n in ("ga_done", "gp_done", "gm_done", "ix_done", "og_done"))
        sg_done = sem("sg_done")
        vt_mm, vt_cp = sem("vt_mm"), sem("vt_cp")
        prep = sem("prep")
        dg_mm, dg_rd = sem("dg_mm"), sem("dg_rd")
        lv_mm, lv_rd, lv_up = sem("lv_mm"), sem("lv_rd"), sem("lv_up")
        kt_mm, kt_cp, kv_mm, st_done = sem("kt_mm"), sem("kt_cp"), sem("kv_mm"), sem("st_done")
        o_mm, o_cp = sem("o_mm"), sem("o_cp")
        hst_mm, hms, hroot, hdiag, hbc_mm, on_done = (
            sem(n) for n in ("hst_mm", "hms", "hroot", "hdiag", "hbc_mm", "on_done"))

        def events(t):
            return t

        def ev_mlp1(b, n):
            return HG_OUT + NT * b + n

        def seen(t, norms):
            return t + 2 + norms

        def tiled(w):
            return w.rearrange("(k p) n -> p k n", p=P)

        SPILLED0, SPILLED1 = 16 * (NT - 1), 16 * (2 * NT - 1)

        block = ctx.enter_context(nc.Block())

        @block.sync
        def _(sp):
            for r in range(NC):
                sp.dma_start(xin[:, r, :], x[0, r * P:(r + 1) * P, :]).then_inc(x_loaded[r], 16)

            def mod_part(layer, name):
                return tiled(mod_w[layer])[:, :, D * PART[name]:D * PART[name] + D]

            for k in range(NT):
                sp.dma_start(w_scale[:, k, :], mod_part(0, "sc_t")[:, k, :]).then_inc(scale_loaded[k], 16)

            def load_w(s, src, summed=None, split=None):
                if summed is not None:
                    sp.wait_ge(sums_ready, summed)
                if split is not None:
                    sp.wait_ge(lo_ready, split)
                sp.dma_start(stage[:, s.odd, :, :], src).then_inc(w_loaded[s.odd], 16)

            def load_mod(n, odd, src):
                sp.dma_start(mstage[:, odd, :, :], src).then_inc(m_loaded[odd], 16)

            rg_in = tiled(rg_w_in[0]).rearrange("p k (s n c) -> p k s n c", s=2, c=P)
            rg_out = tiled(rg_w_out[0])
            hg_in = tiled(hg_w_in[0]).rearrange("p k (s n c) -> p k s n c", s=4, c=P)
            hg_out = tiled(hg_w_out[0])

            load_w(step_of(0, 2, 0, 0), rg_in[:, :, 0, 0, :])
            load_w(step_of(0, 2, 0, 1), rg_in[:, :, 1, 0, :])
            sp.wait_ge(xt_cp, NC)
            sp.dma_start(x_spill[0, 0], res[:, 0, :]).then_inc(spilled0, 16)
            sp.wait_ge(x_squared, NC)
            for k in range(NT):
                sp.dma_start(w_shift[:, k, :], mod_part(0, "sh_t")[:, k, :]).then_inc(shift_loaded[k], 16)
            g_t, sc_c = mod_part(0, "g_t"), mod_part(0, "sc_c")
            load_mod(0, 0, g_t[:, :, 0:P])
            load_mod(1, 1, g_t[:, :, P:2 * P])
            for n in range(1, NT):
                sp.dma_start(x_spill[0, n], res[:, n, :]).then_inc(spilled, 16)

            def load_gate(h):
                sp.dma_start(gst[:, 0, :], rg_w_a[0, bass.ds(h, 1)].rearrange("a p n -> p (a n)")
                             ).then_inc(g_loaded, 16)
                sp.dma_start(gst[:, 1, :], rg_w_x[0, bass.ds(h, 1)].rearrange("a p n -> p (a n)")
                             ).then_inc(g_loaded, 16)

            sp.wait_ge(small_d, 2)
            load_gate(0)

            def rg_loads(j, part, at):
                for k in range(2):
                    s = step_of(RG_IN, 2, j, k)
                    load_w(s, rg_in[:, :, k, bass.ds(j, 1), :].rearrange("p k a c -> p k (a c)"), s.t - 1)
                    sp.wait_ge(mod_used, s.t - 1)
                    load_mod(s.t, k, part[:, :, bass.ds(at + k * P, P)])
                sp.wait_ge(gw_lo_r, j)
                load_gate(j)

            with sp.Fori(1, 4) as j:
                rg_loads(j, g_t, j * (2 * P))
            with sp.Fori(4, 8) as j:
                rg_loads(j, sc_c, j * (2 * P) - D)

            def rg_out_loads(m, part, at):
                for k in range(2):
                    s = step_of(RG_OUT, 2, m, k)
                    load_w(s, rg_out[:, :, bass.ds(m * (2 * P) + k * P, P)], s.t - 1)
                    for q in range(2):
                        n = 2 * NT + m * 4 + 2 * k + q
                        sp.wait_ge(mod_used, n - 1)
                        load_mod(n, q, part[:, :, bass.ds(at + (2 * k + q) * P, P)])

            def reload(which):
                for n in range(NT):
                    sp.dma_start(res[:, n, :], x_spill[which, n]).then_inc(reloaded[which], 16)

            rg_out_loads(0, mod_part(0, "sh_c"), 0)
            sp.wait_ge(og_done, NT)
            reload(0)
            rg_out_loads(1, mod_part(0, "sh_c"), 4 * P)
            with sp.Fori(2, 4) as m:
                rg_out_loads(m, mod_part(0, "g_c"), m * (4 * P) - D)

            mod1 = tiled(mod_w[1])

            def mlp_loads(layer, base, b):
                w1 = tiled(mlp_w1[layer])
                w2 = mlp_w2[layer].rearrange("(b k p) n -> p b k n", p=P, k=NT)
                for n in range(NT):
                    s = step_of(base, 2 * NT, b, n)
                    src = w1[:, :, bass.ds(b * D + n * P, P)]
                    if layer == 0:
                        load_w(s, src, summed=s.t - 1)
                    elif n < 2:
                        load_w(s, src, split=s.t - 1)
                    else:
                        load_w(s, src, summed=ev_mlp1(b, n - 1))
                m = 0
                for n in range(NT):
                    s = step_of(base + NT, 2 * NT, b, n)
                    src = w2[:, bass.ds(b, 1), :, n * P:(n + 1) * P].rearrange("p a k n -> p (a k) n")
                    if layer == 0:
                        load_w(s, src, summed=s.t - 1)
                    elif n < 2:
                        load_w(s, src, summed=ev_mlp1(b, NT - 1 + n))
                    else:
                        load_w(s, src, split=s.t - 1)
                    for _ in range(2 - n % 2 if layer == 0 else 0):
                        sp.wait_ge(mod_used, b * 12 + (m + 31))
                        load_mod(None, m % 2, mod1[:, :, bass.ds(b * (12 * P) + m * P, P)])
                        m += 1

            with sp.Fori(0, BLOCKS) as b:
                mlp_loads(0, MLP0, b)

            def hg_loads(h, ks=range(4)):
                for k in ks:
                    s = step_of(HG_IN, 4, h, k)
                    load_w(s, hg_in[:, :, k, bass.ds(h, 1), :].rearrange("p k a c -> p k (a c)"), s.t - 1)

            hg_loads(0, (0, 1))
            for n in range(NT):
                sp.wait_ge(x_new, NT + NT * (BLOCKS - 1) + n + 1)
                sp.dma_start(x_spill[1, n], res[:, n, :]).then_inc(spilled, 16)
            hg_loads(0, (2, 3))
            with sp.Fori(1, NT) as h:
                hg_loads(h)
            sp.wait_ge(sums_ready, HG_OUT)
            for n in range(NT):
                s = step_of(HG_OUT, 2 * NT, 0, n)
                load_w(s, hg_out[:, :, n * P:(n + 1) * P], split=s.t - 1)
                if n == 2:
                    sp.wait_ge(on_done, NT)
                    reload(1)
            with sp.Fori(0, BLOCKS) as b:
                mlp_loads(1, MLP1, b)
            for r in range(NC):
                sp.wait_ge(row_out[r % 2], r // 2 + 1)
                sp.dma_start(out[0, r * P:(r + 1) * P, :], o_hg[:, r, :]).then_inc(stored, 16)
            sp.wait_ge(stored, 16 * NC)
            sp.wait_ge(spilled0, 16)
            sp.wait_ge(spilled, SPILLED1)

        @block.gpsimd
        def _(pool):
            pool.memset(ident[:, :], 0.0)
            pool.memset(ones[:, :], 1.0)
            pool.memset(mask[:, :, :], 1.0)
            pool.drain()
            pool.affine_select(out=ident[:, :], in_=ident[:, :], compare_op=ALU.not_equal, fill=1.0,
                               base=0, pattern=[[-1, P]], channel_multiplier=1)
            for lv in range(LEVELS):
                h = 1 << lv
                m = mask[:, lv, :].rearrange("p (n j) -> p n j", j=h)
                pool.affine_select(out=m, in_=m, compare_op=ALU.is_ge, fill=0.0, base=0,
                                   pattern=[[-2 * h, P // 2 // h], [0, h]], channel_multiplier=1)
                pool.drain()
                pool.affine_select(out=m, in_=m, compare_op=ALU.is_ge, fill=0.0, base=h - 1,
                                   pattern=[[2 * h, P // 2 // h], [0, h]], channel_multiplier=-1)
            pool.drain().then_inc(consts, 1)

            def sums(buf, vector, slot):
                pool.tensor_tensor(buf, buf, vector.unsqueeze(2).broadcast_to([P, NT, P]), ALU.mult)
                pool.drain()
                pool.tensor_tensor(buf[:, 0:4, :], buf[:, 0:4, :], buf[:, 4:8, :], ALU.add)
                pool.drain()
                pool.tensor_tensor(buf[:, 0:2, :], buf[:, 0:2, :], buf[:, 2:4, :], ALU.add)
                pool.drain()
                return pool.tensor_tensor(slot, buf[:, 0, :], buf[:, 1, :], ALU.add)

            def w_sums(s, shift):
                pool.wait_ge(lo_ready, s.t + 1)
                return sums(stage[:, s.odd, :, :], shift, pv[:, s.odd, 0, :])

            def m_sums(odd, loads, s, slot):
                pool.wait_ge(m_loaded[odd], loads * 16)
                last = sums(mstage[:, odd, :, :], cs[:, :], pv[:, s.odd, slot, :])
                last.then_inc(mod_used, 1)
                pool.drain()

            def pv_free(s):
                pool.wait_ge(mm_done, s.t - 1)

            def mark():
                pool.drain().then_inc(sums_ready, 1)

            def shift_of(table, name):
                return mod[:, table[name]:table[name] + NT]

            pool.wait_ge(small_d, 3)

            def rg_sums(j, k, first=False):
                s = step_of(RG_IN, 2, j, k)
                if not first:
                    pv_free(s)
                w_sums(s, shift_of(MOD0, "sh_t"))
                m_sums(k, j + 1, s, 1)
                mark()

            def rg_gy(h):
                pool.wait_ge(y_sig, h + 1)
                pool.tensor_tensor(yb[:, :], yb[:, :], ysig[:, :], ALU.mult).then_inc(gy_done, 1)

            for k in range(2):
                rg_sums(0, k, first=True)
            with pool.Fori(1, NT) as j:
                rg_sums(j, 0)
                rg_gy(j - 1)
                rg_sums(j, 1)
            rg_gy(NT - 1)

            def rg_out_sums(m):
                for k in range(2):
                    s = step_of(RG_OUT, 2, m, k)
                    pv_free(s)
                    pool.wait_ge(lo_ready, s.t + 1)
                    for q in range(2):
                        m_sums(q, NT + m * 2 + k + 1, s, q)
                    mark()

            with pool.Fori(0, 4) as m:
                rg_out_sums(m)

            def mlp_sums(layer, base, b):
                table = MOD0 if layer == 0 else MOD1
                with pool.Fori(0, 2) as q:
                    for k in range(4):
                        s = Step(base + b * (2 * NT) + q * 4 + k, None, k % 2)
                        pv_free(s)
                        w_sums(s, shift_of(table, "sh_c"))
                        mark()
                if layer == 1:
                    return
                with pool.Fori(0, 2) as q:
                    n = 0
                    for k in range(4):
                        s = Step(base + NT + b * (2 * NT) + q * 4 + k, None, k % 2)
                        pv_free(s)
                        pool.wait_ge(lo_ready, s.t + 1)
                        for slot in range(2 - k % 2):
                            m_sums(n % 2, b * 6 + q * 3 + (n // 2 + 1) + 2 * NT, s, slot)
                            n += 1
                        mark()

            with pool.Fori(0, BLOCKS) as b:
                mlp_sums(0, MLP0, b)
            with pool.Fori(0, NT) as h:
                for k in range(4):
                    s = step_of(HG_IN, 4, h, k)
                    pv_free(s)
                    w_sums(s, shift_of(MOD1, "sh_t"))
                    mark()
            with pool.Fori(0, BLOCKS) as b:
                mlp_sums(1, MLP1, b)

        @block.tensor
        def _(pe):
            def mm(dst, lhs, rhs, start=True, stop=True):
                return pe.matmul(dst, lhs, rhs, start=start, stop=stop)

            pe.wait_ge(consts, 1)
            for r in range(NC):
                if r >= 2:
                    pe.wait_ge(xt_cp, r - 1)
                pe.wait_ge(x_loaded[r], 16)
                for n in range(NT):
                    last = pe.transpose(acc[r % 2][:, n * P:(n + 1) * P], xin[:, r, n * P:(n + 1) * P],
                                        ident[:, :])
                last.then_inc(xt_mm, 1)
                if r == NC // 2:
                    pe.wait_ge(vec_loaded, 16 * 18)
                    pe.transpose(bank[0][:, 0:P], rstd[:, 0:P], ident[:, :]).then_inc(vec_t, 1)
                    pe.transpose(bank[1][:, 0:V2], rstd[0:V2, P:2 * P], ident[0:V2, 0:V2]).then_inc(vec_t, 1)

            def over_partitions(sums_of, n_before):
                pe.wait_ge(wsum_done, n_before + 1)
                if n_before:
                    pe.wait_ge(cols_read, n_before)
                for n in range(NT):
                    last = mm(cols[:, n:n + 1], sums_of[:, n * P:(n + 1) * P], ones[:, 0:1])
                last.then_inc(vec_t, 1)

            over_partitions(scale_sum, 0)

            def step(s, src, ready=None, gaps=None, fresh=False, tiles=range(NT)):
                hi, lo = src
                if tiles[0] == 0:
                    pe.wait_ge(lo_ready, s.t + 1)
                    if not fresh:
                        pe.wait_ge(ps_free, s.t - 1)
                for k in tiles:
                    if ready is not None:
                        pe.wait_ge(in_lo, ready + k + 1)
                    for w, parts in ((w_hi, (hi, lo)), (w_lo, (hi,))):
                        for v in parts:
                            for n in range(2):
                                last = mm(acc[s.odd][:, n * HALF:(n + 1) * HALF], w[:, s.odd, k, :],
                                          v[:, k, n * HALF:(n + 1) * HALF],
                                          k == 0 and w is w_hi and v is hi,
                                          k == NT - 1 and w is w_lo)
                    if gaps and k in gaps:
                        gaps[k]()
                return last

            def sums(s, n, events_before, cols_before):
                pe.wait_ge(sums_ready, events_before + 1)
                pe.wait_ge(cols_read, cols_before)
                for i in range(n):
                    last = mm(cols[:, i:i + 1], pv[:, s.odd, i, :], ones[:, 0:1])
                return last

            def stats(norm, cols_before):
                pe.wait_ge(sq_added, 9 * (norm - 1))
                pe.wait_ge(cols_read, cols_before)
                for g in range(NC):
                    last = mm(cols[:, g:g + 1], rstd[:, g * P:(g + 1) * P], ones[:, 0:1])
                last.then_inc(stat_mm, 1)

            def spread(norm):
                pe.wait_ge(diag_ready, norm)
                for n in range(2):
                    last = mm(bank[n][:, :], ones[:, :], tmp[:, n * HALF:(n + 1) * HALF])
                last.then_inc(bc_mm, 1)

            def norm_gaps(norm, cols_before):
                return {5: lambda: stats(norm, cols_before), 7: lambda: spread(norm)}

            A, B = (a_hi, a_lo), (b_hi, b_lo)

            def gates(j, first=False):
                pe.wait_ge(gw_lo_r, j + 1)
                pe.wait_ge(xc_lo_r, j + 1)
                if first:
                    pe.wait_ge(rstd_ready, 1)
                else:
                    pe.wait_ge(gate_rd, j * 4)
                for q in range(4):
                    g, n = q % 2, q // 2
                    if q == 3:
                        pe.wait_ge(gate_rd, j * 4 + 1)
                    cut = slice(n * HALF, (n + 1) * HALF)
                    mm(bank[q % 3][:, :], gw_hi[:, g, :], xc_hi[:, cut], True, False)
                    mm(bank[q % 3][:, :], gw_hi[:, g, :], xc_lo[:, cut], False, False)
                    mm(bank[q % 3][:, :], gw_lo[:, g, :], xc_hi[:, cut], False, True).then_inc(gate_mm, 1)

            def in_sums(s):
                sums(s, 2, events(s.t), seen(s.t, 0)).then_inc(mm_done, 1)

            s0, s1 = step_of(RG_IN, 2, 0, 0), step_of(RG_IN, 2, 0, 1)
            step(s0, A, ready=0, fresh=True, gaps={6: lambda: spread(1)})
            step(s1, A, fresh=True, gaps={2: lambda: over_partitions(shift_sum, 1), 6: lambda: in_sums(s0)})
            in_sums(s1)
            for j in range(1, 2):
                for k in range(2):
                    s = step_of(RG_IN, 2, j, k)
                    step(s, A, gaps={3: lambda: gates(j - 1, first=True)} if k == 0 else None)
                    in_sums(s)
            with pe.Fori(2, NT) as j:
                for k in range(2):
                    s = step_of(RG_IN, 2, j, k)
                    step(s, A, gaps={3: lambda: gates(j - 1)} if k == 0 else None)
                    in_sums(s)
            gates(NT - 1)
            out_steps = [step_of(RG_OUT, 2, 0, n) for n in range(2)]
            for n, s in enumerate(out_steps):
                step(s, A, ready=NT if n == 0 else None, tiles=range(NT - 1))
            for s in out_steps:
                step(s, A, ready=NT, tiles=range(NT - 1, NT))
                in_sums(s)
            with pe.Fori(1, 4) as m:
                for k in range(2):
                    s = step_of(RG_OUT, 2, m, k)
                    step(s, A)
                    sums(s, 2, events(s.t), seen(s.t, 0)).then_inc(mm_done, 1)

            def mlp(layer, base, b, src, hid, tiles, first=False):
                norms = 1 if layer == 0 else None
                for q in range(2):
                    for k in range(4):
                        n = q * 4 + k
                        s = step_of(base, 2 * NT, b, n)
                        head = first and n == 0
                        step(s, src, ready=tiles - NT if head else None,
                             gaps=norm_gaps(2 + 2 * layer, seen(MLP0, 0) if layer == 0 else
                                            seen(HG_OUT, 2)) if head else None)
                        if layer == 0:
                            sums(s, 1, events(s.t), seen(s.t, norms)).then_inc(mm_done, 1)
                        else:
                            sums(s, 1, ev_mlp1(b, n), ev_mlp1(b, n) + 2 + 3).then_inc(mm_done, 1)
                for n in range(NT):
                    s = step_of(base + NT, 2 * NT, b, n)
                    last = step(s, hid, ready=tiles + b * NT if n == 0 else None)
                    if layer == 0:
                        last = sums(s, 2 - n % 2, events(s.t), seen(s.t, norms))
                    last.then_inc(mm_done, 1)

            mlp(0, MLP0, 0, B, A, 3 * NT, first=True)
            with pe.Fori(1, BLOCKS) as b:
                mlp(0, MLP0, b, B, A, 3 * NT)

            def att_diag(h, first=False):
                pe.wait_ge(prep, h + 1)
                if first:
                    pe.wait_ge(rstd_ready, 3)
                else:
                    pe.wait_ge(on_done, h)
                for n in range(2):
                    for g in range(4):
                        cut = slice((4 * n + g) * P, (4 * n + g + 1) * P)
                        last = mm(bank[2 if n == 0 else 0][:, g * P:(g + 1) * P], k_w[:, cut], L_q[:, cut])
                    last.then_inc(dg_mm, 1)

            def att_vt(h, n):
                if n == 0:
                    pe.wait_ge(ps_free, h * 4 + (HG_IN + 3))
                    pe.wait_ge(dg_rd, h * 2 + 2)
                else:
                    pe.wait_ge(vt_cp, h * 2 + 1)
                for g in range(4):
                    last = pe.transpose(bank[0][:, g * P:(g + 1) * P],
                                        L_v[:, (4 * n + g) * P:(4 * n + g + 1) * P], ident[:, :])
                last.then_inc(vt_mm, 1)

            def att_level(h, lv):
                size = 1 << lv
                if lv == 1:
                    pe.wait_ge(dg_rd, h * 2 + 1)
                if lv:
                    pe.wait_ge(lv_up, h * LEVELS + lv)
                if lv >= 2:
                    pe.wait_ge(lv_rd, h * LEVELS + lv - 1)
                q4 = q_w.rearrange("p (g n two j) -> p g n two j", g=NC, two=2, j=size)
                for g in range(NC):
                    last = mm(bank[1 + lv % 2][:, g * 64:(g + 1) * 64].rearrange("p (n j) -> p n j", j=size),
                              k_w[:, g * P:(g + 1) * P], q4[:, g, :, 1, :])
                last.then_inc(lv_mm, 1)

            def att_kt(h):
                pe.wait_ge(lv_up, h * LEVELS + LEVELS)
                pe.wait_ge(vt_cp, h * 2 + 2)
                pe.wait_ge(lv_rd, h * LEVELS + LEVELS - 1)
                for n in range(2):
                    for g in range(4):
                        last = pe.transpose(bank[2 if n == 0 else 0][:, g * P:(g + 1) * P],
                                            k_w[:, (4 * n + g) * P:(4 * n + g + 1) * P], ident[:, :])
                    last.then_inc(kt_mm, 1)

            def att_kv(h):
                pe.wait_ge(lv_rd, h * LEVELS + LEVELS)
                for n in range(2):
                    pe.wait_ge(kt_cp, h * 2 + 1 + n)
                    for g in range(4 - n):
                        cut = slice((4 * n + g) * P, (4 * n + g + 1) * P)
                        last = mm(bank[1 + n][:, g * P:(g + 1) * P], k_t[:, cut], v_t[:, cut])
                    last.then_inc(kv_mm, 1)

            def att_out(h, n):
                pe.wait_ge(st_done, h * 2 + 1 + n)
                for g in range(4):
                    cut = slice((4 * n + g) * P, (4 * n + g + 1) * P)
                    alone = 4 * n + g == 0
                    last = mm(bank[n][:, g * P:(g + 1) * P], v_t[:, cut], att[:, cut], True, alone)
                    if not alone:
                        last = mm(bank[n][:, g * P:(g + 1) * P], s_st[:, cut], q_w[:, cut], False, True)
                last.then_inc(o_mm, 1)

            def att_stats(h):
                pe.wait_ge(o_cp, h * 2 + 2)
                for g in range(NC):
                    last = mm(bank[2][:, g:g + 1], o_sq[:, g * P:(g + 1) * P], ones[:, 0:1])
                last.then_inc(hst_mm, 1)

            def att_spread(h):
                pe.wait_ge(hdiag, h + 1)
                for n in range(2):
                    last = mm(bank[n][:, :], ones[:, :], att[:, n * HALF:(n + 1) * HALF])
                last.then_inc(hbc_mm, 1)

            def attention(h, first=False):
                def level(lv):
                    return lambda: att_level(h, lv)

                def start():
                    att_diag(h, first)
                    att_level(h, 0)

                return {(0, 1): start, (0, 3): level(1), (0, 5): level(2), (0, 7): lambda: att_vt(h, 0),
                        (1, 1): level(3), (1, 3): level(4), (1, 5): level(5), (1, 7): lambda: att_vt(h, 1),
                        (2, 1): level(6), (2, 3): lambda: att_kt(h), (2, 5): lambda: att_kv(h),
                        (2, 7): lambda: att_out(h, 0), (3, 1): lambda: att_out(h, 1),
                        (3, 3): lambda: att_stats(h), (3, 6): lambda: att_spread(h)}

            def hg_head(h, pieces, first=False):
                for k in range(4):
                    s = step_of(HG_IN, 4, h, k)
                    gaps = {at: piece for (step_at, at), piece in pieces.items() if step_at == k}
                    if first and k == 0:
                        gaps = norm_gaps(3, seen(HG_IN, 1))
                    step(s, B, ready=3 * NT + NT * BLOCKS if first and k == 0 else None, gaps=gaps)
                    sums(s, 1, events(s.t), seen(s.t, 2)).then_inc(mm_done, 1)

            hg_head(0, {}, first=True)
            hg_head(1, attention(0, first=True))
            with pe.Fori(2, NT) as i:
                hg_head(i, attention(i - 1))

            after_hg = 4 * NT + NT * BLOCKS
            pieces = list(attention(NT - 1).values())
            out_steps = [step_of(HG_OUT, 4, 0, n) for n in range(2)]
            for n, s in enumerate(out_steps):
                step(s, B, ready=after_hg if n == 0 else None, tiles=range(NT - 1),
                     gaps={k: pieces.pop(0) for k in range(NT - 1)})
            while pieces:
                pieces.pop(0)()
            for s in out_steps:
                step(s, B, ready=after_hg, tiles=range(NT - 1, NT)).then_inc(mm_done, 1)
            for n in range(2, NT):
                step(step_of(HG_OUT, 4, 0, n), B).then_inc(mm_done, 1)

            mlp(1, MLP1, 0, A, B, after_hg + 2 * NT, first=True)
            with pe.Fori(1, BLOCKS) as b:
                mlp(1, MLP1, b, A, B, after_hg + 2 * NT)

            stats(5, ev_mlp1(BLOCKS, 0) + 2 + 3)
            for r in range(NC):
                if r >= 2:
                    pe.wait_ge(row_out[r % 2], r // 2)
                else:
                    pe.wait_ge(ps_free, END - 1 + r)
                if r == 0:
                    pe.wait_ge(gained, NT)
                for n in range(NT):
                    last = pe.transpose(acc[r % 2][:, n * P:(n + 1) * P],
                                        at2[:, n, r * P:(r + 1) * P], ident[:, :])
                last.then_inc(out_mm, 1)

        @block.scalar
        def _(act):
            def split_hi(s, fresh=False):
                act.wait_ge(w_loaded[s.odd], s.half * 16 + 16)
                if not fresh:
                    act.wait_ge(mm_done, s.t - 1)
                act.activation(w_hi[:, s.odd, :, :], stage[:, s.odd, :, :], ACT.Copy).then_inc(hi_ready, 1)

            def tile(buf, n):
                return buf[:, bass.ds(n, 1), :].rearrange("p a t -> p (a t)")

            def root(norm):
                act.wait_ge(ms_ready, norm)
                act.activation(nst[:, 1, :], nst[:, 0, :], ACT.Sqrt).then_inc(root_ready, 1)

            vr1, vr2 = rstd[:, 0:P], rstd[0:V2, P:2 * P]

            def rows(dst, src):
                act.dma_start(dst, src).then_inc(vec_loaded, 16)

            mb = mod_b.rearrange("l (n p) -> l n p", p=P)
            for name, at in MOD0.items():
                rows(vr1[at:at + 8, :], mb[0, 8 * PART[name]:8 * PART[name] + 8, :])
            rows(vr1[48:96, :], mb[1])
            rows(vr1[96:112, :], norm_mix.rearrange("l (n p) -> (l n) p", p=P))
            rows(vr1[112:128, :], norm_mlp.rearrange("l (n p) -> (l n) p", p=P))
            for at, n, src in ((C_C, 8, c.rearrange("a (n p) -> (a n) p", p=P)),
                               (C_NF, 8, norm_final.rearrange("(n p) -> n p", p=P)),
                               (C_CW, 32, rg_conv_w.rearrange("a w (n p) -> (a w n) p", p=P)),
                               (C_CB, 8, rg_conv_b.rearrange("a (n p) -> (a n) p", p=P)),
                               (C_BA, 8, rg_b_a.rearrange("a (n p) -> (a n) p", p=P)),
                               (C_BX, 8, rg_b_x.rearrange("a (n p) -> (a n) p", p=P)),
                               (C_LAM, 8, rg_lambda.rearrange("a (n p) -> (a n) p", p=P)),
                               (C_LB, 16, hg_lower_bounds.rearrange("l (n p) -> (l n) p", p=P)),
                               (C_GN, 1, hg_gnorm)):
                rows(vr2[at:at + n, :], src)
            act.wait_ge(vec_c, 2)
            act.activation(cs[:, :], vec2[:, C_C:C_C + 8], ACT.Silu).then_inc(small_a, 1)
            act.wait_ge(small_d, 1)
            act.activation(sm[:, 1, :], sm[:, 0, :], ACT.Exp, scale=-1.0)
            act.activation(sm[:, 3:5, :], sm[:, 3:5, :], ACT.Exp).then_inc(small_a, 1)
            for r in range(NC):
                act.wait_ge(x_loaded[r], 16)
                act.activation(tmp[:, :], xin[:, r, :], ACT.Square, accum_out=nst[:, 1, r:r + 1]
                               ).then_inc(x_squared, 1)
                act.drain()
            split_hi(step_of(0, 2, 0, 0), fresh=True)
            act.wait_ge(xt_cp, NC)
            act.wait_ge(small_d, 2)
            for n in range(NT):
                act.activation(a_hi[:, n, :], res[:, n, :], ACT.Identity, scale=amp[:, 0, n:n + 1]
                               ).then_inc(in_hi, 1)
                if n == 1:
                    root(1)
            split_hi(step_of(0, 2, 0, 1), fresh=True)

            def vcol(at, h):
                return vec2[:, bass.ds(at + h, 1)]

            def gate_split(h, first=False):
                act.wait_ge(g_loaded, h * 32 + 32)
                if not first:
                    act.wait_ge(gate_mm, h * 4)
                act.activation(gw_hi[:, :, :], gst[:, :, :], ACT.Copy).then_inc(gw_hi_r, 1)

            def rg_even(h, first=False):
                act.wait_ge(scaled, h * 2 + 1)
                if first:
                    act.wait_ge(spilled0, 16)
                    act.wait_ge(in_lo, NT)
                    act.wait_ge(small_d, 4)
                else:
                    act.wait_ge(xc_done, h)
                act.activation(xbp[:, TAPS - 1:], acc[0][:, :], ACT.Identity, bias=bcol[:, 0:1]
                               ).then_inc(ps_free, 1)
                act.drain()
                if not first:
                    act.wait_ge(ix_done, h)
                act.activation(xc, xbp[:, 0:T], ACT.Identity, scale=vcol(C_CW, h), bias=vcol(C_CB, h)
                               ).then_inc(xc0, 1)

            def rg_even_split(h, first=False):
                act.wait_ge(xc_done, h + 1)
                if not first:
                    act.wait_ge(gate_mm, h * 4)
                act.activation(xc_hi[:, :], xc, ACT.Copy).then_inc(xc_hi_r, 1)

            def rg_odd(h, first=False):
                act.wait_ge(scaled, h * 2 + 2)
                if not first:
                    act.wait_ge(og_done, h)
                act.activation(yb[:, :], acc[1][:, :], ACT.Identity, bias=bcol[:, 1:2]).then_inc(ps_free, 1)
                act.drain()
                act.activation(ytmp[:, :], yb[:, :], ACT.Square)
                act.drain()
                act.activation(ytmp[:, :], ytmp[:, :], ACT.Identity, scale=0.044715, bias=1.0
                               ).then_inc(y_poly, 1)

            def rg_gates(h):
                for g in range(2):
                    act.activation(gbias[:, g:g + 1], vcol((C_BA, C_BX)[g], h), ACT.Copy)
                act.drain()
                act.wait_ge(y_arg, h + 1)
                act.activation(ysig[:, :], ytmp[:, :], ACT.Sigmoid, scale=2 * 0.7978845608028654
                               ).then_inc(y_sig, 1)
                for q in range(4):
                    g, n = q % 2, q // 2
                    act.wait_ge(gate_mm, h * 4 + q + 1)
                    act.activation((r_g, i_g)[g][:, n * HALF:(n + 1) * HALF], bank[q % 3][:, :], ACT.Sigmoid,
                                   bias=gbias[:, g:g + 1]).then_inc(gate_rd, 1)
                act.drain()
                act.activation(th, r_g, ACT.Tanh, scale=decay[:, 0, bass.ds(h, 1)])
                act.activation(a_g, r_g, ACT.Exp, scale=decay[:, 1, bass.ds(h, 1)])
                act.drain()
                act.activation(m_g, a_g, ACT.Square).then_inc(ga_done, 1)

            def rg_factor(h):
                act.wait_ge(gp_done, h + 1)
                act.activation(m_g, m_g, ACT.Sqrt).then_inc(gm_done, 1)

            split_hi(step_of(RG_IN, 2, 0, 2))
            gate_split(0, first=True)
            rg_even(0, first=True)
            rg_even_split(0, first=True)
            split_hi(step_of(RG_IN, 2, 0, 3))
            rg_odd(0, first=True)
            act.wait_ge(spilled, SPILLED0)
            with act.Fori(1, NT) as j:
                rg_gates(j - 1)
                split_hi(step_of(RG_IN, 2, j, 2))
                rg_even(j)
                gate_split(j)
                rg_factor(j - 1)
                rg_even_split(j)
                split_hi(step_of(RG_IN, 2, j, 3))
                rg_odd(j)

            A, B = (a_hi, a_lo), (b_hi, b_lo)

            def rg_split(heads):
                for n in heads:
                    act.activation(a_hi[:, n, :], o_rg[:, n, :], ACT.Copy).then_inc(in_hi, 1)

            act.wait_ge(og_done, NT - 1)
            act.wait_ge(mm_done, RG_OUT)
            rg_split(range(NT // 2))
            rg_gates(NT - 1)
            rg_split(range(NT // 2, NT - 1))
            rg_factor(NT - 1)
            act.wait_ge(og_done, NT)
            rg_split(range(NT - 1, NT))

            def new_input(dst, k, n, x_before):
                act.wait_ge(x_new, x_before + n + 1)
                act.wait_ge(sq_added, n + (9 * k - 8))
                act.wait_ge(small_d, 4 + k)
                act.activation(tile(dst, n), tile(res, n), ACT.Identity, scale=amp[:, k, bass.ds(n, 1)]
                               ).then_inc(in_hi, 1)
                act.activation(tmp[:, :], tile(res, n), ACT.Square).then_inc(sq_part, 1)

            with act.Fori(0, 4) as m:
                for k in range(2):
                    split_hi(step_of(RG_OUT, 2, m, k + 2))
                    new_input(b_hi, 1, m * 2 + k, 0)

            def mlp(layer, base, b, hid, scaled_before, last=False, first=False):
                def one(q, k):
                    n = q * 4 + k
                    s = Step(base + b * (2 * NT) + n, None, k % 2)
                    act.wait_ge(scaled, scaled_before + b * NT + n + 1)
                    act.activation(acc[k % 2][:, :], acc[k % 2][:, :], ACT.Relu, bias=bcol[:, k % 2:k % 2 + 1])
                    act.drain()
                    act.activation(acc[k % 2][:, :], acc[k % 2][:, :], ACT.Square)
                    act.drain()
                    act.activation(tile(hid[0], n), acc[k % 2][:, :], ACT.Copy).then_inc(in_hi, 1)

                def ahead(q, k, off):
                    st = step_of(base + off, 2 * NT, b, k + 2)
                    split_hi(Step(st.t + q * 4, st.half + q * 2, st.odd))

                if first:
                    root(2 + 2 * layer)
                with act.Fori(0, 2) as q:
                    for k in range(4):
                        one(q, k)
                        ahead(q, k, 0)
                for q in range(2) if last and layer == 1 else [None]:
                    if q is None:
                        with act.Fori(0, 2) as q:
                            for k in range(4):
                                ahead(q, k, NT)
                                if last:
                                    new_input(last[0], last[1], q * 4 + k, last[2])
                    else:
                        for k in range(4):
                            n = q * 4 + k
                            if n < NT - 2:
                                ahead(q, k, NT)
                            act.wait_ge(x_new, 2 * (NT + NT * BLOCKS) - NT + n + 1)
                            act.wait_ge(sq_added, n + (9 * 4 - 8))
                            act.activation(tmp[:, :], res[:, n, :], ACT.Square).then_inc(sq_part, 1)
                            act.activation(at2[:, n, :], res[:, n, :], ACT.Identity,
                                           scale=vec2[:, C_NF + n:C_NF + n + 1]).then_inc(gained, 1)

            mlp(0, MLP0, 0, A, 2 * NT, first=True)
            with act.Fori(1, BLOCKS - 1) as b:
                mlp(0, MLP0, b, A, 2 * NT)
            mlp(0, MLP0, BLOCKS - 1, A, 2 * NT, last=(b_hi, 2, NT * BLOCKS))
            root(3)

            def hg_evict(h, k):
                act.wait_ge(scaled, h * 4 + (2 * NT + NT * BLOCKS) + k + 1)
                b = bcol[:, k % 2:k % 2 + 1]
                if k == 1:
                    act.activation(L_s, acc[1][:, :], ACT.Sigmoid, bias=b).then_inc(ps_free, 1)
                elif k == 2:
                    act.activation(L_v, acc[0][:, :], ACT.Identity, bias=b).then_inc(ps_free, 1)
                else:
                    act.activation(t_s, acc[k % 2][:, :], ACT.Sigmoid, bias=b).then_inc(sg_done, 1)

            def hg_vt(h, n):
                act.wait_ge(vt_mm, h * 2 + n + 1)
                act.activation(v_t[:, n * HALF:(n + 1) * HALF], bank[0][:, :], ACT.Copy).then_inc(vt_cp, 1)

            def hg_kt(h):
                for n in range(2):
                    act.wait_ge(kt_mm, h * 2 + n + 1)
                    act.activation(k_t[:, n * HALF:(n + 1) * HALF], bank[2 if n == 0 else 0][:, :], ACT.Copy
                                   ).then_inc(kt_cp, 1)

            def hg_o(h, n):
                cut = slice(n * HALF, (n + 1) * HALF)
                act.wait_ge(o_mm, h * 2 + n + 1)
                act.activation(o_sb[:, cut], bank[n][:, :], ACT.Copy)
                act.activation(o_sq[:, cut], bank[n][:, :], ACT.Square).then_inc(o_cp, 1)

            def hg_root(h):
                act.wait_ge(hms, h + 1)
                act.activation(nst[:, 1, :], nst[:, 0, :], ACT.Sqrt).then_inc(hroot, 1)

            def hg_step(i, k):
                split_hi(step_of(HG_IN, 4, i, k + 2))
                hg_evict(i, k)

            act.wait_ge(spilled, SPILLED1)
            act.wait_ge(in_lo, 3 * NT + NT * BLOCKS + NT)
            for k in range(4):
                hg_step(0, k)
            with act.Fori(1, NT) as i:
                hg_vt(i - 1, 0)
                hg_step(i, 0)
                hg_vt(i - 1, 1)
                hg_step(i, 1)
                hg_kt(i - 1)
                hg_o(i - 1, 0)
                hg_step(i, 2)
                hg_o(i - 1, 1)
                hg_root(i - 1)
                hg_step(i, 3)

            def head_split(n):
                act.activation(b_hi[:, n, :], o_hg[:, n, :], ACT.Copy).then_inc(in_hi, 1)

            act.wait_ge(on_done, NT - 1)
            act.wait_ge(mm_done, HG_OUT)
            for n in range(NT - 1):
                head_split(n)
            for n in range(2):
                hg_vt(NT - 1, n)
            hg_kt(NT - 1)
            for n in range(2):
                hg_o(NT - 1, n)
            hg_root(NT - 1)
            act.wait_ge(on_done, NT)
            head_split(NT - 1)
            with act.Fori(0, 2) as m:
                for k in range(4):
                    split_hi(step_of(HG_OUT, 4, m, k + 2))
                    new_input(a_hi, 3, m * 4 + k, NT + NT * BLOCKS)

            before = 2 * NT + NT * BLOCKS + 4 * NT
            mlp(1, MLP1, 0, B, before, first=True)
            with act.Fori(1, BLOCKS - 1) as b:
                mlp(1, MLP1, b, B, before)
            mlp(1, MLP1, BLOCKS - 1, B, before, last=True)
            root(5)
            act.wait_ge(last_rms, 1)
            for r in range(0, NC, 2):
                act.wait_ge(out_mm, r + 1)
                act.activation(o_hg[:, r, :], acc[0][:, :], ACT.Copy, scale=nst[:, 2, r:r + 1]
                               ).then_inc(row_out[0], 1)

        @block.vector
        def _(dve):
            tt, ts, stt = dve.tensor_tensor, dve.tensor_scalar, dve.scalar_tensor_tensor

            def tile(buf, n):
                return buf[:, bass.ds(n, 1), :].rearrange("p a t -> p (a t)")

            def split_lo(s):
                dve.wait_ge(hi_ready, s.t + 1)
                tt(w_lo[:, s.odd, :, :], stage[:, s.odd, :, :], w_hi[:, s.odd, :, :].bitcast(f32),
                   ALU.subtract).then_inc(lo_ready, 1)

            def ops(*todo):
                for op in todo:
                    op()
                    dve.drain()

            def x_copy(chunks):
                for r in chunks:
                    dve.wait_ge(xt_mm, r + 1)
                    dve.tensor_copy(res[:, :, r * P:(r + 1) * P],
                                    acc[r % 2].rearrange("p (n t) -> p n t", t=P)).then_inc(xt_cp, 1)

            x_copy(range(NC // 2 + 1))
            dve.wait_ge(vec_t, 2)
            dve.tensor_copy(vec1[:, :], bank[0][:, 0:P]).then_inc(vec_c, 1)
            dve.tensor_copy(vec2[:, :], bank[1][:, 0:V2]).then_inc(vec_c, 1)
            dve.drain()
            lam = vec2[:, C_LAM:C_LAM + 8]
            lb0, lb1 = vec2[:, C_LB:C_LB + 8], vec2[:, C_LB + 8:C_LB + 16]
            ops(lambda: ts(sm[:, 0, :], lam, -1.0, None, ALU.mult),
                lambda: ts(sm[:, 2, :], sm[:, 0, :], 0.0, None, ALU.max),
                lambda: tt(sm[:, 0, :], sm[:, 0, :], lam, ALU.max),
                lambda: tt(sm[:, 5, :], lb0, lb1, ALU.max),
                lambda: tt(sm[:, 3, :], lb0, sm[:, 5, :], ALU.subtract))
            tt(sm[:, 4, :], lb1, sm[:, 5, :], ALU.subtract).then_inc(small_d, 1)
            x_copy(range(NC // 2 + 1, NC))

            def weigh(weights, loaded, total):
                for k in range(NT):
                    dve.wait_ge(loaded[k], 16)
                    if k == 0:
                        last = ts(total[:, :], weights[:, 0, :], cs[:, 0:1], None, ALU.mult)
                    else:
                        last = stt(total[:, :], weights[:, k, :], cs[:, k:k + 1], total[:, :],
                                   ALU.mult, ALU.add)
                    dve.drain()
                dve.drain().then_inc(wsum_done, 1)

            dve.wait_ge(small_a, 1)
            weigh(w_scale, scale_loaded, scale_sum)

            def make_amp(k, table, name, gain):
                dve.drain()
                last = stt(amp[:, k, :], mod[:, table[name]:table[name] + NT], 1.0,
                           vec1[:, gain:gain + NT], ALU.add, ALU.mult)
                return last

            dve.wait_ge(vec_t, 3)
            at = MOD0["sc_t"]
            tt(mod[:, at:at + NT], cols[:, 0:NT], vec1[:, at:at + NT], ALU.add).then_inc(cols_read, 1)
            make_amp(0, MOD0, "sc_t", 96).then_inc(small_d, 1)

            def in_lo_res(dst, k, n, hi_before):
                dve.wait_ge(in_hi, hi_before + n + 1)
                stt(tile(dst[1], n), tile(res, n), amp[:, k, bass.ds(n, 1)],
                    tile(dst[0], n).bitcast(f32), ALU.mult, ALU.subtract).then_inc(in_lo, 1)

            A, B = (a_hi, a_lo), (b_hi, b_lo)
            dve.drain()

            def rms(src, n_mean, eps, after, ready, before, buf=None):
                ts(nst[:, 0, :], src, 1.0 / n_mean, eps, ALU.mult, ALU.add).then_inc(ready, 1)
                dve.wait_ge(after, before)
                ops(lambda: dve.reciprocal(nst[:, 2, :], nst[:, 1, :]),
                    lambda: tt(nst[:, 3, :], nst[:, 2, :], nst[:, 2, :], ALU.mult),
                    lambda: tt(nst[:, 3, :], nst[:, 3, :], nst[:, 0, :], ALU.mult),
                    lambda: ts(nst[:, 3, :], nst[:, 3, :], -0.5, 1.5, ALU.mult, ALU.add),
                    lambda: tt(nst[:, 2, :], nst[:, 2, :], nst[:, 3, :], ALU.mult))
                if buf is None:
                    return dve.drain()
                return tt(buf.rearrange("p (g t) -> p g t", t=P),
                          ident[:, :].unsqueeze(1).broadcast_to([P, NC, P]),
                          nst[:, 2, :].unsqueeze(2).broadcast_to([P, NC, P]), ALU.mult)

            def to_rstd(n):
                dve.wait_ge(bc_mm, n)
                for q in range(2):
                    last = dve.tensor_copy(rstd[:, q * HALF:(q + 1) * HALF], bank[q][:, :])
                last.then_inc(rstd_ready, 1)
                dve.drain()

            def norm(n):
                dve.wait_ge(stat_mm, n - 1)
                rms(cols[:, 0:NC], D, EPS, root_ready, ms_ready, n, tmp[:, :]).then_inc(diag_ready, 1)
                dve.drain().then_inc(cols_read, 1)
                to_rstd(n)

            def clear_squares():
                dve.memset(rstd[:, :], 0.0)
                dve.drain().then_inc(sq_added, 1)

            def add_square(k, n):
                dve.wait_ge(sq_part, n + (NT * k + 1))
                tt(rstd[:, :], rstd[:, :], tmp[:, :], ALU.add)
                dve.drain().then_inc(sq_added, 1)

            def scale_sums(s, mods=0, at=None):
                dve.wait_ge(mm_done, s.t + 1)
                last = dve.tensor_copy(bcol[:, s.odd:s.odd + 1], cols[:, 0:1])
                if mods:
                    last = tt(mod[:, bass.ds(at, mods)], cols[:, 1:1 + mods], vec1[:, bass.ds(at, mods)], ALU.add)
                last.then_inc(cols_read, 1)
                return tt(acc[s.odd][:, :], acc[s.odd][:, :], rstd[:, :], ALU.mult).then_inc(scaled, 1)

            split_lo(step_of(0, 2, 0, 0))
            for n in range(2):
                in_lo_res(A, 0, n, 0)
            dve.wait_ge(x_squared, NC)
            rms(nst[:, 1, :], D, EPS, root_ready, ms_ready, 1, tmp[:, :]).then_inc(diag_ready, 1)
            for n in range(2, NT):
                in_lo_res(A, 0, n, 0)
            to_rstd(1)
            split_lo(step_of(0, 2, 0, 1))
            weigh(w_shift, shift_loaded, shift_sum)
            dve.wait_ge(vec_t, 4)
            tt(mod[:, 0:NT], cols[:, 0:NT], vec1[:, 0:NT], ALU.add).then_inc(cols_read, 1)
            dve.drain().then_inc(small_d, 1)
            dve.memset(xbp[:, 0:TAPS - 1], 0.0).then_inc(small_d, 1)

            dve.wait_ge(small_a, 2)
            ops(lambda: tt(sm[:, 5, :], sm[:, 3, :], sm[:, 4, :], ALU.add),
                lambda: dve.reciprocal(sm[:, 5, :], sm[:, 5, :]),
                lambda: tt(sm[:, 3, :], sm[:, 3, :], sm[:, 5, :], ALU.mult),
                lambda: tt(sm[:, 4, :], sm[:, 4, :], sm[:, 5, :], ALU.mult),
                lambda: tt(sm[:, 4, :], sm[:, 3, :], sm[:, 4, :], ALU.add),
                lambda: tt(lbs[:, 0, :], sm[:, 4, :], sm[:, 3, :], ALU.subtract),
                lambda: ts(lbs[:, 1, :], lbs[:, 0, :], -1.0, 1.0, ALU.mult, ALU.add),
                lambda: ts(lbs[:, 2, :], lbs[:, 1, :], -1.0, None, ALU.mult))
            w, z, z2, p = sm[:, 1, :], sm[:, 3, :], sm[:, 4, :], sm[:, 5, :]
            ops(lambda: ts(z, w, 2.0, None, ALU.add),
                lambda: dve.reciprocal(z, z),
                lambda: tt(z, z, w, ALU.mult),
                lambda: tt(z2, z, z, ALU.mult),
                lambda: ts(p, z2, 2.0 / 17, 2.0 / 15, ALU.mult, ALU.add),
                *(lambda n=n, m=m: (tt(p, p, z2, ALU.mult) if m else ts(p, p, 2.0 / n, None, ALU.add))
                  for n in range(13, 0, -2) for m in (1, 0)),
                lambda: tt(p, p, z, ALU.mult),
                lambda: tt(p, p, sm[:, 2, :], ALU.add),
                lambda: ts(decay[:, 0, :], p, 8.0, None, ALU.mult),
                lambda: ts(decay[:, 1, :], p, -8.0, None, ALU.mult))

            def gate_split(h):
                dve.wait_ge(gw_hi_r, h + 1)
                tt(gw_lo[:, :, :], gst[:, :, :], gw_hi[:, :, :].bitcast(f32), ALU.subtract
                   ).then_inc(gw_lo_r, 1)

            def rg_conv(h):
                dve.wait_ge(xc0, h + 1)
                for k in range(1, TAPS):
                    stt(xc, xbp[:, k:k + T], vec2[:, bass.ds(C_CW + NT * k + h, 1)], xc,
                               ALU.mult, ALU.add)
                    last = dve.drain()
                last.then_inc(xc_done, 1)
                dve.wait_ge(xc_hi_r, h + 1)
                tt(xc_lo[:, :], xc, xc_hi[:, :].bitcast(f32), ALU.subtract).then_inc(xc_lo_r, 1)

            def rg_y(h):
                dve.wait_ge(y_poly, h + 1)
                tt(ytmp[:, :], ytmp[:, :], yb[:, :], ALU.mult).then_inc(y_arg, 1)

            def rg_ix(h):
                dve.wait_ge(gate_rd, h * 4 + 4)
                tt(ix_g, i_g, xc, ALU.mult).then_inc(ix_done, 1)

            def rg_root_arg(h):
                dve.wait_ge(ga_done, h + 1)
                stt(m_g, m_g, 1.0, th, ALU.add, ALU.mult).then_inc(gp_done, 1)

            def rg_scan(h):
                dve.wait_ge(gm_done, h + 1)
                dve.memset(m_g[:, 0:1], 1.0)
                dve.drain()
                tt(m_g, m_g, ix_g, ALU.mult)
                dve.drain()
                dve.tensor_tensor_scan(h_g, a_g, m_g, 0.0, ALU.mult, ALU.add)
                dve.drain()
                dve.wait_ge(gy_done, h + 1)
                tt(tile(o_rg, h), h_g, yb[:, :], ALU.mult).then_inc(og_done, 1)

            def rg_head(j, last_head=None):
                if last_head is not None:
                    rg_ix(last_head)
                scale_sums(step_of(RG_IN, 2, j, 0), 1, j * 2 + 16)
                if last_head is not None:
                    rg_root_arg(last_head)
                split_lo(step_of(RG_IN, 2, j, 2))
                rg_conv(j)
                if last_head is not None:
                    rg_scan(last_head)
                gate_split(j)
                scale_sums(step_of(RG_IN, 2, j, 1), 1, j * 2 + 17)
                split_lo(step_of(RG_IN, 2, j, 3))
                rg_y(j)

            rg_head(0)
            with dve.Fori(1, NT) as j:
                rg_head(j, j - 1)

            def rg_split(heads):
                for n in heads:
                    dve.wait_ge(in_hi, NT + n + 1)
                    tt(a_lo[:, n, :], o_rg[:, n, :], a_hi[:, n, :].bitcast(f32), ALU.subtract).then_inc(in_lo, 1)

            rg_split(range(NT // 2))
            rg_ix(NT - 1)
            rg_split(range(NT // 2, NT - 1))
            rg_root_arg(NT - 1)
            rg_scan(NT - 1)
            rg_split(range(NT - 1, NT))
            make_amp(1, MOD0, "sc_c", 112).then_inc(small_d, 1)
            clear_squares()

            def renew(s, n, table, name):
                dve.wait_ge(mm_done, s.t + 1)
                return stt(tile(res, n), acc[s.odd][:, :], mod[:, bass.ds(table[name] + n, 1)], tile(res, n),
                           ALU.mult, ALU.add).then_inc(x_new, 1)

            def freed():
                dve.drain().then_inc(ps_free, 1)

            with dve.Fori(0, 4) as m:
                for k in range(2):
                    s, n = step_of(RG_OUT, 2, m, k), m * 2 + k
                    dve.wait_ge(reloaded[0], 16 * NT)
                    dve.wait_ge(mm_done, s.t + 1)
                    tt(mod[:, bass.ds(n * 2 + 32, 2)], cols[:, 0:2], vec1[:, bass.ds(n * 2 + 32, 2)], ALU.add
                       ).then_inc(cols_read, 1)
                    renew(s, n, MOD0, "g_t")
                    freed()
                    in_lo_res(B, 1, n, 2 * NT)
                    add_square(0, n)
                    split_lo(step_of(RG_OUT, 2, m, k + 2))

            def mlp(layer, base, b, hid, tiles, last=False, first=False):
                table = MOD0 if layer == 0 else MOD1

                def ahead(q, k, off):
                    split_lo(Step(base + off + b * (2 * NT) + q * 4 + k + 2, None, k % 2))

                if first:
                    norm(2 + 2 * layer)
                with dve.Fori(0, 2) as q:
                    for k in range(4):
                        s = Step(base + b * (2 * NT) + q * 4 + k, None, k % 2)
                        scale_sums(s)
                        dve.wait_ge(in_hi, tiles + b * NT + q * 4 + k + 1)
                        tt(tile(hid[1], q * 4 + k), acc[s.odd][:, :], tile(hid[0], q * 4 + k).bitcast(f32),
                           ALU.subtract).then_inc(in_lo, 1)
                        freed()
                        ahead(q, k, 0)

                def out_step(q, k):
                    s = Step(base + NT + b * (2 * NT) + q * 4 + k, None, k % 2)
                    if layer == 0:
                        mods, at = 2 - k % 2, b * 12 + q * 6 + (0, 2, 3, 5)[k] + 48
                        dve.wait_ge(mm_done, s.t + 1)
                        tt(mod[:, bass.ds(at, mods)], cols[:, 0:mods], vec1[:, bass.ds(at, mods)], ALU.add
                           ).then_inc(cols_read, 1)
                    renew(s, q * 4 + k, table, "g_c")
                    freed()
                    if last and layer == 0:
                        in_lo_res(B, 2, q * 4 + k, 3 * NT + NT * BLOCKS)
                    if last:
                        add_square(1 + 2 * layer, q * 4 + k)
                    if not (last and layer == 1 and q * 4 + k >= NT - 2):
                        ahead(q, k, NT)

                if last:
                    clear_squares()
                if last and layer == 0:
                    make_amp(2, MOD1, "sc_t", 104).then_inc(small_d, 1)
                    dve.drain()
                if last and layer == 1:
                    for q in range(2):
                        for k in range(4):
                            out_step(q, k)
                else:
                    with dve.Fori(0, 2) as q:
                        for k in range(4):
                            out_step(q, k)

            mlp(0, MLP0, 0, A, 3 * NT, first=True)
            with dve.Fori(1, BLOCKS - 1) as b:
                mlp(0, MLP0, b, A, 3 * NT)
            mlp(0, MLP0, BLOCKS - 1, A, 3 * NT, last=True)
            norm(3)

            def hg_evict(h, k):
                s = step_of(HG_IN, 4, h, k)
                scale_sums(s)
                split_lo(step_of(HG_IN, 4, h, k + 2))
                if k in (0, 3):
                    dve.wait_ge(sg_done, h * 2 + (1 if k == 0 else 2))
                    stt(L_q if k == 0 else L_g, acc[s.odd][:, :], bcol[:, s.odd:s.odd + 1], t_s,
                        ALU.add, ALU.mult).then_inc(ps_free, 1)

            def blocks(buf, size):
                return buf.rearrange("p (n two j) -> p n two j", two=2, j=size)

            tot_at = [0]
            for lv in range(LEVELS):
                tot_at.append(tot_at[-1] + (T >> (lv + 1)))

            def totals(lv):
                return f_w if lv == 0 else tot[:, tot_at[lv - 1]:tot_at[lv]]

            def hg_prep(h, first=False):
                if not first:
                    dve.wait_ge(o_mm, h * 2)
                dve.wait_ge(ps_free, h * 4 + (HG_IN + 2))
                lb = lambda n: lbs[:, n, bass.ds(h, 1)]
                ts(f_w, L_s, lb(1), lb(0), ALU.mult, ALU.add)
                ts(k_w, L_s, lb(2), lb(1), ALU.mult, ALU.add)
                dve.drain()
                tt(q_w, L_q, f_w, ALU.mult).then_inc(prep, 1)

            def hg_diag(h):
                for n in range(2):
                    dve.wait_ge(dg_mm, h * 2 + n + 1)
                    tt(att[:, n * HALF:(n + 1) * HALF].rearrange("p (g t) -> p g t", t=P),
                       bank[2 if n == 0 else 0][:, :].rearrange("p (g t) -> p g t", t=P),
                       ident[:, :].unsqueeze(1).broadcast_to([P, 4, P]), ALU.mult).then_inc(dg_rd, 1)

            def hg_reach(h, lv):
                size = 1 << lv
                dve.wait_ge(lv_mm, h * LEVELS + lv + 1)
                q4, k4 = blocks(q_w, size), blocks(k_w, size)
                t2 = totals(lv).rearrange("p (n two) -> p n two", two=2)
                shape = [P, T // 2 // size, size]
                tt(q4[:, :, 1, :], q4[:, :, 1, :], t2[:, :, 0:1].broadcast_to(shape), ALU.mult)
                tt(totals(lv + 1), t2[:, :, 0], t2[:, :, 1], ALU.mult)
                tt(k4[:, :, 0, :], k4[:, :, 0, :], t2[:, :, 1:2].broadcast_to(shape), ALU.mult
                   ).then_inc(lv_up, 1)
                dve.drain()

            def hg_take(h, lv):
                size = 1 << lv
                a5 = att.rearrange("p (g n two j) -> p g n two j", g=NC, two=2, j=size)[:, :, :, 1, :]
                m5 = mask[:, lv, :].rearrange("p (n j) -> p n j", j=size).bitcast(u32)
                dve.copy_predicated(
                    a5, m5.unsqueeze(1).broadcast_to([P, NC, P // 2 // size, size]),
                    bank[1 + lv % 2][:, :].rearrange("p (g n j) -> p g n j", g=NC, j=size)).then_inc(lv_rd, 1)

            def hg_levels(h, levels):
                for lv in levels:
                    hg_reach(h, lv)
                    if lv == 0:
                        hg_diag(h)
                        dve.drain()
                    hg_take(h, lv)

            def hg_states(h):
                for g in range(NC - 1):
                    if g % 4 == 0:
                        dve.wait_ge(kv_mm, h * 2 + g // 4 + 1)
                    src = bank[1 + g // 4][:, (g % 4) * P:(g % 4 + 1) * P]
                    dst = s_st[:, (g + 1) * P:(g + 2) * P]
                    if g == 0:
                        last = dve.tensor_copy(dst, src)
                    else:
                        last = stt(dst, s_st[:, g * P:(g + 1) * P], totals(LEVELS)[:, g:g + 1], src,
                                   ALU.mult, ALU.add)
                    if g == 2 or g == NC - 2:
                        last.then_inc(st_done, 1)
                    dve.drain()

            def hg_norm(h):
                dve.wait_ge(hst_mm, h + 1)
                rms(bank[2][:, 0:NC], P, GEPS, hroot, hms, h + 1, att).then_inc(hdiag, 1)

            def hg_o(h):
                dve.wait_ge(hbc_mm, h + 1)
                for n in range(2):
                    cut = slice(n * HALF, (n + 1) * HALF)
                    tt(o_sb[:, cut], o_sb[:, cut], bank[n][:, :], ALU.mult)
                dve.drain()
                stt(tile(o_hg, h), o_sb, vec2[:, C_GN:C_GN + 1], L_g, ALU.mult, ALU.mult).then_inc(on_done, 1)

            for k in range(4):
                hg_evict(0, k)
            hg_prep(0, first=True)
            with dve.Fori(1, NT) as i:
                hg_levels(i - 1, range(0, 3))
                hg_evict(i, 0)
                hg_levels(i - 1, range(3, 6))
                hg_evict(i, 1)
                hg_levels(i - 1, range(6, LEVELS))
                hg_states(i - 1)
                hg_evict(i, 2)
                hg_prep(i)
                hg_norm(i - 1)
                hg_o(i - 1)
                hg_evict(i, 3)
            after = 4 * NT + NT * BLOCKS

            def head_split(n):
                dve.wait_ge(in_hi, after + n + 1)
                tt(b_lo[:, n, :], o_hg[:, n, :], b_hi[:, n, :].bitcast(f32), ALU.subtract).then_inc(in_lo, 1)

            h = NT - 1
            head_split(0)
            for lv in range(LEVELS):
                for n in {2: (3, 4), 5: ()}.get(lv, (lv + 1 if lv < 2 else lv + 2,)):
                    if n < NT - 1:
                        head_split(n)
                hg_levels(h, [lv])
            hg_states(h)
            hg_norm(h)
            hg_o(h)
            head_split(h)
            make_amp(3, MOD1, "sc_c", 120).then_inc(small_d, 1)
            clear_squares()
            with dve.Fori(0, 2) as m:
                for k in range(4):
                    s, n = step_of(HG_OUT, 4, m, k), m * 4 + k
                    dve.wait_ge(reloaded[1], 16 * NT)
                    renew(s, n, MOD1, "g_t")
                    freed()
                    in_lo_res(A, 3, n, after + NT)
                    add_square(2, n)
                    split_lo(step_of(HG_OUT, 4, m, k + 2))
            mlp(1, MLP1, 0, B, after + 2 * NT, first=True)
            with dve.Fori(1, BLOCKS - 1) as b:
                mlp(1, MLP1, b, B, after + 2 * NT)
            mlp(1, MLP1, BLOCKS - 1, B, after + 2 * NT, last=True)
            dve.wait_ge(stat_mm, 4)
            rms(cols[:, 0:NC], D, EPS, root_ready, ms_ready, 5).then_inc(last_rms, 1)
            for r in range(1, NC, 2):
                dve.wait_ge(out_mm, r + 1)
                ts(o_hg[:, r, :], acc[1][:, :], nst[:, 2, r:r + 1], None, ALU.mult).then_inc(row_out[1], 1)


_INS = ['x', 'c', 'mod_w', 'mod_b', 'norm_mix', 'norm_mlp', 'norm_final', 'rg_w_in', 'rg_conv_w',
        'rg_conv_b', 'rg_w_a', 'rg_b_a', 'rg_w_x', 'rg_b_x', 'rg_lambda', 'rg_w_out', 'hg_w_in',
        'hg_lower_bounds', 'hg_gnorm', 'hg_w_out', 'mlp_w1', 'mlp_w2']


def kernel(**inputs):
    import numpy as _np
    import concourse.bacc as _bacc
    from concourse import mybir as _mybir
    from concourse.bass_utils import run_bass_kernel_spmd as _run

    nc = _bacc.Bacc("TRN2", target_bir_lowering=False, num_devices=1)
    arrays, args = {}, []
    for name in _INS:
        a = _np.ascontiguousarray(inputs[name])
        arrays[f"in_{name}"] = a
        args.append(nc.dram_tensor(f"in_{name}", a.shape, _mybir.dt.from_np(a.dtype),
                                   kind="ExternalInput").ap())
    args.append(nc.dram_tensor("out_0", (1, T, D), _mybir.dt.float32, kind="ExternalOutput").ap())
    trunk(nc, *args)
    return _run(nc, [arrays], core_ids=[0]).results[0]["out_0"]
```

```python
from collections import namedtuple
from contextlib import ExitStack

import concourse.bass as bass
from concourse import mybir

P = 128
D = 1024
T = 1024
NT = D // P
NC = T // P
HALF = T // 2
DFF = 4 * D
BLOCKS = DFF // D
TAPS = 4
LEVELS = 7
POOL_K = 3
EPS, GEPS = 1e-6, 1e-5

RG_IN, RG_OUT = 0, 2 * NT
MLP0 = RG_OUT + NT
HG_IN = MLP0 + 2 * NT * BLOCKS
HG_OUT = HG_IN + 4 * NT
MLP1 = HG_OUT + NT
END = MLP1 + 2 * NT * BLOCKS

MOD0 = {"sh_t": 0, "sc_t": 8, "g_t": 16, "sc_c": 24, "sh_c": 32, "g_c": 40}
MOD1 = {"sh_t": 48, "sc_t": 56, "g_t": 64, "sh_c": 72, "sc_c": 80, "g_c": 88}
PART = {"sh_t": 0, "sc_t": 1, "g_t": 2, "sh_c": 3, "sc_c": 4, "g_c": 5}
C_C, C_NF, C_CW, C_CB, C_BA, C_BX, C_LAM, C_LB, C_GN = 0, 8, 16, 48, 56, 64, 72, 80, 96
V2 = 97

Step = namedtuple("Step", "t half odd")


def step_of(base, mult, r, c):
    return Step(base + mult * r + c, base // 2 + (mult // 2) * r + c // 2, c % 2)


def trunk(nc, x, c, mod_w, mod_b, norm_mix, norm_mlp, norm_final, rg_w_in, rg_conv_w, rg_conv_b,
          rg_w_a, rg_b_a, rg_w_x, rg_b_x, rg_lambda, rg_w_out, hg_w_in, hg_lower_bounds, hg_gnorm,
          hg_w_out, mlp_w1, mlp_w2, out):
    f32, f32r, u32 = mybir.dt.float32, mybir.dt.float32r, mybir.dt.uint32
    ALU = mybir.AluOpType
    ACT = mybir.ActivationFunctionType
    x_spill = nc.dram_tensor("x_spill", (2, NT, P, T), f32, kind="Internal").ap()

    ctx = ExitStack()
    with ctx:
        def sb(name, shape, dt=f32):
            at = nc.sbuf_base
            h = ctx.enter_context(nc.sbuf_tensor(name, shape, dt))
            return h, at

        def over(name, shape, at, dt=f32):
            return nc.alloc_sbuf_tensor_at(name, shape, dt, offset=at)

        def sem(name):
            return ctx.enter_context(nc.semaphore(name))

        res, _ = sb("res", [P, NT, T])
        a_hi, at_ahi = sb("a_hi", [P, NT, T], f32r)
        a_lo, at_alo = sb("a_lo", [P, NT, T], f32r)
        b_hi, at_bhi = sb("b_hi", [P, NT, T], f32r)
        b_lo, at_blo = sb("b_lo", [P, NT, T], f32r)
        w_hi, _ = sb("w_hi", [P, 2, NT, P], f32r)
        w_lo, _ = sb("w_lo", [P, 2, NT, P], f32r)
        stage, _ = sb("stage", [P, 2, NT, P])
        mstage, _ = sb("mstage", [P, 2, NT, P])
        rstd, _ = sb("rstd", [P, T])
        tmp, _ = sb("tmp", [P, T])
        pv, _ = sb("pv", [P, 2, 2, P])
        ident, _ = sb("ident", [P, P])
        mask, _ = sb("mask", [P, LEVELS, P // 2])
        vec1, _ = sb("vec1", [P, P])
        vec2, _ = sb("vec2", [P, V2])
        mod, _ = sb("mod", [P, 96])
        amp, _ = sb("amp", [P, 4, NT])
        cs, _ = sb("cs", [P, NT])
        decay, _ = sb("decay", [P, 2, NT])
        lbs, _ = sb("lbs", [P, 3, NT])
        sm, _ = sb("sm", [P, 6, NT])
        small, _ = sb("small", [P, 3, NT])
        bcol, _ = sb("bcol", [P, 2])
        gbias, _ = sb("gbias", [P, 2])
        nst, _ = sb("nst", [P, 4, NT])
        ones, _ = sb("ones", [P, P])

        xin = over("xin", [P, NT, D], at_blo)
        w_scale = over("w_scale", [P, NT, D], at_bhi)
        w_shift = over("w_shift", [P, NT, D], at_blo)
        scale_sum = over("scale_sum", [P, D], at_alo)
        o_rg = over("o_rg", [P, NT, T], at_blo)
        o_hg = over("o_hg", [P, NT, T], at_alo)
        free = [at_bhi]

        def rg_place(name, shape, dt=f32):
            h = over(name, shape, free[0], dt)
            words = shape[1] * (shape[2] if len(shape) > 2 else 1)
            free[0] += 4 * (-(-words // 8) * 8)
            return h

        xbp = rg_place("xbp", [P, T + TAPS - 1])
        gst = rg_place("gst", [P, 2, P])
        gw_hi, gw_lo = rg_place("gw_hi", [P, 2, P], f32r), rg_place("gw_lo", [P, 2, P], f32r)
        xc_hi, xc_lo = rg_place("xc_hi", [P, T], f32r), rg_place("xc_lo", [P, T], f32r)
        yb = rg_place("yb", [P, T])
        shift_sum = over("shift_sum", [P, D], free[0])
        ysig = rg_place("ysig", [P, T])
        ytmp = rg_place("ytmp", [P, T])
        rg_product = rg_place("rg_product", [P, NT, P])
        xc, r_g, i_g, th, a_g, m_g, ix_g, h_g = (res[:, n, :] for n in range(8))
        at2 = over("at2", [P, NT, T], at_ahi)
        L_q, L_s, L_v, L_g, q_w, k_w, f_w, tot = (res[:, n, :] for n in range(8))
        v_t, k_t, att, s_st, o_sb, o_sq, t_s = (at2[:, n, :] for n in range(7))

        acc = [ctx.enter_context(nc.psum_tensor(f"acc{n}", [P, T], f32)) for n in range(2)]
        bank = [ctx.enter_context(nc.psum_tensor(f"bank{n}", [P, HALF], f32)) for n in range(3)]
        cols = ctx.enter_context(nc.psum_tensor("cols", [P, HALF], f32))

        vec_loaded = sem("vec_loaded")
        x_loaded = [sem(f"x_loaded{r}") for r in range(NC)]
        scale_loaded = [sem(f"scale_loaded{k}") for k in range(NT)]
        shift_loaded = [sem(f"shift_loaded{k}") for k in range(NT)]
        shift_part = sem("shift_part")
        x_squared = sem("x_squared")
        wsum_done = sem("wsum_done")
        w_loaded = [sem(f"w_loaded{n}") for n in range(2)]
        m_loaded = [sem(f"m_loaded{n}") for n in range(2)]
        g_loaded = sem("g_loaded")
        spilled, spilled0 = sem("spilled"), sem("spilled0")
        reloaded_head = [sem("reloaded_head0"), sem("reloaded_head1")]
        reloaded = [sem("reloaded0"), sem("reloaded1")]
        stored = sem("stored")
        consts = sem("consts")
        vec_t = sem("vec_t")
        vec_c = sem("vec_c")
        small_a = sem("small_a")
        small_d = sem("small_d")
        xt_mm, xt_cp = sem("xt_mm"), [sem("xt_cp0"), sem("xt_cp1")]
        gained, out_mm = sem("gained"), sem("out_mm")
        row_out = [sem("row_out0"), sem("row_out1")]
        last_rms = sem("last_rms")
        hi_ready, lo_ready = sem("hi_ready"), sem("lo_ready")
        in_hi, in_lo = sem("in_hi"), sem("in_lo")
        mm_done, ps_free = sem("mm_done"), sem("ps_free")
        scaled = sem("scaled")
        stage_summed = sem("stage_summed")
        sums_ready = sem("sums_ready")
        mod_used = sem("mod_used")
        cols_read = sem("cols_read")
        stat_mm, ms_ready, root_ready, diag_ready, bc_mm, rstd_ready = (
            sem(n) for n in ("stat_mm", "ms_ready", "root_ready", "diag_ready", "bc_mm", "rstd_ready"))
        x_new = sem("x_new")
        sq_part = sem("sq_part")
        sq_added = sem("sq_added")
        xc0, xc_done, gw_hi_r, gw_lo_r = (
            sem(n) for n in ("xc0", "xc_done", "gw_hi_r", "gw_lo_r"))
        xc_hi_r, xc_lo_r = sem("xc_hi_r"), sem("xc_lo_r")
        gate_mm, gate_rd = sem("gate_mm"), sem("gate_rd")
        y_poly, y_arg, y_sig, gy_done = (sem(n) for n in ("y_poly", "y_arg", "y_sig", "gy_done"))
        ga_done, gp_done, gm_done, ix_done, og_done = (
            sem(n) for n in ("ga_done", "gp_done", "gm_done", "ix_done", "og_done"))
        sg_done = sem("sg_done")
        vt_mm, vt_cp = sem("vt_mm"), sem("vt_cp")
        prep = sem("prep")
        dg_mm, dg_rd = sem("dg_mm"), sem("dg_rd")
        lv_mm, lv_rd, lv_up = sem("lv_mm"), sem("lv_rd"), sem("lv_up")
        kt_mm, kt_cp, kv_mm, st_done = sem("kt_mm"), sem("kt_cp"), sem("kv_mm"), sem("st_done")
        o_mm, o_cp = sem("o_mm"), sem("o_cp")
        hms, hroot, o_scaled, back_mm, on_done = (
            sem(n) for n in ("hms", "hroot", "o_scaled", "back_mm", "on_done"))

        def events(t):
            return t

        def ev_mlp1(b, n):
            return HG_OUT + NT * b + n

        def seen(t, norms):
            return t + 2 + norms

        def tiled(w):
            return w.rearrange("(k p) n -> p k n", p=P)

        HEAD = 2
        SPILLED0, SPILLED1 = 16 * (NT - 1), 16 * (2 * NT - 1)

        vr1, vr2 = rstd[:, 0:P], rstd[0:V2, P:2 * P]
        mb = mod_b.rearrange("l (n p) -> l n p", p=P)
        vectors = [(vr2[at:at + n, :], src) for at, n, src in (
            (C_C, 8, c.rearrange("a (n p) -> (a n) p", p=P)),
            (C_NF, 8, norm_final.rearrange("(n p) -> n p", p=P)),
            (C_CW, 32, rg_conv_w.rearrange("a w (n p) -> (a w n) p", p=P)),
            (C_CB, 8, rg_conv_b.rearrange("a (n p) -> (a n) p", p=P)),
            (C_BA, 8, rg_b_a.rearrange("a (n p) -> (a n) p", p=P)),
            (C_BX, 8, rg_b_x.rearrange("a (n p) -> (a n) p", p=P)),
            (C_LAM, 8, rg_lambda.rearrange("a (n p) -> (a n) p", p=P)),
            (C_LB, 16, hg_lower_bounds.rearrange("l (n p) -> (l n) p", p=P)),
            (C_GN, 1, hg_gnorm))]
        vectors += [(vr1[at:at + n, :], src) for at, n, src in (
            (0, 24, mb[0, 0:24, :]),
            (MOD0["sc_c"], 8, mb[0, 8 * PART["sc_c"]:8 * PART["sc_c"] + 8, :]),
            (MOD0["sh_c"], 8, mb[0, 8 * PART["sh_c"]:8 * PART["sh_c"] + 8, :]),
            (MOD0["g_c"], 56, mod_b.rearrange("l (n p) -> (l n) p", p=P)[40:96, :]),
            (96, 16, norm_mix.rearrange("l (n p) -> (l n) p", p=P)),
            (112, 16, norm_mlp.rearrange("l (n p) -> (l n) p", p=P)))]

        block = ctx.enter_context(nc.Block())

        @block.sync
        def _(sp):
            for r in range(NC):
                sp.dma_start(xin[:, r, :], x[0, r * P:(r + 1) * P, :]).then_inc(x_loaded[r], 16)
                for dst, src in vectors[:len(vectors) // 2][2 * r:2 * r + 2]:
                    sp.dma_start(dst, src).then_inc(vec_loaded, 16)

            def mod_part(layer, name):
                return tiled(mod_w[layer])[:, :, D * PART[name]:D * PART[name] + D]

            for k in range(NT):
                sp.dma_start(w_scale[:, k, :], mod_part(0, "sc_t")[:, k, :]).then_inc(scale_loaded[k], 16)

            def load_w(s, src, summed=None, split=None):
                if summed is not None:
                    sp.wait_ge(stage_summed, summed)
                if split is not None:
                    sp.wait_ge(lo_ready, split)
                sp.dma_start(stage[:, s.odd, :, :], src).then_inc(w_loaded[s.odd], 16)

            def load_mod(odd, src):
                sp.dma_start(mstage[:, odd, :, :], src).then_inc(m_loaded[odd], 16)

            rg_in = tiled(rg_w_in[0]).rearrange("p k (s n c) -> p k s n c", s=2, c=P)
            rg_out = tiled(rg_w_out[0])
            hg_in = tiled(hg_w_in[0]).rearrange("p k (s n c) -> p k s n c", s=4, c=P)
            hg_out = tiled(hg_w_out[0])

            load_w(step_of(0, 2, 0, 0), rg_in[:, :, 0, 0, :])
            load_w(step_of(0, 2, 0, 1), rg_in[:, :, 1, 0, :])
            g_t, sc_c = mod_part(0, "g_t"), mod_part(0, "sc_c")
            load_mod(0, g_t[:, :, 0:P])
            load_mod(1, g_t[:, :, P:2 * P])
            for n in range(2):
                sp.wait_ge(xt_cp[n], NC // 2)
            sp.dma_start(x_spill[0, 0], res[:, 0, :]).then_inc(spilled0, 16)
            sp.wait_ge(x_squared, NC)
            for k in range(NT):
                sp.dma_start(w_shift[:, k, :], mod_part(0, "sh_t")[:, k, :]).then_inc(shift_loaded[k], 16)
            for n in range(1, NT):
                sp.dma_start(x_spill[0, n], res[:, n, :]).then_inc(spilled, 16)

            def load_gate(h):
                sp.dma_start(gst[:, 0, :], rg_w_a[0, bass.ds(h, 1)].rearrange("a p n -> p (a n)")
                             ).then_inc(g_loaded, 16)
                sp.dma_start(gst[:, 1, :], rg_w_x[0, bass.ds(h, 1)].rearrange("a p n -> p (a n)")
                             ).then_inc(g_loaded, 16)

            sp.wait_ge(small_d, 2)
            load_gate(0)

            def rg_loads(j, part, at):
                for k in range(2):
                    s = step_of(RG_IN, 2, j, k)
                    load_w(s, rg_in[:, :, k, bass.ds(j, 1), :].rearrange("p k a c -> p k (a c)"), s.t - 1)
                    sp.wait_ge(mod_used, s.t - 1)
                    load_mod(k, part[:, :, bass.ds(at + k * P, P)])
                sp.wait_ge(gw_lo_r, j)
                load_gate(j)

            with sp.Fori(1, 4) as j:
                rg_loads(j, g_t, j * (2 * P))
            with sp.Fori(4, 8) as j:
                rg_loads(j, sc_c, j * (2 * P) - D)

            def rg_out_loads(m, part, at, first=False, ks=range(2)):
                for k in ks:
                    s = step_of(RG_OUT, 2, m, k)
                    load_w(s, rg_out[:, :, bass.ds(m * (2 * P) + k * P, P)],
                           summed=s.t - 1 if first else None, split=None if first else s.t - 1)
                    for q in range(2):
                        n = 2 * NT + m * 4 + 2 * k + q
                        sp.wait_ge(mod_used, n - 1)
                        load_mod(q, part[:, :, bass.ds(at + (2 * k + q) * P, P)])

            def reload(which, tiles):
                for n in tiles:
                    sp.dma_start(res[:, n, :], x_spill[which, n]).then_inc(
                        (reloaded_head if n < HEAD else reloaded)[which], 16)

            rg_out_loads(0, mod_part(0, "sh_c"), 0, first=True)
            sp.wait_ge(ga_done, NT)
            sp.wait_ge(ix_done, NT)
            reload(0, (0, 1, 2))
            sp.wait_ge(gp_done, NT)
            reload(0, (3,))
            rg_out_loads(1, mod_part(0, "sh_c"), 4 * P, ks=(0,))
            sp.wait_ge(og_done, NT)
            reload(0, range(4, NT))
            rg_out_loads(1, mod_part(0, "sh_c"), 4 * P, ks=(1,))
            with sp.Fori(2, 4) as m:
                rg_out_loads(m, mod_part(0, "g_c"), m * (4 * P) - D)

            mod1 = tiled(mod_w[1])

            def mlp_loads(layer, base, b):
                w1 = tiled(mlp_w1[layer])
                summed = 2 * NT if layer == 0 else 6 * NT + NT * BLOCKS
                w2 = mlp_w2[layer].rearrange("(b k p) n -> p b k n", p=P, k=NT)
                for n in range(NT):
                    s = step_of(base, 2 * NT, b, n)
                    src = w1[:, :, bass.ds(b * D + n * P, P)]
                    if n < 2:
                        load_w(s, src, split=s.t - 1)
                    else:
                        load_w(s, src, summed=summed + b * NT + n - 1)
                m = 0
                for n in range(NT):
                    s = step_of(base + NT, 2 * NT, b, n)
                    src = w2[:, bass.ds(b, 1), :, n * P:(n + 1) * P].rearrange("p a k n -> p (a k) n")
                    if n < 2:
                        load_w(s, src, summed=summed + b * NT + n + NT - 1)
                    else:
                        load_w(s, src, split=s.t - 1)
                    for _ in range(2 - n % 2 if layer == 0 else 0):
                        sp.wait_ge(mod_used, b * 12 + (m + 31))
                        load_mod(m % 2, mod1[:, :, bass.ds(b * (12 * P) + m * P, P)])
                        m += 1

            with sp.Fori(0, BLOCKS) as b:
                mlp_loads(0, MLP0, b)

            def hg_loads(h, ks=range(4), first=False):
                for k in ks:
                    s = step_of(HG_IN, 4, h, k)
                    src = hg_in[:, :, k, bass.ds(h, 1), :].rearrange("p k a c -> p k (a c)")
                    if first and k < 2:
                        load_w(s, src, split=s.t - 1)
                    else:
                        load_w(s, src, summed=h * 4 + (2 * NT + NT * BLOCKS + k - 1))

            hg_loads(0, (0, 1), first=True)
            for n in range(NT):
                sp.wait_ge(x_new, NT + NT * (BLOCKS - 1) + n + 1)
                sp.dma_start(x_spill[1, n], res[:, n, :]).then_inc(spilled, 16)
            hg_loads(0, (2, 3))
            with sp.Fori(1, NT) as h:
                hg_loads(h)
            sp.wait_ge(stage_summed, 6 * NT + NT * BLOCKS)
            for n in range(NT):
                s = step_of(HG_OUT, 2 * NT, 0, n)
                load_w(s, hg_out[:, :, n * P:(n + 1) * P], split=s.t - 1)
                if n == 2:
                    for done, count, at in ((dg_mm, 2, 0), (prep, 1, 1), (vt_mm, 2, 2), (lv_up, LEVELS, 6),
                                            (kt_mm, 2, 5), (st_done, 2, 7), (o_mm, 2, 4), (on_done, 1, 3)):
                        sp.wait_ge(done, count * NT)
                        reload(1, (at,))
            with sp.Fori(0, BLOCKS) as b:
                mlp_loads(1, MLP1, b)
            for r in range(NC):
                sp.wait_ge(row_out[r % 2], r // 2 + 1)
                sp.dma_start(out[0, r * P:(r + 1) * P, :], o_hg[:, r, :]).then_inc(stored, 16)
            sp.wait_ge(stored, 16 * NC)
            sp.wait_ge(spilled0, 16)
            sp.wait_ge(spilled, SPILLED1)

        @block.gpsimd
        def _(pool):
            pool.memset(ident[:, :], 0.0)
            pool.memset(ones[:, :], 1.0)
            pool.memset(mask[:, :, :], 1.0)
            pool.drain()
            pool.affine_select(out=ident[:, :], in_=ident[:, :], compare_op=ALU.not_equal, fill=1.0,
                               base=0, pattern=[[-1, P]], channel_multiplier=1)
            pool.drain().then_inc(consts, 1)
            for lv in range(LEVELS):
                h = 1 << lv
                m = mask[:, lv, :].rearrange("p (n j) -> p n j", j=h)
                pool.affine_select(out=m, in_=m, compare_op=ALU.is_ge, fill=0.0, base=0,
                                   pattern=[[-2 * h, P // 2 // h], [0, h]], channel_multiplier=1)
                pool.drain()
                pool.affine_select(out=m, in_=m, compare_op=ALU.is_ge, fill=0.0, base=h - 1,
                                   pattern=[[2 * h, P // 2 // h], [0, h]], channel_multiplier=-1)
            pool.drain().then_inc(consts, 1)

            def sums(buf, vector, slot, read, product=None):
                work = buf if product is None else product[:, :, :]
                first = pool.tensor_tensor(work, buf, vector.unsqueeze(2).broadcast_to([P, NT, P]), ALU.mult)
                pool.drain()
                for n in (4, 2):
                    pool.tensor_tensor(work[:, 0:n, :], work[:, 0:n, :], work[:, n:2 * n, :], ALU.add)
                    pool.drain()
                last = pool.tensor_tensor(slot, work[:, 0, :], work[:, 1, :], ALU.add)
                (last if product is None else first).then_inc(read, 1)
                pool.drain()

            def w_sums(s, shift, product=None):
                pool.wait_ge(lo_ready, s.t + 1)
                sums(stage[:, s.odd, :, :], shift, pv[:, s.odd, 0, :], stage_summed, product)

            def m_sums(odd, loads, s, slot, product=None):
                pool.wait_ge(m_loaded[odd], loads * 16)
                sums(mstage[:, odd, :, :], cs[:, :], pv[:, s.odd, slot, :], mod_used, product)

            def pv_free(s):
                pool.wait_ge(mm_done, s.t - 1)

            def mark():
                pool.drain().then_inc(sums_ready, 1)

            def shift_of(table, name):
                return mod[:, table[name]:table[name] + NT]

            pool.wait_ge(small_a, 1)
            for k in range(2):
                m_sums(k, 1, step_of(RG_IN, 2, 0, k), 1)
            for k in range(POOL_K):
                pool.wait_ge(shift_loaded[k], 16)
                pool.tensor_tensor(w_shift[:, k, :], w_shift[:, k, :],
                                   cs[:, k:k + 1].broadcast_to([P, D]), ALU.mult)
                pool.drain()
                if k:
                    pool.tensor_tensor(w_shift[:, 0, :], w_shift[:, 0, :], w_shift[:, k, :], ALU.add)
                    pool.drain()
            pool.drain().then_inc(shift_part, 1)

            def rg_sums(j, k):
                s = step_of(RG_IN, 2, j, k)
                pv_free(s)
                w_sums(s, shift_of(MOD0, "sh_t"), rg_product)
                if k:
                    rg_gy(j - 1)
                m_sums(k, j + 1, s, 1, rg_product)
                mark()

            def rg_gy(h):
                pool.wait_ge(y_sig, h + 1)
                pool.tensor_tensor(ysig[:, :], yb[:, :], ysig[:, :], ALU.mult).then_inc(gy_done, 1)

            pool.wait_ge(small_d, 3)
            for k in range(2):
                w_sums(step_of(RG_IN, 2, 0, k), shift_of(MOD0, "sh_t"), rg_product)
                mark()
            with pool.Fori(1, NT) as j:
                rg_sums(j, 0)
                rg_sums(j, 1)
            def rg_out_sums(m, ks=range(2)):
                for k in ks:
                    s = step_of(RG_OUT, 2, m, k)
                    pv_free(s)
                    for q in range(2):
                        m_sums(q, NT + m * 2 + k + 1, s, q)
                    mark()

            rg_out_sums(0, (0,))
            rg_gy(NT - 1)
            rg_out_sums(0, (1,))
            with pool.Fori(1, 4) as m:
                rg_out_sums(m)

            def mlp_sums(layer, base, b):
                table = MOD0 if layer == 0 else MOD1
                with pool.Fori(0, 2) as q:
                    for k in range(4):
                        s = Step(base + b * (2 * NT) + q * 4 + k, None, k % 2)
                        pv_free(s)
                        w_sums(s, shift_of(table, "sh_c"))
                        mark()
                if layer == 1:
                    return
                with pool.Fori(0, 2) as q:
                    n = 0
                    for k in range(4):
                        s = Step(base + NT + b * (2 * NT) + q * 4 + k, None, k % 2)
                        pv_free(s)
                        for slot in range(2 - k % 2):
                            m_sums(n % 2, b * 6 + q * 3 + (n // 2 + 1) + 2 * NT, s, slot)
                            n += 1
                        mark()

            with pool.Fori(0, BLOCKS) as b:
                mlp_sums(0, MLP0, b)
            with pool.Fori(0, NT) as h:
                for k in range(4):
                    s = step_of(HG_IN, 4, h, k)
                    pv_free(s)
                    w_sums(s, shift_of(MOD1, "sh_t"))
                    mark()
            for n in range(NT - 1):
                pool.wait_ge(in_hi, 4 * NT + NT * BLOCKS + n + 1)
                pool.tensor_tensor(b_lo[:, n, :], o_hg[:, n, :], b_hi[:, n, :].bitcast(f32), ALU.subtract
                                   ).then_inc(in_lo, 1)
            with pool.Fori(0, BLOCKS) as b:
                mlp_sums(1, MLP1, b)

        @block.tensor
        def _(pe):
            def mm(dst, lhs, rhs, start=True, stop=True):
                return pe.matmul(dst, lhs, rhs, start=start, stop=stop)

            pe.wait_ge(consts, 1)
            for r in range(NC):
                if r >= 2:
                    pe.wait_ge(xt_cp[r % 2], r // 2)
                pe.wait_ge(x_loaded[r], 16)
                for n in range(NT):
                    last = pe.transpose(acc[r % 2][:, n * P:(n + 1) * P], xin[:, r, n * P:(n + 1) * P],
                                        ident[:, :])
                last.then_inc(xt_mm, 1)
                if r == NC // 2:
                    pe.wait_ge(vec_loaded, 16 * len(vectors))
                    pe.transpose(bank[0][:, 0:P], rstd[:, 0:P], ident[:, :]).then_inc(vec_t, 1)
                    pe.transpose(bank[1][:, 0:V2], rstd[0:V2, P:2 * P], ident[0:V2, 0:V2]).then_inc(vec_t, 1)

            def over_partitions(sums_of, n_before):
                pe.wait_ge(wsum_done, n_before + 1)
                if n_before:
                    pe.wait_ge(cols_read, n_before)
                for n in range(NT):
                    last = mm(cols[:, n:n + 1], sums_of[:, n * P:(n + 1) * P], ones[:, 0:1])
                last.then_inc(vec_t, 1)

            over_partitions(scale_sum, 0)

            def step(s, src, ready=None, gaps=None, fresh=False, tiles=range(NT)):
                hi, lo = src
                if tiles[0] == 0:
                    pe.wait_ge(lo_ready, s.t + 1)
                    if not fresh:
                        pe.wait_ge(ps_free, s.t - 1)
                for k in tiles:
                    if ready is not None:
                        pe.wait_ge(in_lo, ready + k + 1)
                    for w, parts in ((w_hi, (hi, lo)), (w_lo, (hi,))):
                        for v in parts:
                            for n in range(2):
                                last = mm(acc[s.odd][:, n * HALF:(n + 1) * HALF], w[:, s.odd, k, :],
                                          v[:, k, n * HALF:(n + 1) * HALF],
                                          k == 0 and w is w_hi and v is hi,
                                          k == NT - 1 and w is w_lo)
                    if gaps and k in gaps:
                        gaps[k]()
                return last

            def sums(s, n, events_before, cols_before):
                pe.wait_ge(sums_ready, events_before + 1)
                pe.wait_ge(cols_read, cols_before)
                for i in range(n):
                    last = mm(cols[:, i:i + 1], pv[:, s.odd, i, :], ones[:, 0:1])
                return last

            def stats(norm, cols_before):
                pe.wait_ge(sq_added, 9 * (norm - 1))
                pe.wait_ge(cols_read, cols_before)
                for g in range(NC):
                    last = mm(cols[:, g:g + 1], rstd[:, g * P:(g + 1) * P], ones[:, 0:1])
                last.then_inc(stat_mm, 1)

            def spread(norm):
                pe.wait_ge(diag_ready, norm)
                for n in range(2):
                    last = mm(bank[n][:, :], ones[:, :], tmp[:, n * HALF:(n + 1) * HALF])
                last.then_inc(bc_mm, 1)

            def norm_gaps(norm, cols_before):
                return {5: lambda: stats(norm, cols_before), 7: lambda: spread(norm)}

            A, B = (a_hi, a_lo), (b_hi, b_lo)

            def gates(j, qs, first=False):
                if 0 in qs:
                    pe.wait_ge(gw_lo_r, j + 1)
                    pe.wait_ge(xc_lo_r, j + 1)
                    if first:
                        pe.wait_ge(rstd_ready, 1)
                    else:
                        pe.wait_ge(gate_rd, j * 4)
                for q in qs:
                    g, n = q % 2, q // 2
                    if q == 3:
                        pe.wait_ge(gate_rd, j * 4 + 1)
                    cut = slice(n * HALF, (n + 1) * HALF)
                    mm(bank[q % 3][:, :], gw_hi[:, g, :], xc_hi[:, cut], True, False)
                    mm(bank[q % 3][:, :], gw_hi[:, g, :], xc_lo[:, cut], False, False)
                    mm(bank[q % 3][:, :], gw_lo[:, g, :], xc_hi[:, cut], False, True).then_inc(gate_mm, 1)

            def gate_gaps(j):
                return {1: lambda: gates(j, range(3)), 6: lambda: gates(j, (3,))}

            def in_sums(s):
                sums(s, 2, events(s.t), seen(s.t, 0)).then_inc(mm_done, 1)

            s0, s1 = step_of(RG_IN, 2, 0, 0), step_of(RG_IN, 2, 0, 1)
            step(s0, A, ready=0, fresh=True, gaps={6: lambda: spread(1)})
            step(s1, A, fresh=True, gaps={3: lambda: over_partitions(shift_sum, 1)})
            in_sums(s0)
            for k in range(2):
                s = step_of(RG_IN, 2, 1, k)
                step(s, A, gaps={1: lambda: in_sums(s1), 3: lambda: gates(0, range(3), first=True),
                                 6: lambda: gates(0, (3,))} if k == 0 else None)
                in_sums(s)
            with pe.Fori(2, NT) as j:
                for k in range(2):
                    s = step_of(RG_IN, 2, j, k)
                    step(s, A, gaps=gate_gaps(j - 1) if k == 0 else None)
                    in_sums(s)
            gates(NT - 1, range(3))
            out_steps = [step_of(RG_OUT, 2, 0, n) for n in range(2)]
            for tiles in (range(4), range(4, NT - 1)):
                for n, s in enumerate(out_steps):
                    step(s, A, ready=NT if n == 0 else None, tiles=tiles,
                         gaps={1: lambda: gates(NT - 1, (3,))} if n == 0 else None)
            for s in out_steps:
                step(s, A, ready=NT, tiles=range(NT - 1, NT))
                in_sums(s)
            with pe.Fori(1, 4) as m:
                for k in range(2):
                    s = step_of(RG_OUT, 2, m, k)
                    step(s, A)
                    sums(s, 2, events(s.t), seen(s.t, 0)).then_inc(mm_done, 1)

            def mlp(layer, base, b, src, hid, tiles, first=False):
                norms = 1 if layer == 0 else None
                for q in range(2):
                    for k in range(4):
                        n = q * 4 + k
                        s = step_of(base, 2 * NT, b, n)
                        head = first and n == 0
                        step(s, src, ready=tiles - NT if head else None,
                             gaps=norm_gaps(2 + 2 * layer, seen(MLP0, 0) if layer == 0 else
                                            seen(HG_OUT, 2)) if head else None)
                        if layer == 0:
                            sums(s, 1, events(s.t), seen(s.t, norms)).then_inc(mm_done, 1)
                        else:
                            sums(s, 1, ev_mlp1(b, n), ev_mlp1(b, n) + 2 + 3).then_inc(mm_done, 1)
                for n in range(NT):
                    s = step_of(base + NT, 2 * NT, b, n)
                    last = step(s, hid, ready=tiles + b * NT if n == 0 else None)
                    if layer == 0:
                        last = sums(s, 2 - n % 2, events(s.t), seen(s.t, norms))
                    last.then_inc(mm_done, 1)

            mlp(0, MLP0, 0, B, A, 3 * NT, first=True)
            with pe.Fori(1, BLOCKS) as b:
                mlp(0, MLP0, b, B, A, 3 * NT)

            def att_diag(h, first=False):
                pe.wait_ge(prep, h + 1)
                if first:
                    pe.wait_ge(rstd_ready, 3)
                else:
                    pe.wait_ge(on_done, h)
                for n in range(2):
                    for g in range(4):
                        cut = slice((4 * n + g) * P, (4 * n + g + 1) * P)
                        last = mm(bank[2 if n == 0 else 0][:, g * P:(g + 1) * P], k_w[:, cut], L_q[:, cut])
                    last.then_inc(dg_mm, 1)

            def att_vt(h, n):
                if n == 0:
                    pe.wait_ge(ps_free, h * 4 + (HG_IN + 3))
                    pe.wait_ge(dg_rd, h * 2 + 2)
                else:
                    pe.wait_ge(vt_cp, h * 2 + 1)
                for g in range(4):
                    last = pe.transpose(bank[0][:, g * P:(g + 1) * P],
                                        L_v[:, (4 * n + g) * P:(4 * n + g + 1) * P], ident[:, :])
                last.then_inc(vt_mm, 1)

            def att_level(h, lv):
                size = 1 << lv
                if lv == 1:
                    pe.wait_ge(dg_rd, h * 2 + 1)
                if lv:
                    pe.wait_ge(lv_up, h * LEVELS + lv)
                if lv >= 2:
                    pe.wait_ge(lv_rd, h * LEVELS + lv - 1)
                q4 = q_w.rearrange("p (g n two j) -> p g n two j", g=NC, two=2, j=size)
                for g in range(NC):
                    last = mm(bank[1 + lv % 2][:, g * 64:(g + 1) * 64].rearrange("p (n j) -> p n j", j=size),
                              k_w[:, g * P:(g + 1) * P], q4[:, g, :, 1, :])
                last.then_inc(lv_mm, 1)

            def att_kt(h):
                pe.wait_ge(lv_up, h * LEVELS + LEVELS)
                pe.wait_ge(vt_cp, h * 2 + 2)
                pe.wait_ge(lv_rd, h * LEVELS + LEVELS - 1)
                for n in range(2):
                    for g in range(4):
                        last = pe.transpose(bank[2 if n == 0 else 0][:, g * P:(g + 1) * P],
                                            k_w[:, (4 * n + g) * P:(4 * n + g + 1) * P], ident[:, :])
                    last.then_inc(kt_mm, 1)

            def att_kv(h):
                pe.wait_ge(lv_rd, h * LEVELS + LEVELS)
                for n in range(2):
                    pe.wait_ge(kt_cp, h * 2 + 1 + n)
                    for g in range(4 - n):
                        cut = slice((4 * n + g) * P, (4 * n + g + 1) * P)
                        last = mm(bank[1 + n][:, g * P:(g + 1) * P], k_t[:, cut], v_t[:, cut])
                    last.then_inc(kv_mm, 1)

            def att_out(h, n):
                pe.wait_ge(st_done, h * 2 + 1 + n)
                for g in range(4):
                    cut = slice((4 * n + g) * P, (4 * n + g + 1) * P)
                    alone = 4 * n + g == 0
                    last = mm(bank[n][:, g * P:(g + 1) * P], att[:, cut], v_t[:, cut], True, alone)
                    if not alone:
                        last = mm(bank[n][:, g * P:(g + 1) * P], q_w[:, cut], s_st[:, cut], False, True)
                last.then_inc(o_mm, 1)

            def att_back(h):
                for n in range(2):
                    pe.wait_ge(o_scaled, h * 2 + 1 + n)
                    for g in range(4):
                        last = pe.transpose(bank[2 if n == 0 else 0][:, g * P:(g + 1) * P],
                                            o_sb[:, (4 * n + g) * P:(4 * n + g + 1) * P], ident[:, :])
                    last.then_inc(back_mm, 1)

            def attention(h, first=False):
                def level(lv):
                    return lambda: att_level(h, lv)

                def start():
                    att_diag(h, first)
                    att_level(h, 0)

                return {(0, 1): start, (0, 3): level(1), (0, 5): level(2), (0, 7): lambda: att_vt(h, 0),
                        (1, 1): level(3), (1, 3): level(4), (1, 5): level(5), (1, 7): lambda: att_vt(h, 1),
                        (2, 1): level(6), (2, 3): lambda: att_kt(h), (2, 5): lambda: att_kv(h),
                        (2, 7): lambda: att_out(h, 0), (3, 1): lambda: att_out(h, 1),
                        (3, 6): lambda: att_back(h)}

            def hg_head(h, pieces, first=False):
                for k in range(4):
                    s = step_of(HG_IN, 4, h, k)
                    gaps = {at: piece for (step_at, at), piece in pieces.items() if step_at == k}
                    if first and k == 0:
                        gaps = norm_gaps(3, seen(HG_IN, 1))
                    step(s, B, ready=3 * NT + NT * BLOCKS if first and k == 0 else None, gaps=gaps)
                    sums(s, 1, events(s.t), seen(s.t, 2)).then_inc(mm_done, 1)

            hg_head(0, {}, first=True)
            hg_head(1, attention(0, first=True))
            with pe.Fori(2, NT) as i:
                hg_head(i, attention(i - 1))

            after_hg = 4 * NT + NT * BLOCKS
            pieces = list(attention(NT - 1).values())
            pieces.pop(0)()
            out_steps = [step_of(HG_OUT, 4, 0, n) for n in range(2)]
            for n, s in enumerate(out_steps):
                step(s, B, ready=after_hg if n == 0 else None, tiles=range(NT - 1),
                     gaps={k: pieces.pop(0) for k in range(min(NT - 1, len(pieces)))})
            while pieces:
                pieces.pop(0)()
            for s in out_steps:
                step(s, B, ready=after_hg, tiles=range(NT - 1, NT)).then_inc(mm_done, 1)
            for n in range(2, NT):
                step(step_of(HG_OUT, 4, 0, n), B).then_inc(mm_done, 1)

            mlp(1, MLP1, 0, A, B, after_hg + 2 * NT, first=True)
            with pe.Fori(1, BLOCKS) as b:
                mlp(1, MLP1, b, A, B, after_hg + 2 * NT)

            stats(5, ev_mlp1(BLOCKS, 0) + 2 + 3)
            pe.wait_ge(gained, NT)
            for r in range(NC):
                if r >= 2:
                    pe.wait_ge(row_out[r % 2], r // 2)
                else:
                    pe.wait_ge(ps_free, END - 1 + r)
                for n in range(NT):
                    last = pe.transpose(acc[r % 2][:, n * P:(n + 1) * P],
                                        at2[:, n, r * P:(r + 1) * P], ident[:, :])
                last.then_inc(out_mm, 1)

        @block.scalar
        def _(act):
            def split_hi(s, fresh=False):
                act.wait_ge(w_loaded[s.odd], s.half * 16 + 16)
                if not fresh:
                    act.wait_ge(mm_done, s.t - 1)
                act.activation(w_hi[:, s.odd, :, :], stage[:, s.odd, :, :], ACT.Copy).then_inc(hi_ready, 1)

            def tile(buf, n):
                return buf[:, bass.ds(n, 1), :].rearrange("p a t -> p (a t)")

            def root(norm):
                act.wait_ge(ms_ready, norm)
                act.activation(nst[:, 1, :], nst[:, 0, :], ACT.Sqrt).then_inc(root_ready, 1)

            for dst, src in vectors[len(vectors) // 2:]:
                act.dma_start(dst, src).then_inc(vec_loaded, 16)

            def x_part(r):
                act.wait_ge(x_loaded[r], 16)
                act.activation(tmp[:, :], xin[:, r, :], ACT.Square, accum_out=nst[:, 1, r:r + 1]
                               ).then_inc(x_squared, 1)
                act.drain()
                if r % 2:
                    act.wait_ge(xt_mm, r + 1)
                    act.activation(res[:, :, r * P:(r + 1) * P], acc[1].rearrange("p (n t) -> p n t", t=P),
                                   ACT.Copy).then_inc(xt_cp[1], 1)

            for r in range(NC // 2):
                x_part(r)
            act.wait_ge(vec_c, 2)
            act.activation(cs[:, :], vec2[:, C_C:C_C + 8], ACT.Silu).then_inc(small_a, 1)
            for r in range(NC // 2, NC):
                x_part(r)
            act.wait_ge(small_d, 1)
            act.activation(sm[:, 1, :], sm[:, 0, :], ACT.Exp, scale=-1.0)
            act.activation(sm[:, 3:5, :], sm[:, 3:5, :], ACT.Exp).then_inc(small_a, 1)
            split_hi(step_of(0, 2, 0, 0), fresh=True)
            for n in range(2):
                act.wait_ge(xt_cp[n], NC // 2)
            act.wait_ge(small_d, 2)
            for n in range(NT):
                act.activation(a_hi[:, n, :], res[:, n, :], ACT.Identity, scale=amp[:, 0, n:n + 1]
                               ).then_inc(in_hi, 1)
                if n == 1:
                    root(1)
            split_hi(step_of(0, 2, 0, 1), fresh=True)

            def vcol(at, h):
                return vec2[:, bass.ds(at + h, 1)]

            def gate_split(h, first=False):
                act.wait_ge(g_loaded, h * 32 + 32)
                if not first:
                    act.wait_ge(gate_mm, h * 4)
                act.activation(gw_hi[:, :, :], gst[:, :, :], ACT.Copy).then_inc(gw_hi_r, 1)

            def rg_even(h, first=False):
                act.wait_ge(scaled, h * 2 + 1)
                if first:
                    act.wait_ge(spilled0, 16)
                    act.wait_ge(in_lo, NT)
                    act.wait_ge(small_d, 4)
                else:
                    act.wait_ge(xc_done, h)
                act.activation(xbp[:, TAPS - 1:], acc[0][:, :], ACT.Identity, bias=bcol[:, 0:1]
                               ).then_inc(ps_free, 1)
                act.drain()
                if not first:
                    act.wait_ge(ix_done, h)
                act.activation(xc, xbp[:, 0:T], ACT.Identity, scale=vcol(C_CW, h), bias=vcol(C_CB, h)
                               ).then_inc(xc0, 1)

            def rg_even_split(h, first=False):
                act.wait_ge(xc_done, h + 1)
                if not first:
                    act.wait_ge(gate_mm, h * 4)
                act.activation(xc_hi[:, :], xc, ACT.Copy).then_inc(xc_hi_r, 1)

            def rg_odd(h, first=False):
                act.wait_ge(scaled, h * 2 + 2)
                if not first:
                    act.wait_ge(gy_done, h)
                act.activation(yb[:, :], acc[1][:, :], ACT.Identity, bias=bcol[:, 1:2]).then_inc(ps_free, 1)
                act.drain()

            def rg_poly():
                act.activation(ytmp[:, :], yb[:, :], ACT.Square)
                act.drain()
                act.activation(ytmp[:, :], ytmp[:, :], ACT.Identity, scale=0.044715, bias=1.0
                               ).then_inc(y_poly, 1)

            def rg_gates(h):
                for g in range(2):
                    act.activation(gbias[:, g:g + 1], vcol((C_BA, C_BX)[g], h), ACT.Copy)
                act.drain()
                for q in range(4):
                    g, n = q % 2, q // 2
                    act.wait_ge(gate_mm, h * 4 + q + 1)
                    act.activation((r_g, i_g)[g][:, n * HALF:(n + 1) * HALF], bank[q % 3][:, :], ACT.Sigmoid,
                                   bias=gbias[:, g:g + 1]).then_inc(gate_rd, 1)
                act.drain()
                act.activation(th, r_g, ACT.Tanh, scale=decay[:, 0, bass.ds(h, 1)])

            def rg_gelu(h, first=False):
                if not first:
                    act.wait_ge(og_done, h)
                act.wait_ge(y_arg, h + 1)
                act.activation(ysig[:, :], ytmp[:, :], ACT.Sigmoid, scale=2 * 0.7978845608028654
                               ).then_inc(y_sig, 1)

            def rg_decay(h):
                act.activation(a_g, r_g, ACT.Exp, scale=decay[:, 1, bass.ds(h, 1)])
                act.drain()
                act.activation(m_g, a_g, ACT.Square).then_inc(ga_done, 1)

            def rg_factor(h):
                act.wait_ge(gp_done, h + 1)
                act.activation(m_g, m_g, ACT.Sqrt).then_inc(gm_done, 1)

            split_hi(step_of(RG_IN, 2, 0, 2))
            rg_even(0, first=True)
            gate_split(0, first=True)
            rg_even_split(0, first=True)
            rg_odd(0, first=True)
            rg_poly()
            split_hi(step_of(RG_IN, 2, 0, 3))
            act.wait_ge(spilled, SPILLED0)

            def rg_head(j, first=False, last=False):
                rg_gates(j - 1)
                rg_gelu(j - 1, first)
                split_hi(step_of(RG_IN, 2, j, 2))
                rg_even(j)
                rg_decay(j - 1)
                gate_split(j)
                rg_even_split(j)
                rg_factor(j - 1)
                if last:
                    act.wait_ge(mm_done, RG_OUT)
                    rg_split(range(4))
                rg_odd(j)
                if not last:
                    rg_poly()
                split_hi(step_of(RG_IN, 2, j, 3))

            A, B = (a_hi, a_lo), (b_hi, b_lo)

            def rg_split(heads):
                for n in heads:
                    act.activation(a_hi[:, n, :], o_rg[:, n, :], ACT.Copy).then_inc(in_hi, 1)

            rg_head(1, first=True)
            with act.Fori(2, NT - 1) as j:
                rg_head(j)
            rg_head(NT - 1, last=True)
            rg_gates(NT - 1)
            act.wait_ge(og_done, NT - 1)
            rg_decay(NT - 1)
            rg_poly()
            rg_split((4,))
            rg_factor(NT - 1)
            rg_split((5,))
            rg_gelu(NT - 1)
            rg_split((6,))
            act.wait_ge(og_done, NT)
            rg_split(range(NT - 1, NT))

            def new_input(dst, k, n, x_before):
                act.wait_ge(x_new, x_before + n + 1)
                act.wait_ge(sq_added, n + (9 * k - 8))
                act.wait_ge(small_d, 4 + k)
                act.activation(tile(dst, n), tile(res, n), ACT.Identity, scale=amp[:, k, bass.ds(n, 1)]
                               ).then_inc(in_hi, 1)
                act.activation(tmp[:, :], tile(res, n), ACT.Square).then_inc(sq_part, 1)

            with act.Fori(0, 4) as m:
                for k in range(2):
                    split_hi(step_of(RG_OUT, 2, m, k + 2))
                    new_input(b_hi, 1, m * 2 + k, 0)

            def mlp(layer, base, b, hid, scaled_before, last=False, first=False):
                def one(q, k):
                    n = q * 4 + k
                    s = Step(base + b * (2 * NT) + n, None, k % 2)
                    act.wait_ge(scaled, scaled_before + b * NT + n + 1)
                    act.activation(acc[k % 2][:, :], acc[k % 2][:, :], ACT.Relu, bias=bcol[:, k % 2:k % 2 + 1])
                    act.drain()
                    act.activation(acc[k % 2][:, :], acc[k % 2][:, :], ACT.Square)
                    act.drain()
                    act.activation(tile(hid[0], n), acc[k % 2][:, :], ACT.Copy).then_inc(in_hi, 1)

                def ahead(q, k, off):
                    st = step_of(base + off, 2 * NT, b, k + 2)
                    split_hi(Step(st.t + q * 4, st.half + q * 2, st.odd))

                if first:
                    root(2 + 2 * layer)
                with act.Fori(0, 2) as q:
                    for k in range(4):
                        one(q, k)
                        ahead(q, k, 0)
                for q in range(2) if last and layer == 1 else [None]:
                    if q is None:
                        with act.Fori(0, 2) as q:
                            for k in range(4):
                                ahead(q, k, NT)
                                if last:
                                    new_input(last[0], last[1], q * 4 + k, last[2])
                    else:
                        for k in range(4):
                            n = q * 4 + k
                            if n < NT - 2:
                                ahead(q, k, NT)
                            act.wait_ge(x_new, 2 * (NT + NT * BLOCKS) - NT + n + 1)
                            act.wait_ge(sq_added, n + (9 * 4 - 8))
                            act.activation(tmp[:, :], res[:, n, :], ACT.Square).then_inc(sq_part, 1)
                            act.activation(at2[:, n, :], res[:, n, :], ACT.Identity,
                                           scale=vec2[:, C_NF + n:C_NF + n + 1]).then_inc(gained, 1)

            mlp(0, MLP0, 0, A, 2 * NT, first=True)
            with act.Fori(1, BLOCKS - 1) as b:
                mlp(0, MLP0, b, A, 2 * NT)
            mlp(0, MLP0, BLOCKS - 1, A, 2 * NT, last=(b_hi, 2, NT * BLOCKS))
            root(3)

            def hg_evict(h, k):
                act.wait_ge(scaled, h * 4 + (2 * NT + NT * BLOCKS) + k + 1)
                b = bcol[:, k % 2:k % 2 + 1]
                if k == 1:
                    act.activation(L_s, acc[1][:, :], ACT.Sigmoid, bias=b).then_inc(ps_free, 1)
                elif k == 2:
                    act.activation(L_v, acc[0][:, :], ACT.Identity, bias=b).then_inc(ps_free, 1)
                else:
                    act.activation(t_s, acc[k % 2][:, :], ACT.Sigmoid, bias=b).then_inc(sg_done, 1)

            def hg_vt(h, n):
                act.wait_ge(vt_mm, h * 2 + n + 1)
                act.activation(v_t[:, n * HALF:(n + 1) * HALF], bank[0][:, :], ACT.Copy).then_inc(vt_cp, 1)

            def hg_kt(h):
                for n in range(2):
                    act.wait_ge(kt_mm, h * 2 + n + 1)
                    act.activation(k_t[:, n * HALF:(n + 1) * HALF], bank[2 if n == 0 else 0][:, :], ACT.Copy
                                   ).then_inc(kt_cp, 1)

            def hg_o(h, n):
                act.wait_ge(o_mm, h * 2 + n + 1)
                for g in range(4 * n, 4 * n + 4):
                    last = act.activation(o_sq[:, g * P:(g + 1) * P], bank[n][:, g % 4 * P:(g % 4 + 1) * P],
                                          ACT.Square, accum_out=nst[:, 1, g:g + 1])
                last.then_inc(o_cp, 1)

            def hg_root(h):
                act.wait_ge(hms, h + 1)
                act.activation(nst[:, 1, :], nst[:, 0, :], ACT.Sqrt).then_inc(hroot, 1)

            def hg_step(i, k):
                split_hi(step_of(HG_IN, 4, i, k + 2))
                hg_evict(i, k)

            act.wait_ge(spilled, SPILLED1)
            act.wait_ge(in_lo, 3 * NT + NT * BLOCKS + NT)
            for k in range(3):
                hg_step(0, k)
            with act.Fori(1, NT) as i:
                hg_step(i - 1, 3)
                hg_vt(i - 1, 0)
                hg_step(i, 0)
                hg_vt(i - 1, 1)
                hg_step(i, 1)
                hg_kt(i - 1)
                hg_o(i - 1, 0)
                hg_step(i, 2)
                hg_o(i - 1, 1)
                hg_root(i - 1)

            def head_split(n):
                act.activation(b_hi[:, n, :], o_hg[:, n, :], ACT.Copy).then_inc(in_hi, 1)

            act.wait_ge(on_done, NT - 1)
            act.wait_ge(mm_done, HG_OUT)
            for n in range(NT - 1):
                head_split(n)
            hg_step(NT - 1, 3)
            for n in range(2):
                hg_vt(NT - 1, n)
            hg_kt(NT - 1)
            for n in range(2):
                hg_o(NT - 1, n)
            hg_root(NT - 1)
            act.wait_ge(on_done, NT)
            head_split(NT - 1)
            with act.Fori(0, 2) as m:
                for k in range(4):
                    split_hi(step_of(HG_OUT, 4, m, k + 2))
                    new_input(a_hi, 3, m * 4 + k, NT + NT * BLOCKS)

            before = 2 * NT + NT * BLOCKS + 4 * NT
            mlp(1, MLP1, 0, B, before, first=True)
            with act.Fori(1, BLOCKS - 1) as b:
                mlp(1, MLP1, b, B, before)
            mlp(1, MLP1, BLOCKS - 1, B, before, last=True)
            root(5)
            act.wait_ge(last_rms, 1)
            for r in range(0, NC, 2):
                act.wait_ge(out_mm, r + 1)
                act.activation(o_hg[:, r, :], acc[0][:, :], ACT.Copy, scale=nst[:, 2, r:r + 1]
                               ).then_inc(row_out[0], 1)

        @block.vector
        def _(dve):
            tt, ts, stt = dve.tensor_tensor, dve.tensor_scalar, dve.scalar_tensor_tensor

            def tile(buf, n):
                return buf[:, bass.ds(n, 1), :].rearrange("p a t -> p (a t)")

            def split_lo(s):
                dve.wait_ge(hi_ready, s.t + 1)
                tt(w_lo[:, s.odd, :, :], stage[:, s.odd, :, :], w_hi[:, s.odd, :, :].bitcast(f32),
                   ALU.subtract).then_inc(lo_ready, 1)

            def ops(*todo):
                for op in todo:
                    op()
                    dve.drain()

            def x_copy(r):
                dve.wait_ge(xt_mm, r + 1)
                dve.tensor_copy(res[:, :, r * P:(r + 1) * P],
                                acc[0].rearrange("p (n t) -> p n t", t=P)).then_inc(xt_cp[0], 1)

            for r in range(0, NC // 2 + 1, 2):
                x_copy(r)
            dve.wait_ge(vec_t, 2)
            dve.tensor_copy(vec1[:, :], bank[0][:, 0:P]).then_inc(vec_c, 1)
            dve.tensor_copy(vec2[:, :], bank[1][:, 0:V2]).then_inc(vec_c, 1)
            dve.drain()
            lam = vec2[:, C_LAM:C_LAM + 8]
            lb0, lb1 = vec2[:, C_LB:C_LB + 8], vec2[:, C_LB + 8:C_LB + 16]
            ops(lambda: ts(sm[:, 0, :], lam, -1.0, None, ALU.mult),
                lambda: ts(sm[:, 2, :], sm[:, 0, :], 0.0, None, ALU.max),
                lambda: tt(sm[:, 0, :], sm[:, 0, :], lam, ALU.max),
                lambda: tt(sm[:, 5, :], lb0, lb1, ALU.max),
                lambda: tt(sm[:, 3, :], lb0, sm[:, 5, :], ALU.subtract))
            tt(sm[:, 4, :], lb1, sm[:, 5, :], ALU.subtract).then_inc(small_d, 1)
            x_copy(NC - 2)

            def weigh(weights, loaded, total, start):
                for k in range(start, NT):
                    dve.wait_ge(loaded[k], 16)
                    if k == start:
                        ts(total[:, :], weights[:, k, :], cs[:, k:k + 1], None, ALU.mult)
                    else:
                        stt(total[:, :], weights[:, k, :], cs[:, k:k + 1], total[:, :], ALU.mult, ALU.add)
                    dve.drain()

            dve.wait_ge(small_a, 1)
            weigh(w_scale, scale_loaded, scale_sum, 0)
            dve.drain().then_inc(wsum_done, 1)
            split_lo(step_of(0, 2, 0, 0))

            def make_amp(k, table, name, gain):
                dve.drain()
                last = stt(amp[:, k, :], mod[:, table[name]:table[name] + NT], 1.0,
                           vec1[:, gain:gain + NT], ALU.add, ALU.mult)
                return last

            dve.wait_ge(vec_t, 3)
            at = MOD0["sc_t"]
            tt(mod[:, at:at + NT], cols[:, 0:NT], vec1[:, at:at + NT], ALU.add).then_inc(cols_read, 1)
            make_amp(0, MOD0, "sc_t", 96).then_inc(small_d, 1)

            def in_lo_res(dst, k, n, hi_before):
                dve.wait_ge(in_hi, hi_before + n + 1)
                stt(tile(dst[1], n), tile(res, n), amp[:, k, bass.ds(n, 1)],
                    tile(dst[0], n).bitcast(f32), ALU.mult, ALU.subtract).then_inc(in_lo, 1)

            A, B = (a_hi, a_lo), (b_hi, b_lo)
            dve.drain()

            def rms(src, n_mean, eps, after, ready, before, buf=None):
                ts(nst[:, 0, :], src, 1.0 / n_mean, eps, ALU.mult, ALU.add).then_inc(ready, 1)
                dve.wait_ge(after, before)
                ops(lambda: dve.reciprocal(nst[:, 2, :], nst[:, 1, :]),
                    lambda: tt(nst[:, 3, :], nst[:, 2, :], nst[:, 2, :], ALU.mult),
                    lambda: tt(nst[:, 3, :], nst[:, 3, :], nst[:, 0, :], ALU.mult),
                    lambda: ts(nst[:, 3, :], nst[:, 3, :], -0.5, 1.5, ALU.mult, ALU.add),
                    lambda: tt(nst[:, 2, :], nst[:, 2, :], nst[:, 3, :], ALU.mult))
                if buf is None:
                    return dve.drain()
                return tt(buf.rearrange("p (g t) -> p g t", t=P),
                          ident[:, :].unsqueeze(1).broadcast_to([P, NC, P]),
                          nst[:, 2, :].unsqueeze(2).broadcast_to([P, NC, P]), ALU.mult)

            def to_rstd(n):
                dve.wait_ge(bc_mm, n)
                for q in range(2):
                    last = dve.tensor_copy(rstd[:, q * HALF:(q + 1) * HALF], bank[q][:, :])
                last.then_inc(rstd_ready, 1)
                dve.drain()

            def norm(n):
                dve.wait_ge(stat_mm, n - 1)
                rms(cols[:, 0:NC], D, EPS, root_ready, ms_ready, n, tmp[:, :]).then_inc(diag_ready, 1)
                dve.drain().then_inc(cols_read, 1)
                to_rstd(n)

            def clear_squares():
                dve.memset(rstd[:, :], 0.0)
                dve.drain().then_inc(sq_added, 1)

            def add_square(k, n):
                dve.wait_ge(sq_part, n + (NT * k + 1))
                tt(rstd[:, :], rstd[:, :], tmp[:, :], ALU.add)
                dve.drain().then_inc(sq_added, 1)

            def scale_sums(s, mods=0, at=None):
                dve.wait_ge(mm_done, s.t + 1)
                last = dve.tensor_copy(bcol[:, s.odd:s.odd + 1], cols[:, 0:1])
                if mods:
                    last = tt(mod[:, bass.ds(at, mods)], cols[:, 1:1 + mods], vec1[:, bass.ds(at, mods)], ALU.add)
                last.then_inc(cols_read, 1)
                return tt(acc[s.odd][:, :], acc[s.odd][:, :], rstd[:, :], ALU.mult).then_inc(scaled, 1)

            for n in range(2):
                in_lo_res(A, 0, n, 0)
            dve.wait_ge(x_squared, NC)
            rms(nst[:, 1, :], D, EPS, root_ready, ms_ready, 1, tmp[:, :]).then_inc(diag_ready, 1)
            for n in range(2, NT):
                in_lo_res(A, 0, n, 0)
            split_lo(step_of(0, 2, 0, 1))
            weigh(w_shift, shift_loaded, shift_sum, POOL_K)
            dve.wait_ge(shift_part, 1)
            tt(shift_sum[:, :], shift_sum[:, :], w_shift[:, 0, :], ALU.add)
            dve.drain().then_inc(wsum_done, 1)
            to_rstd(1)
            dve.wait_ge(vec_t, 4)
            tt(mod[:, 0:NT], cols[:, 0:NT], vec1[:, 0:NT], ALU.add).then_inc(cols_read, 1)
            dve.drain().then_inc(small_d, 1)
            dve.memset(xbp[:, 0:TAPS - 1], 0.0).then_inc(small_d, 1)
            dve.wait_ge(small_a, 2)
            w, z, z2, p = sm[:, 1, :], small[:, 0, :], small[:, 1, :], small[:, 2, :]
            ops(lambda: ts(z, w, 2.0, None, ALU.add),
                lambda: dve.reciprocal(z, z),
                lambda: tt(z, z, w, ALU.mult),
                lambda: tt(z2, z, z, ALU.mult),
                lambda: ts(p, z2, 2.0 / 17, None, ALU.mult),
                *(lambda n=n: stt(p, p, 2.0 / n, z2, ALU.add, ALU.mult) for n in range(15, 1, -2)),
                lambda: stt(p, p, 2.0, z, ALU.add, ALU.mult),
                lambda: tt(p, p, sm[:, 2, :], ALU.add),
                lambda: ts(decay[:, 0, :], p, 8.0, None, ALU.mult),
                lambda: ts(decay[:, 1, :], p, -8.0, None, ALU.mult))


            def gate_split(h):
                dve.wait_ge(gw_hi_r, h + 1)
                tt(gw_lo[:, :, :], gst[:, :, :], gw_hi[:, :, :].bitcast(f32), ALU.subtract
                   ).then_inc(gw_lo_r, 1)

            def rg_conv(h):
                dve.wait_ge(xc0, h + 1)
                for k in range(1, TAPS):
                    stt(xc, xbp[:, k:k + T], vec2[:, bass.ds(C_CW + NT * k + h, 1)], xc,
                               ALU.mult, ALU.add)
                    last = dve.drain()
                last.then_inc(xc_done, 1)

            def rg_conv_split(h):
                dve.wait_ge(xc_hi_r, h + 1)
                tt(xc_lo[:, :], xc, xc_hi[:, :].bitcast(f32), ALU.subtract).then_inc(xc_lo_r, 1)

            def rg_y(h):
                dve.wait_ge(y_poly, h + 1)
                tt(ytmp[:, :], ytmp[:, :], yb[:, :], ALU.mult).then_inc(y_arg, 1)

            def rg_ix(h):
                dve.wait_ge(gate_rd, h * 4 + 4)
                tt(ix_g, i_g, xc, ALU.mult).then_inc(ix_done, 1)

            def rg_root_arg(h):
                dve.wait_ge(ga_done, h + 1)
                stt(m_g, m_g, 1.0, th, ALU.add, ALU.mult).then_inc(gp_done, 1)

            def rg_scan(h):
                dve.wait_ge(gm_done, h + 1)
                dve.memset(m_g[:, 0:1], 1.0)
                dve.drain()
                tt(m_g, m_g, ix_g, ALU.mult)
                dve.drain()
                dve.tensor_tensor_scan(h_g, a_g, m_g, 0.0, ALU.mult, ALU.add)
                dve.drain()
                dve.wait_ge(gy_done, h + 1)
                tt(tile(o_rg, h), h_g, ysig[:, :], ALU.mult).then_inc(og_done, 1)

            def rg_head(j, last_head=None, last=False):
                if last_head is not None:
                    rg_ix(last_head)
                scale_sums(step_of(RG_IN, 2, j, 0), 1, j * 2 + 16)
                split_lo(step_of(RG_IN, 2, j, 2))
                rg_conv(j)
                gate_split(j)
                if last_head is not None:
                    rg_root_arg(last_head)
                rg_conv_split(j)
                scale_sums(step_of(RG_IN, 2, j, 1), 1, j * 2 + 17)
                if last:
                    rg_split(range(4))
                if last_head is not None:
                    rg_scan(last_head)
                if not last:
                    rg_y(j)
                split_lo(step_of(RG_IN, 2, j, 3))

            def rg_split(heads):
                for n in heads:
                    dve.wait_ge(in_hi, NT + n + 1)
                    tt(a_lo[:, n, :], o_rg[:, n, :], a_hi[:, n, :].bitcast(f32), ALU.subtract).then_inc(in_lo, 1)

            rg_head(0)
            with dve.Fori(1, NT - 1) as j:
                rg_head(j, j - 1)
            rg_head(NT - 1, NT - 2, last=True)
            rg_ix(NT - 1)
            rg_root_arg(NT - 1)
            rg_y(NT - 1)
            rg_split((4, 5, 6))
            rg_scan(NT - 1)
            rg_split(range(NT - 1, NT))
            make_amp(1, MOD0, "sc_c", 112).then_inc(small_d, 1)
            clear_squares()

            def renew(s, n, table, name):
                dve.wait_ge(mm_done, s.t + 1)
                return stt(tile(res, n), acc[s.odd][:, :], mod[:, bass.ds(table[name] + n, 1)], tile(res, n),
                           ALU.mult, ALU.add).then_inc(x_new, 1)

            def freed():
                dve.drain().then_inc(ps_free, 1)

            def rg_out(m):
                for k in range(2):
                    s, n = step_of(RG_OUT, 2, m, k), m * 2 + k
                    dve.wait_ge(mm_done, s.t + 1)
                    tt(mod[:, bass.ds(n * 2 + 32, 2)], cols[:, 0:2], vec1[:, bass.ds(n * 2 + 32, 2)], ALU.add
                       ).then_inc(cols_read, 1)
                    renew(s, n, MOD0, "g_t")
                    freed()
                    split_lo(step_of(RG_OUT, 2, m, k + 2))
                    in_lo_res(B, 1, n, 2 * NT)
                    add_square(0, n)

            dve.wait_ge(reloaded_head[0], 16 * HEAD)
            rg_out(0)
            dve.wait_ge(reloaded[0], 16 * (NT - HEAD))
            with dve.Fori(1, 4) as m:
                rg_out(m)

            def mlp(layer, base, b, hid, tiles, last=False, first=False):
                table = MOD0 if layer == 0 else MOD1

                def ahead(q, k, off):
                    split_lo(Step(base + off + b * (2 * NT) + q * 4 + k + 2, None, k % 2))

                if first:
                    norm(2 + 2 * layer)
                with dve.Fori(0, 2) as q:
                    for k in range(4):
                        s = Step(base + b * (2 * NT) + q * 4 + k, None, k % 2)
                        scale_sums(s)
                        dve.wait_ge(in_hi, tiles + b * NT + q * 4 + k + 1)
                        tt(tile(hid[1], q * 4 + k), acc[s.odd][:, :], tile(hid[0], q * 4 + k).bitcast(f32),
                           ALU.subtract).then_inc(in_lo, 1)
                        freed()
                        ahead(q, k, 0)

                def out_step(q, k):
                    s = Step(base + NT + b * (2 * NT) + q * 4 + k, None, k % 2)
                    if layer == 0:
                        mods, at = 2 - k % 2, b * 12 + q * 6 + (0, 2, 3, 5)[k] + 48
                        dve.wait_ge(mm_done, s.t + 1)
                        tt(mod[:, bass.ds(at, mods)], cols[:, 0:mods], vec1[:, bass.ds(at, mods)], ALU.add
                           ).then_inc(cols_read, 1)
                    renew(s, q * 4 + k, table, "g_c")
                    freed()
                    if last and layer == 0:
                        in_lo_res(B, 2, q * 4 + k, 3 * NT + NT * BLOCKS)
                    if last:
                        add_square(1 + 2 * layer, q * 4 + k)
                    if not (last and layer == 1 and q * 4 + k >= NT - 2):
                        ahead(q, k, NT)

                if last:
                    clear_squares()
                if last and layer == 0:
                    make_amp(2, MOD1, "sc_t", 104).then_inc(small_d, 1)
                    dve.drain()
                if last and layer == 1:
                    for q in range(2):
                        for k in range(4):
                            out_step(q, k)
                else:
                    with dve.Fori(0, 2) as q:
                        for k in range(4):
                            out_step(q, k)

            mlp(0, MLP0, 0, A, 3 * NT, first=True)
            with dve.Fori(1, BLOCKS - 1) as b:
                mlp(0, MLP0, b, A, 3 * NT)
            ops(lambda: tt(sm[:, 5, :], sm[:, 3, :], sm[:, 4, :], ALU.add),
                lambda: dve.reciprocal(sm[:, 5, :], sm[:, 5, :]),
                lambda: tt(sm[:, 3, :], sm[:, 3, :], sm[:, 5, :], ALU.mult),
                lambda: tt(sm[:, 4, :], sm[:, 4, :], sm[:, 5, :], ALU.mult),
                lambda: tt(sm[:, 4, :], sm[:, 3, :], sm[:, 4, :], ALU.add),
                lambda: tt(lbs[:, 0, :], sm[:, 4, :], sm[:, 3, :], ALU.subtract),
                lambda: ts(lbs[:, 1, :], lbs[:, 0, :], -1.0, 1.0, ALU.mult, ALU.add),
                lambda: ts(lbs[:, 2, :], lbs[:, 1, :], -1.0, None, ALU.mult))
            mlp(0, MLP0, BLOCKS - 1, A, 3 * NT, last=True)
            norm(3)

            def hg_evict(h, k):
                s = step_of(HG_IN, 4, h, k)
                scale_sums(s)
                split_lo(step_of(HG_IN, 4, h, k + 2))
                if k in (0, 3):
                    dve.wait_ge(sg_done, h * 2 + (1 if k == 0 else 2))
                    stt(L_q if k == 0 else L_g, acc[s.odd][:, :], bcol[:, s.odd:s.odd + 1], t_s,
                        ALU.add, ALU.mult).then_inc(ps_free, 1)

            def blocks(buf, size):
                return buf.rearrange("p (n two j) -> p n two j", two=2, j=size)

            tot_at = [0]
            for lv in range(LEVELS):
                tot_at.append(tot_at[-1] + (T >> (lv + 1)))

            def totals(lv):
                return f_w if lv == 0 else tot[:, tot_at[lv - 1]:tot_at[lv]]

            def hg_prep(h, first=False):
                if not first:
                    dve.wait_ge(o_mm, h * 2)
                dve.wait_ge(ps_free, h * 4 + (HG_IN + 2))
                lb = lambda n: lbs[:, n, bass.ds(h, 1)]
                ts(f_w, L_s, lb(1), lb(0), ALU.mult, ALU.add)
                ts(k_w, L_s, lb(2), lb(1), ALU.mult, ALU.add)
                dve.drain()
                tt(q_w, L_q, f_w, ALU.mult).then_inc(prep, 1)

            def hg_diag(h):
                for n in range(2):
                    dve.wait_ge(dg_mm, h * 2 + n + 1)
                    tt(att[:, n * HALF:(n + 1) * HALF].rearrange("p (g t) -> p g t", t=P),
                       bank[2 if n == 0 else 0][:, :].rearrange("p (g t) -> p g t", t=P),
                       ident[:, :].unsqueeze(1).broadcast_to([P, 4, P]), ALU.mult).then_inc(dg_rd, 1)

            def hg_reach(h, lv):
                size = 1 << lv
                dve.wait_ge(lv_mm, h * LEVELS + lv + 1)
                q4, k4 = blocks(q_w, size), blocks(k_w, size)
                t2 = totals(lv).rearrange("p (n two) -> p n two", two=2)
                shape = [P, T // 2 // size, size]
                tt(q4[:, :, 1, :], q4[:, :, 1, :], t2[:, :, 0:1].broadcast_to(shape), ALU.mult)
                tt(totals(lv + 1), t2[:, :, 0], t2[:, :, 1], ALU.mult)
                tt(k4[:, :, 0, :], k4[:, :, 0, :], t2[:, :, 1:2].broadcast_to(shape), ALU.mult
                   ).then_inc(lv_up, 1)
                dve.drain()

            def hg_take(lv):
                size = 1 << lv
                a5 = att.rearrange("p (g n two j) -> p g n two j", g=NC, two=2, j=size)[:, :, :, 1, :]
                m5 = mask[:, lv, :].rearrange("p (n j) -> p n j", j=size).bitcast(u32)
                dve.copy_predicated(
                    a5, m5.unsqueeze(1).broadcast_to([P, NC, P // 2 // size, size]),
                    bank[1 + lv % 2][:, :].rearrange("p (g n j) -> p g n j", g=NC, j=size)).then_inc(lv_rd, 1)

            def hg_levels(h, levels):
                for lv in levels:
                    hg_reach(h, lv)
                    if lv == 0:
                        hg_diag(h)
                        dve.drain()
                    hg_take(lv)

            def hg_states(h):
                for g in range(NC - 1):
                    if g % 4 == 0:
                        dve.wait_ge(kv_mm, h * 2 + g // 4 + 1)
                    src = bank[1 + g // 4][:, (g % 4) * P:(g % 4 + 1) * P]
                    dst = s_st[:, (g + 1) * P:(g + 2) * P]
                    if g == 0:
                        last = dve.tensor_copy(dst, src)
                    else:
                        last = stt(dst, s_st[:, g * P:(g + 1) * P], totals(LEVELS)[:, g:g + 1], src,
                                   ALU.mult, ALU.add)
                    if g == 2 or g == NC - 2:
                        last.then_inc(st_done, 1)
                    dve.drain()

            def hg_norm(h):
                dve.wait_ge(o_cp, h * 2 + 2)
                rms(nst[:, 1, :], P, GEPS, hroot, hms, h + 1)
                for n in range(2):
                    tt(o_sb[:, n * HALF:(n + 1) * HALF].rearrange("p (g v) -> p g v", v=P),
                       bank[n][:, :].rearrange("p (g v) -> p g v", v=P),
                       nst[:, 2, 4 * n:4 * n + 4].unsqueeze(2).broadcast_to([P, 4, P]), ALU.mult
                       ).then_inc(o_scaled, 1)

            def hg_o(h):
                for n in range(2):
                    cut = slice(n * HALF, (n + 1) * HALF)
                    dve.wait_ge(back_mm, h * 2 + n + 1)
                    last = stt(o_hg[:, bass.ds(h, 1), cut].rearrange("p a t -> p (a t)"),
                               bank[2 if n == 0 else 0][:, :], vec2[:, C_GN:C_GN + 1], L_g[:, cut],
                               ALU.mult, ALU.mult)
                last.then_inc(on_done, 1)

            dve.wait_ge(consts, 2)
            for k in range(3):
                hg_evict(0, k)
            hg_prep(0, first=True)
            with dve.Fori(1, NT) as i:
                hg_evict(i - 1, 3)
                hg_levels(i - 1, range(0, 3))
                hg_evict(i, 0)
                hg_levels(i - 1, range(3, 6))
                hg_evict(i, 1)
                hg_levels(i - 1, range(6, LEVELS))
                hg_states(i - 1)
                hg_evict(i, 2)
                hg_prep(i)
                hg_norm(i - 1)
                hg_o(i - 1)
            h = NT - 1
            hg_levels(h, range(3))
            hg_evict(h, 3)
            hg_levels(h, range(3, LEVELS))
            hg_states(h)
            hg_norm(h)
            hg_o(h)
            after = 4 * NT + NT * BLOCKS
            dve.wait_ge(in_hi, after + NT)
            dve.wait_ge(in_lo, after + NT - 1)
            tt(b_lo[:, h, :], o_hg[:, h, :], b_hi[:, h, :].bitcast(f32), ALU.subtract).then_inc(in_lo, 1)
            make_amp(3, MOD1, "sc_c", 120).then_inc(small_d, 1)
            clear_squares()
            dve.wait_ge(reloaded_head[1], 16 * HEAD)

            def hg_out(m, ks):
                for k in ks:
                    s, n = step_of(HG_OUT, 4, m, k), m * 4 + k
                    renew(s, n, MOD1, "g_t")
                    freed()
                    split_lo(step_of(HG_OUT, 4, m, k + 2))
                    in_lo_res(A, 3, n, after + NT)
                    add_square(2, n)

            hg_out(0, range(HEAD))
            dve.wait_ge(reloaded[1], 16 * (NT - HEAD))
            hg_out(0, range(HEAD, 4))
            with dve.Fori(1, 2) as m:
                hg_out(m, range(4))
            mlp(1, MLP1, 0, B, after + 2 * NT, first=True)
            with dve.Fori(1, BLOCKS - 1) as b:
                mlp(1, MLP1, b, B, after + 2 * NT)
            mlp(1, MLP1, BLOCKS - 1, B, after + 2 * NT, last=True)
            dve.wait_ge(stat_mm, 4)
            rms(cols[:, 0:NC], D, EPS, root_ready, ms_ready, 5).then_inc(last_rms, 1)
            for r in range(1, NC, 2):
                dve.wait_ge(out_mm, r + 1)
                ts(o_hg[:, r, :], acc[1][:, :], nst[:, 2, r:r + 1], None, ALU.mult).then_inc(row_out[1], 1)


_INS = ['x', 'c', 'mod_w', 'mod_b', 'norm_mix', 'norm_mlp', 'norm_final', 'rg_w_in', 'rg_conv_w',
        'rg_conv_b', 'rg_w_a', 'rg_b_a', 'rg_w_x', 'rg_b_x', 'rg_lambda', 'rg_w_out', 'hg_w_in',
        'hg_lower_bounds', 'hg_gnorm', 'hg_w_out', 'mlp_w1', 'mlp_w2']


def kernel(**inputs):
    import numpy as _np
    import concourse.bacc as _bacc
    from concourse import mybir as _mybir
    from concourse.bass_utils import run_bass_kernel_spmd as _run

    nc = _bacc.Bacc("TRN2", target_bir_lowering=False, num_devices=1)
    arrays, args = {}, []
    for name in _INS:
        a = _np.ascontiguousarray(inputs[name])
        arrays[f"in_{name}"] = a
        args.append(nc.dram_tensor(f"in_{name}", a.shape, _mybir.dt.from_np(a.dtype),
                                   kind="ExternalInput").ap())
    args.append(nc.dram_tensor("out_0", (1, T, D), _mybir.dt.float32, kind="ExternalOutput").ap())
    trunk(nc, *args)
    return _run(nc, [arrays], core_ids=[0]).results[0]["out_0"]
```
